# Optimizing a Trainium2 kernel written in Bass

```python
import jax, jax.numpy as jnp
from jax import lax
import numpy as np
import math

D_MODEL = 1024
BATCH = 1
SEQ = 256
DEPTH = 2

CHUNK = 128
EPS = 1e-6
A_GROUPS = 4
A_GROUP_DIM = 128
A_WIDTH = A_GROUPS * A_GROUP_DIM
B_HEADS = 4
B_KEY_DIM = 64
B_VAL_DIM = 128
B_QK_WIDTH = B_HEADS * B_KEY_DIM
B_V_WIDTH = B_HEADS * B_VAL_DIM
B_GATE_RANK = 16
B_GATE_NORMALIZER = 16.0
EVEN_SPLITS = (A_WIDTH, A_WIDTH, B_QK_WIDTH, B_QK_WIDTH, B_GATE_RANK, B_V_WIDTH, B_V_WIDTH)
EVEN_IN = sum(EVEN_SPLITS)
EVEN_MIX_WIDTH = A_WIDTH + B_V_WIDTH
C_HEADS = 16
C_HEAD_DIM = 64
C_WIDTH = C_HEADS * C_HEAD_DIM
ODD_SPLITS = (C_WIDTH, C_WIDTH, C_WIDTH, C_WIDTH, C_HEADS)
ODD_IN = sum(ODD_SPLITS)
D_FF_DENSE = 2816
N_EXPERTS = 8
TOP_K = 2
D_FF_EXPERT = 3584
N_EVEN = (DEPTH + 1) // 2
N_ODD = DEPTH // 2


def _split(z, sizes):
    idx = np.cumsum(np.array(sizes))[:-1].tolist()
    return jnp.split(z, idx, axis=-1)

def rmsnorm(x, g):
    xf = x.astype(jnp.float32)
    y = xf * lax.rsqrt(jnp.mean(xf * xf, axis=-1, keepdims=True) + EPS)
    return (y * g.astype(jnp.float32)).astype(x.dtype)

def layernorm(x, g, b):
    xf = x.astype(jnp.float32)
    mu = jnp.mean(xf, axis=-1, keepdims=True)
    xc = xf - mu
    y = xc * lax.rsqrt(jnp.mean(xc * xc, axis=-1, keepdims=True) + EPS)
    return (y * g.astype(jnp.float32) + b.astype(jnp.float32)).astype(x.dtype)

def swiglu(h, w1, w3, w2):
    return (jax.nn.silu(h @ w1) * (h @ w3)) @ w2

def chunk_spatial_gating(u, v, w_s, b_s):
    bsz, seq, _ = u.shape
    n = seq // CHUNK
    mask = jnp.tril(jnp.ones((CHUNK, CHUNK), dtype=bool))
    w = jnp.where(mask[None], w_s, jnp.zeros_like(w_s))
    v5 = v.reshape(bsz, n, CHUNK, A_GROUPS, A_GROUP_DIM)
    mixed = jnp.einsum('gts,bnsgd->bntgd', w, v5) + b_s.T[None, None, :, :, None]
    return (u.reshape(bsz, n, CHUNK, A_GROUPS, A_GROUP_DIM) * mixed).reshape(bsz, seq, A_WIDTH)

def gla_chunked(q, k, v, log_a):
    bsz, seq, nh, dk = q.shape
    dv = v.shape[-1]
    n = seq // CHUNK
    def to_chunks(t):
        return jnp.swapaxes(t.reshape(bsz, n, CHUNK, nh, t.shape[-1]), 0, 1)
    g = jnp.cumsum(log_a.astype(jnp.float32).reshape(bsz, n, CHUNK, nh, dk), axis=2)
    g = jnp.swapaxes(g, 0, 1)
    causal = jnp.tril(jnp.ones((CHUNK, CHUNK), dtype=bool))

    def step(state, inp):
        qc, kc, vc, gc = inp
        qf = qc.astype(jnp.float32)
        kf = kc.astype(jnp.float32)
        vf = vc.astype(jnp.float32)
        o_inter = jnp.einsum('bthk,bhkv->bthv', qf * jnp.exp(gc), state)
        diff = gc[:, :, None] - gc[:, None, :]
        diff = jnp.where(causal[None, :, :, None, None], diff, -jnp.inf)
        attn = jnp.einsum('bthk,bshk,btshk->btsh', qf, kf, jnp.exp(diff))
        o_intra = jnp.einsum('btsh,bshv->bthv', attn, vf)
        g_last = gc[:, -1]
        k_dec = kf * jnp.exp(g_last[:, None] - gc)
        new_state = jnp.exp(g_last)[..., None] * state + jnp.einsum('bshk,bshv->bhkv', k_dec, vf)
        return new_state, o_inter + o_intra

    state0 = jnp.zeros((bsz, nh, dk, dv), jnp.float32)
    _, out = lax.scan(step, state0, (to_chunks(q), to_chunks(k), to_chunks(v), g))
    return jnp.swapaxes(out, 0, 1).reshape(bsz, seq, nh, dv).astype(v.dtype)

def forgetting_attention(q, k, v, log_f):
    bsz, seq, nh, hd = q.shape
    n = seq // CHUNK
    scale = hd ** -0.5
    c = jnp.cumsum(log_f, axis=1)
    c_key = jnp.swapaxes(c, 1, 2)
    q_blocks = jnp.swapaxes(q.reshape(bsz, n, CHUNK, nh, hd), 0, 1)
    c_blocks = jnp.swapaxes(c.reshape(bsz, n, CHUNK, nh), 0, 1)
    s_pos = jnp.arange(seq)

    def block(args):
        qb, cb, bi = args
        logits = jnp.einsum('bthd,bshd->bhts', qb, k).astype(jnp.float32) * scale
        logits = logits + jnp.swapaxes(cb, 1, 2)[..., None] - c_key[:, :, None, :]
        t_pos = bi * CHUNK + jnp.arange(CHUNK)
        mask = s_pos[None, :] <= t_pos[:, None]
        logits = jnp.where(mask[None, None], logits, -jnp.inf)
        p = jax.nn.softmax(logits, axis=-1)
        return jnp.einsum('bhts,bshd->bthd', p.astype(v.dtype), v)

    out = lax.map(block, (q_blocks, c_blocks, jnp.arange(n)))
    return jnp.swapaxes(out, 0, 1).reshape(bsz, seq, nh * hd)

def mixer_even(h, w_in, gate_up, gate_bias, w_s, b_s, ln_g, ln_b, head_g, w_o):
    bsz, seq, _ = h.shape
    z = h @ w_in
    u, v, q, k, g_lr, vb, og = _split(z, EVEN_SPLITS)
    u = jax.nn.gelu(u)
    v = layernorm(jax.nn.gelu(v), ln_g, ln_b)
    a_out = chunk_spatial_gating(u, v, w_s, b_s)
    gate_logit = (g_lr @ gate_up + gate_bias).astype(jnp.float32)
    log_a = jax.nn.log_sigmoid(gate_logit) / B_GATE_NORMALIZER
    qh = q.reshape(bsz, seq, B_HEADS, B_KEY_DIM) * (B_KEY_DIM ** -0.5)
    kh = k.reshape(bsz, seq, B_HEADS, B_KEY_DIM)
    vh = vb.reshape(bsz, seq, B_HEADS, B_VAL_DIM)
    o = gla_chunked(qh, kh, vh, log_a.reshape(bsz, seq, B_HEADS, B_KEY_DIM))
    o = rmsnorm(o, head_g) * jax.nn.silu(og.reshape(bsz, seq, B_HEADS, B_VAL_DIM))
    b_out = o.reshape(bsz, seq, B_V_WIDTH)
    return jnp.concatenate([a_out, b_out], axis=-1) @ w_o

def mixer_odd(h, w_in, forget_bias, q_g, k_g, w_o):
    bsz, seq, _ = h.shape
    z = h @ w_in
    q, k, v, og, f = _split(z, ODD_SPLITS)
    q = rmsnorm(q.reshape(bsz, seq, C_HEADS, C_HEAD_DIM), q_g)
    k = rmsnorm(k.reshape(bsz, seq, C_HEADS, C_HEAD_DIM), k_g)
    v = v.reshape(bsz, seq, C_HEADS, C_HEAD_DIM)
    log_f = jax.nn.log_sigmoid(f.astype(jnp.float32) + forget_bias.astype(jnp.float32))
    o = forgetting_attention(q, k, v, log_f)
    o = o * jax.nn.sigmoid(og)
    return o @ w_o

def moe_swiglu(h, router, w1, w3, w2):
    logits = (h @ router).astype(jnp.float32)
    top_vals, top_idx = lax.top_k(logits, TOP_K)
    top_w = jax.nn.softmax(top_vals, axis=-1)
    gates = jnp.sum(jax.nn.one_hot(top_idx, N_EXPERTS, dtype=jnp.float32) * top_w[..., None], axis=-2)
    gates = gates.astype(h.dtype)
    out = jnp.zeros_like(h)
    for e in range(N_EXPERTS):
        out = out + gates[..., e:e + 1] * swiglu(h, w1[e], w3[e], w2[e])
    return out

def first_inputs(seed: int = 0) -> dict:
    key = jax.random.key(seed)
    ks = iter(jax.random.split(key, 32))
    f32 = jnp.float32
    def nrm(shape, scale):
        return jax.random.normal(next(ks), shape, f32) * scale
    def gain(shape):
        return 1.0 + 0.05 * jax.random.normal(next(ks), shape, f32)
    d = D_MODEL
    return {
        "x": jax.random.normal(next(ks), (BATCH, SEQ, d), f32),
        "even_norm_mix": gain((N_EVEN, d)),
        "even_w_in": nrm((N_EVEN, d, EVEN_IN), d ** -0.5),
        "even_gate_up": nrm((N_EVEN, B_GATE_RANK, B_QK_WIDTH), B_GATE_RANK ** -0.5),
        "even_gate_bias": nrm((N_EVEN, B_QK_WIDTH), 0.1),
        "even_w_s": nrm((N_EVEN, A_GROUPS, CHUNK, CHUNK), CHUNK ** -0.5),
        "even_b_s": 1.0 + 0.1 * jax.random.normal(next(ks), (N_EVEN, A_GROUPS, CHUNK), f32),
        "even_ln_g": gain((N_EVEN, A_WIDTH)),
        "even_ln_b": nrm((N_EVEN, A_WIDTH), 0.02),
        "even_head_g": gain((N_EVEN, B_HEADS, B_VAL_DIM)),
        "even_w_o": nrm((N_EVEN, EVEN_MIX_WIDTH, d), EVEN_MIX_WIDTH ** -0.5),
        "even_norm_ffn": gain((N_EVEN, d)),
        "even_ffn_w1": nrm((N_EVEN, d, D_FF_DENSE), d ** -0.5),
        "even_ffn_w3": nrm((N_EVEN, d, D_FF_DENSE), d ** -0.5),
        "even_ffn_w2": nrm((N_EVEN, D_FF_DENSE, d), D_FF_DENSE ** -0.5),
        "odd_norm_mix": gain((N_ODD, d)),
        "odd_w_in": nrm((N_ODD, d, ODD_IN), d ** -0.5),
        "odd_forget_bias": 2.0 + 0.5 * jax.random.normal(next(ks), (N_ODD, C_HEADS), f32),
        "odd_q_g": gain((N_ODD, C_HEAD_DIM)),
        "odd_k_g": gain((N_ODD, C_HEAD_DIM)),
        "odd_w_o": nrm((N_ODD, C_WIDTH, d), C_WIDTH ** -0.5),
        "odd_norm_ffn": gain((N_ODD, d)),
        "odd_router": nrm((N_ODD, d, N_EXPERTS), d ** -0.5),
        "odd_exp_w1": nrm((N_ODD, N_EXPERTS, d, D_FF_EXPERT), d ** -0.5),
        "odd_exp_w3": nrm((N_ODD, N_EXPERTS, d, D_FF_EXPERT), d ** -0.5),
        "odd_exp_w2": nrm((N_ODD, N_EXPERTS, D_FF_EXPERT, d), D_FF_EXPERT ** -0.5),
        "final_norm": gain((d,)),
    }

def first_block(x, even_norm_mix, even_w_in, even_gate_up, even_gate_bias, even_w_s, even_b_s,
              even_ln_g, even_ln_b, even_head_g, even_w_o, even_norm_ffn, even_ffn_w1,
              even_ffn_w3, even_ffn_w2, odd_norm_mix, odd_w_in, odd_forget_bias, odd_q_g,
              odd_k_g, odd_w_o, odd_norm_ffn, odd_router, odd_exp_w1, odd_exp_w3,
              odd_exp_w2, final_norm):
    for i in range(DEPTH):
        j = i // 2
        if i % 2 == 0:
            h = rmsnorm(x, even_norm_mix[j])
            x = x + mixer_even(h, even_w_in[j], even_gate_up[j], even_gate_bias[j], even_w_s[j],
                               even_b_s[j], even_ln_g[j], even_ln_b[j], even_head_g[j], even_w_o[j])
            h = rmsnorm(x, even_norm_ffn[j])
            x = x + swiglu(h, even_ffn_w1[j], even_ffn_w3[j], even_ffn_w2[j])
        else:
            h = rmsnorm(x, odd_norm_mix[j])
            x = x + mixer_odd(h, odd_w_in[j], odd_forget_bias[j], odd_q_g[j], odd_k_g[j], odd_w_o[j])
            h = rmsnorm(x, odd_norm_ffn[j])
            x = x + moe_swiglu(h, odd_router[j], odd_exp_w1[j], odd_exp_w3[j], odd_exp_w2[j])
    return rmsnorm(x, final_norm)


GRID_W = 64
CTX_LEN = 256
ROPE_THETA = 10000.0
Q_BLOCK = 128

MLA_HEADS = 4
MLA_Q_RANK = 256
MLA_KV_RANK = 128
MLA_NOPE = 64
MLA_ROPE = 32
MLA_V = 64
DIFF_HEADS = 4
DIFF_QK = 32
DIFF_V = 2 * DIFF_QK
GQA_HEADS = 8
GQA_KV_HEADS = 2
GQA_DIM = 64
GQA_GROUP = GQA_HEADS // GQA_KV_HEADS

MIX_WIDTH = MLA_HEADS * MLA_V + DIFF_HEADS * DIFF_V + GQA_HEADS * GQA_DIM
FFN_HIDDEN = -(-8 * D_MODEL // (3 * 256)) * 256

IN_SIZES = (
    MLA_Q_RANK,
    MLA_KV_RANK + MLA_ROPE,
    DIFF_HEADS * 2 * DIFF_QK,
    DIFF_HEADS * 2 * DIFF_QK,
    DIFF_HEADS * DIFF_V,
    GQA_HEADS * GQA_DIM,
    GQA_KV_HEADS * GQA_DIM,
    GQA_KV_HEADS * GQA_DIM,
)
IN_WIDTH = sum(IN_SIZES)

MLA_SCALE = 1.0 / math.sqrt(MLA_NOPE + MLA_ROPE)
DIFF_SCALE = 1.0 / math.sqrt(DIFF_QK)
GQA_SCALE = 1.0 / math.sqrt(GQA_DIM)


def _rms(x, g):
    xf = x.astype(jnp.float32)
    y = xf * lax.rsqrt(jnp.mean(xf * xf, axis=-1, keepdims=True) + EPS)
    return (y * g.astype(jnp.float32)).astype(x.dtype)

def _axial_rope_tables(row, col, rot_dim):
    quarter = rot_dim // 4
    inv = ROPE_THETA ** (-jnp.arange(quarter, dtype=jnp.float32) / quarter)
    ang = jnp.concatenate([row.astype(jnp.float32)[:, None] * inv,
                           col.astype(jnp.float32)[:, None] * inv], axis=-1)
    return jnp.cos(ang), jnp.sin(ang)

def _rope(x, tables):
    if tables is None:
        return x
    cos, sin = tables
    half = x.shape[-1] // 2
    xf = x.astype(jnp.float32)
    x1, x2 = xf[..., :half], xf[..., half:]
    c = cos[None, :, None, :]
    s = sin[None, :, None, :]
    return jnp.concatenate([x1 * c - x2 * s, x2 * c + x1 * s], axis=-1).astype(x.dtype)

def _hf(t):
    return t.transpose(0, 2, 1, 3)

def _sdpa(q, k, v, scale):
    s = jnp.einsum('bhgqd,bhkd->bhgqk', q, k).astype(jnp.float32) * scale
    p = jax.nn.softmax(s, axis=-1).astype(v.dtype)
    return jnp.einsum('bhgqk,bhkd->bhgqd', p, v)

def _latent_attention(q, k, v, scale):
    B, Hk, G, S, d = q.shape
    nb = S // Q_BLOCK
    qb = q.reshape(B, Hk, G, nb, Q_BLOCK, d).transpose(3, 0, 1, 2, 4, 5)
    ob = lax.map(lambda qi: _sdpa(qi, k, v, scale), qb)
    return ob.transpose(1, 2, 3, 0, 4, 5).reshape(B, Hk, G, S, ob.shape[-1])

def _project(h, w_in, g_mla_q, w_mla_qb, g_mla_kv, w_mla_kvb, g_gqa_q, g_gqa_k,
             rope_small, rope_large):
    B, T, _ = h.shape
    p = h @ w_in
    idx = np.cumsum(IN_SIZES)[:-1].tolist()
    q_a, kv_a, dq, dk, dv, gq, gk, gv = jnp.split(p, idx, axis=-1)

    q = (_rms(q_a, g_mla_q) @ w_mla_qb).reshape(B, T, MLA_HEADS, MLA_NOPE + MLA_ROPE)
    q_nope, q_pe = q[..., :MLA_NOPE], _rope(q[..., MLA_NOPE:], rope_small)
    c_kv = kv_a[..., :MLA_KV_RANK]
    k_pe = _rope(kv_a[..., MLA_KV_RANK:][:, :, None, :], rope_small)
    kv = (_rms(c_kv, g_mla_kv) @ w_mla_kvb).reshape(B, T, MLA_HEADS, MLA_NOPE + MLA_V)
    k_nope, v_mla = kv[..., :MLA_NOPE], kv[..., MLA_NOPE:]
    q_mla = jnp.concatenate([q_nope, q_pe], axis=-1)
    k_mla = jnp.concatenate([k_nope, jnp.broadcast_to(k_pe, (B, T, MLA_HEADS, MLA_ROPE))], axis=-1)
    mla = (_hf(q_mla)[:, :, None], _hf(k_mla), _hf(v_mla))

    q_d = _rope(dq.reshape(B, T, DIFF_HEADS * 2, DIFF_QK), rope_small)
    k_d = _rope(dk.reshape(B, T, DIFF_HEADS * 2, DIFF_QK), rope_small)
    v_d = jnp.repeat(dv.reshape(B, T, DIFF_HEADS, DIFF_V), 2, axis=2)
    diff = (_hf(q_d)[:, :, None], _hf(k_d), _hf(v_d))

    q_g = _rope(_rms(gq.reshape(B, T, GQA_HEADS, GQA_DIM), g_gqa_q), rope_large)
    k_g = _rope(_rms(gk.reshape(B, T, GQA_KV_HEADS, GQA_DIM), g_gqa_k), rope_large)
    v_g = gv.reshape(B, T, GQA_KV_HEADS, GQA_DIM)
    q_g = q_g.reshape(B, T, GQA_KV_HEADS, GQA_GROUP, GQA_DIM).transpose(0, 2, 3, 1, 4)
    gqa = (q_g, _hf(k_g), _hf(v_g))
    return (mla, diff, gqa)

def _merge(o_mla, o_diff, o_gqa, lam, lam_init, g_diff_sub):
    B, _, _, T, _ = o_mla.shape
    y_mla = o_mla[:, :, 0].transpose(0, 2, 1, 3).reshape(B, T, MLA_HEADS * MLA_V)
    od = o_diff[:, :, 0].reshape(B, DIFF_HEADS, 2, T, DIFF_V)
    d = od[:, :, 0] - lam.astype(od.dtype) * od[:, :, 1]
    d = _rms(d, g_diff_sub) * (1.0 - lam_init)
    y_diff = d.transpose(0, 2, 1, 3).reshape(B, T, DIFF_HEADS * DIFF_V)
    y_gqa = o_gqa.transpose(0, 3, 1, 2, 4).reshape(B, T, GQA_HEADS * GQA_DIM)
    return jnp.concatenate([y_mla, y_diff, y_gqa], axis=-1)

def _swiglu(h, w_gate, w_up, w_down):
    return (jax.nn.silu(h @ w_gate) * (h @ w_up)) @ w_down

def second_inputs(seed: int = 0) -> dict:
    key = jax.random.key(seed)
    ks = iter(jax.random.split(key, 32))

    def nrm(shape, scale):
        return jax.random.normal(next(ks), shape, jnp.float32) * scale

    def gain(shape):
        return 1.0 + 0.05 * jax.random.normal(next(ks), shape, jnp.float32)

    D = D_MODEL
    return {
        "x": nrm((BATCH, SEQ, D), 1.0),
        "c": nrm((BATCH, D), 1.0),
        "ctx": nrm((BATCH, CTX_LEN, D), 1.0),
        "c_ctx": nrm((D,), 1.0),
        "w_ada": nrm((DEPTH, D, 6 * D), 0.5 * D ** -0.5),
        "b_ada": nrm((DEPTH, 6 * D), 0.01),
        "g_attn_pre": gain((DEPTH, D)),
        "g_attn_post": gain((DEPTH, D)),
        "w_in": nrm((DEPTH, D, IN_WIDTH), D ** -0.5),
        "g_mla_q": gain((DEPTH, MLA_Q_RANK)),
        "w_mla_qb": nrm((DEPTH, MLA_Q_RANK, MLA_HEADS * (MLA_NOPE + MLA_ROPE)), MLA_Q_RANK ** -0.5),
        "g_mla_kv": gain((DEPTH, MLA_KV_RANK)),
        "w_mla_kvb": nrm((DEPTH, MLA_KV_RANK, MLA_HEADS * (MLA_NOPE + MLA_V)), MLA_KV_RANK ** -0.5),
        "lambda_q1": nrm((DEPTH, DIFF_QK), 0.1),
        "lambda_k1": nrm((DEPTH, DIFF_QK), 0.1),
        "lambda_q2": nrm((DEPTH, DIFF_QK), 0.1),
        "lambda_k2": nrm((DEPTH, DIFF_QK), 0.1),
        "g_diff_sub": gain((DEPTH, DIFF_V)),
        "g_gqa_q": gain((DEPTH, GQA_DIM)),
        "g_gqa_k": gain((DEPTH, GQA_DIM)),
        "w_out": nrm((DEPTH, MIX_WIDTH, D), MIX_WIDTH ** -0.5),
        "g_ffn_pre": gain((DEPTH, D)),
        "g_ffn_post": gain((DEPTH, D)),
        "w_ffn_gate": nrm((DEPTH, D, FFN_HIDDEN), D ** -0.5),
        "w_ffn_up": nrm((DEPTH, D, FFN_HIDDEN), D ** -0.5),
        "w_ffn_down": nrm((DEPTH, FFN_HIDDEN, D), FFN_HIDDEN ** -0.5),
    }

def second_block(x, c, ctx, c_ctx, w_ada, b_ada, g_attn_pre, g_attn_post, w_in, g_mla_q, w_mla_qb,
              g_mla_kv, w_mla_kvb, lambda_q1, lambda_k1, lambda_q2, lambda_k2, g_diff_sub,
              g_gqa_q, g_gqa_k, w_out, g_ffn_pre, g_ffn_post, w_ffn_gate, w_ffn_up, w_ffn_down):
    n_tok = x.shape[1]
    rows = n_tok // GRID_W
    row = jnp.repeat(jnp.arange(rows, dtype=jnp.int32), GRID_W)
    col = jnp.tile(jnp.arange(GRID_W, dtype=jnp.int32), rows)
    rope_small = _axial_rope_tables(row, col, MLA_ROPE)
    rope_large = _axial_rope_tables(row, col, GQA_DIM)

    silu_c = jax.nn.silu(c)
    silu_cc = jax.nn.silu(c_ctx)
    xc = ctx
    scales = (MLA_SCALE, DIFF_SCALE, GQA_SCALE)

    for l in range(DEPTH):
        last = l == DEPTH - 1
        mod = (silu_c @ w_ada[l] + b_ada[l])[:, None, :]
        mod_c = (silu_cc @ w_ada[l] + b_ada[l])[None, None, :]
        sh_a, sc_a, gt_a, sh_f, sc_f, gt_f = jnp.split(mod, 6, axis=-1)
        csh_a, csc_a, cgt_a, csh_f, csc_f, cgt_f = jnp.split(mod_c, 6, axis=-1)

        lam_init = 0.8 - 0.6 * math.exp(-0.3 * l)
        lam = (jnp.exp(jnp.sum(lambda_q1[l].astype(jnp.float32) * lambda_k1[l].astype(jnp.float32)))
               - jnp.exp(jnp.sum(lambda_q2[l].astype(jnp.float32) * lambda_k2[l].astype(jnp.float32)))
               + lam_init)

        h = _rms(x, g_attn_pre[l]) * (1.0 + sc_a) + sh_a
        hc = _rms(xc, g_attn_pre[l]) * (1.0 + csc_a) + csh_a
        proj_args = (w_in[l], g_mla_q[l], w_mla_qb[l], g_mla_kv[l], w_mla_kvb[l], g_gqa_q[l], g_gqa_k[l])
        lat = _project(h, *proj_args, rope_small, rope_large)
        cxt = _project(hc, *proj_args, None, None)

        o_lat = []
        for (q, k, v), (qc, kc, vc), s in zip(lat, cxt, scales):
            k_all = jnp.concatenate([k, kc], axis=2)
            v_all = jnp.concatenate([v, vc], axis=2)
            o_lat.append(_latent_attention(q, k_all, v_all, s))
        y = _merge(o_lat[0], o_lat[1], o_lat[2], lam, lam_init, g_diff_sub[l]) @ w_out[l]
        x = x + gt_a * _rms(y, g_attn_post[l])

        if not last:
            o_ctx = [_sdpa(qc, kc, vc, s) for (qc, kc, vc), s in zip(cxt, scales)]
            yc = _merge(o_ctx[0], o_ctx[1], o_ctx[2], lam, lam_init, g_diff_sub[l]) @ w_out[l]
            xc = xc + cgt_a * _rms(yc, g_attn_post[l])

        hf = _rms(x, g_ffn_pre[l]) * (1.0 + sc_f) + sh_f
        x = x + gt_f * _rms(_swiglu(hf, w_ffn_gate[l], w_ffn_up[l], w_ffn_down[l]), g_ffn_post[l])
        if not last:
            hfc = _rms(xc, g_ffn_pre[l]) * (1.0 + csc_f) + csh_f
            xc = xc + cgt_f * _rms(_swiglu(hfc, w_ffn_gate[l], w_ffn_up[l], w_ffn_down[l]), g_ffn_post[l])

    return x


def setup_inputs(seed=0):
    out = dict(first_inputs(seed))
    for name, value in second_inputs(seed + 1).items():
        if name != "x":
            out[name + "_2"] = value
    return out


def reference(
    x, even_norm_mix, even_w_in, even_gate_up, even_gate_bias, even_w_s, even_b_s, even_ln_g,
    even_ln_b, even_head_g, even_w_o, even_norm_ffn, even_ffn_w1, even_ffn_w3, even_ffn_w2,
    odd_norm_mix, odd_w_in, odd_forget_bias, odd_q_g, odd_k_g, odd_w_o, odd_norm_ffn,
    odd_router, odd_exp_w1, odd_exp_w3, odd_exp_w2, final_norm, c_2, ctx_2, c_ctx_2, w_ada_2,
    b_ada_2, g_attn_pre_2, g_attn_post_2, w_in_2, g_mla_q_2, w_mla_qb_2, g_mla_kv_2,
    w_mla_kvb_2, lambda_q1_2, lambda_k1_2, lambda_q2_2, lambda_k2_2, g_diff_sub_2, g_gqa_q_2,
    g_gqa_k_2, w_out_2, g_ffn_pre_2, g_ffn_post_2, w_ffn_gate_2, w_ffn_up_2, w_ffn_down_2,
):
    x = first_block(
        x, even_norm_mix, even_w_in, even_gate_up, even_gate_bias, even_w_s, even_b_s,
        even_ln_g, even_ln_b, even_head_g, even_w_o, even_norm_ffn, even_ffn_w1, even_ffn_w3,
        even_ffn_w2, odd_norm_mix, odd_w_in, odd_forget_bias, odd_q_g, odd_k_g, odd_w_o,
        odd_norm_ffn, odd_router, odd_exp_w1, odd_exp_w3, odd_exp_w2, final_norm,
    )
    return second_block(
        x, c_2, ctx_2, c_ctx_2, w_ada_2, b_ada_2, g_attn_pre_2, g_attn_post_2, w_in_2,
        g_mla_q_2, w_mla_qb_2, g_mla_kv_2, w_mla_kvb_2, lambda_q1_2, lambda_k1_2, lambda_q2_2,
        lambda_k2_2, g_diff_sub_2, g_gqa_q_2, g_gqa_k_2, w_out_2, g_ffn_pre_2, g_ffn_post_2,
        w_ffn_gate_2, w_ffn_up_2, w_ffn_down_2,
    )


_drawn_inputs = setup_inputs


def setup_inputs(seed=0):
    import zlib

    import numpy as np

    out = dict(_drawn_inputs(seed))
    spreads = {}
    factors = {'even_ln_b': 3.379,
     'odd_q_g': 4.427,
     'odd_k_g': 4.613,
     'g_attn_pre_2': 2.837,
     'g_mla_q_2': 8.0,
     'g_mla_kv_2': 6.627,
     'lambda_q2_2': 4.157,
     'lambda_k2_2': 7.056,
     'g_diff_sub_2': 12.034,
     'g_gqa_q_2': 8.0,
     'g_gqa_k_2': 8.0,
     'g_ffn_post_2': 2.896,
     'lambda_q1_2': 4.005,
     'lambda_k1_2': 8.0}
    for name, (base, spread) in spreads.items():
        noise = np.random.default_rng([zlib.crc32(name.encode()), seed]).standard_normal(out[name].shape)
        drawn = base * np.exp(spread * noise) if base else spread * noise
        out[name] = __import__('jax').numpy.asarray(drawn.astype(out[name].dtype))
    for name, factor in factors.items():
        out[name] = (out[name] * factor).astype(out[name].dtype)
    return out
```

```python
from contextlib import ExitStack

import numpy as np

import concourse.bass as bass
from concourse import mybir

ALU = mybir.AluOpType
ACT = mybir.ActivationFunctionType
AX = mybir.AxisListType
F32 = mybir.dt.float32
F32R = mybir.dt.float32r
U32 = mybir.dt.uint32

P = 128
D = 1024
KT = D // P
T = 256
CHUNK = 128
EPS = 1e-6
PACK = KT * P

A_W, B_QK, B_V, RANK = 512, 256, 512, 16
CLAMP = 70.0
SUB = 32
C_HEADS = 16
FF = 2816
FF_STEPS = FF // P
N_EXP, FF_EXP = 8, 3584
EXP_STEPS = FF_EXP // P
MOE_STEPS = N_EXP * EXP_STEPS

GRID_W = 64
ROPE_THETA = 10000.0
MLA_QK = 96
MLA_SCALE = 96.0 ** -0.5
DIFF_SCALE = 32.0 ** -0.5
LAMBDA_INIT = [0.8 - 0.6 * float(np.exp(-0.3 * l)) for l in range(2)]

RING = 6
AHEAD = 5

N_EVEN_IN, N_ODD_IN, N_IN, N_IN_KV, N_ADA = 21, 33, 16, 8, 48
SECTIONS = [("ada0", N_ADA), ("ada1", N_ADA), ("even_in", N_EVEN_IN), ("even_o", 8), ("even_ffn", 3 * FF_STEPS),
            ("odd_in", N_ODD_IN), ("odd_o", 8), ("router", 1), ("moe", 3 * MOE_STEPS)]
for _l in range(2):
    SECTIONS += [(f"in{_l}", N_IN), (f"kvb{_l}", 1), (f"qb{_l}", 1), (f"out{_l}", 8), (f"ffn{_l}", 3 * FF_STEPS)]
START, _n = {}, 0
for _name, _count in SECTIONS:
    START[_name] = _n
    _n += _count
N_PACKS = _n
COUNT = dict(SECTIONS)


def stream_order():
    def all_of(*names):
        return [(START[n], COUNT[n]) for n in names]
    order = all_of("ada0", "ada1", "even_in", "even_o", "even_ffn", "odd_in", "odd_o", "router", "moe")
    for _ in ("context", "latents"):
        order += all_of("in0", "kvb0", "qb0", "out0", "ffn0")
    order += [(START["in1"], N_IN_KV), (START["kvb1"], 1)]
    order += all_of("in1", "kvb1", "qb1", "out1", "ffn1")
    merged = []
    for s, n in order:
        if merged and sum(merged[-1]) == s:
            merged[-1] = (merged[-1][0], merged[-1][1] + n)
        else:
            merged.append((s, n))
    return merged


TOTAL = sum(n for _, n in stream_order())

VEC = {}
_n = 0
for _name, _count in ([("zero", 1), ("one", 1), ("eps", 1), ("eps64", 1),
                       ("g_even_mix", 8), ("g_even_ffn", 8), ("g_odd_mix", 8), ("g_odd_ffn", 8), ("g_final", 8),
                       ("head_g", 4), ("gate_bias", 2), ("odd_q_g", 1), ("odd_k_g", 1), ("forget_bias", 1),
                       ("cond", 16)]
                      + [(f"{n}{l}", c) for l in range(2) for n, c in
                         (("g_attn_pre", 8), ("g_attn_post", 8), ("g_ffn_pre", 8), ("g_ffn_post", 8), ("b_ada", 48),
                          ("g_mla_q", 2), ("g_mla_kv", 1), ("g_gqa_q", 1), ("g_gqa_k", 1), ("g_sub", 1),
                          ("lambdas", 4))]):
    VEC[_name] = (_n, _count)
    _n += _count
N_VEC = _n

MAT = {}
_n = 0
for _name, _count in [("ident", P), ("ones", P), ("block64", P), ("mask01", P), ("mask_add", P),
                      ("rot_mla", P), ("rot_diff", P), ("rot_gqa", P),
                      ("cos_mla", T), ("sin_mla", T), ("cos_diff", T), ("sin_diff", T), ("cos_gqa", T),
                      ("sin_gqa", T), ("pick", N_EXP * P), ("iota", N_EXP), ("head_id", C_HEADS)]:
    MAT[_name] = (_n, _count)
    _n += _count
N_MAT = _n


class Seen:

    def __init__(self):
        self.count = {}

    def next(self, sem, n=1):
        self.count[sem.name] = self.count.get(sem.name, 0) + n
        return self.count[sem.name]

    def now(self, sem):
        return self.count.get(sem.name, 0)


def build(nc, w_packs, vecs, mats, x_t, ctx_t, w_s_t, b_s_row, ln_g_row, ln_b_row, gate_up, out_t):
    with ExitStack() as stack:
        def sb(name, shape, dt=F32):
            return stack.enter_context(nc.sbuf_tensor(name, shape, dt))

        made = {}

        def ev(name):
            if name not in made:
                made[name] = stack.enter_context(nc.semaphore(name))
            return made[name]

        raw = sb("raw", [P, RING, PACK])
        w_hi = sb("w_hi", [P, RING, PACK], F32R)
        w_lo = sb("w_lo", [P, RING, PACK], F32R)
        lat = sb("lat", [P, KT, T])
        con = sb("con", [P, KT, T])
        h_hi = sb("h_hi", [P, KT, T], F32R)
        h_lo = sb("h_lo", [P, KT, T], F32R)
        tmp = sb("tmp", [P, KT, T])
        sq = sb("sq", [P, KT, T])
        vec = sb("vec", [P, N_VEC])
        mat = sb("mat", [P, N_MAT])
        rs = sb("rs", [P, T])
        prob = sb("prob", [P, 2, 512])
        prob_t = sb("prob_t", [P, 2, 4 * T])
        logit = sb("logit", [P, 2, T])
        sg = sb("sg", [P, 2, T])
        prod = sb("prod", [P, 2, T])
        f_hi = sb("f_hi", [P, 2, T], F32R)
        f_lo = sb("f_lo", [P, 2, T], F32R)
        mod = sb("mod", [P, 2, N_ADA, 2])
        gains = sb("gains", [P, 2, 4, KT, 2])
        small = sb("small", [P, 64])
        cond_s = sb("cond_s", [P, KT, 2])
        cond_hi = sb("cond_hi", [P, KT, 2], F32R)
        cond_lo = sb("cond_lo", [P, KT, 2], F32R)
        neg_lam = sb("neg_lam", [P, 2])
        g_sub = sb("g_sub", [P, 2])
        arena = sb("arena", [P, 11264])

        def V(name, j=None):
            a, n = VEC[name]
            return vec[:, a:a + n] if j is None else vec[:, a + j:a + j + 1]

        def M(name):
            a, n = MAT[name]
            return mat[:, a:a + n]

        at = [0]

        def part(*shape, start=None):
            if start is not None:
                at[0] = start
            n = int(np.prod(shape))
            a = arena[:, at[0]:at[0] + n]
            at[0] += n
            assert at[0] <= 11264
            if len(shape) == 2:
                a = a.rearrange("p (a b) -> p a b", b=shape[1])
            if len(shape) == 3:
                a = a.rearrange("p (a b c) -> p a b c", b=shape[1], c=shape[2])
            return a

        U = part(4, T, start=0)
        VA = part(2, A_W)
        VN = part(2, A_W)
        QT = part(2, T)
        KTT = part(2, T)
        VB = part(2, B_V)
        OG = part(4, T)
        G = part(2, T)
        GX = part(2, T)
        EK = part(2, 8, P)
        QQ = part(2, T)
        QI = part(2, P)
        KD = part(2, P)
        WS = part(4, P)
        BS = part(4, P)
        LNG, LNB = prob_t[:, 0, 0:A_W], prob_t[:, 0, A_W:2 * A_W]
        ATS = prob_t[:, 1, :].rearrange("p (a b c) -> p a b c", a=2, b=4)
        KDT = prob[:, 0, 0:2 * P].rearrange("p (a b) -> p a b", a=2)
        ST = prob[:, 0, 2 * P:4 * P].rearrange("p (a b) -> p a b", a=2)
        GUP = prob[0:RANK, 1, 0:B_QK]
        GLR = logit[:, 0, :]
        OQ = part(8, T, start=0)
        OK = part(8, T)
        OV = part(2, D)
        OO = part(8, T)
        OC = part(T)
        ONC = part(T)
        OF = part(T)
        GB = part(8, T, start=0)
        RL = part(2, P, start=2048)
        GATE = part(2, N_EXP)
        GATE2 = part(2, N_EXP)
        GT = part(T)
        KM = part(4, 2 * T, start=0)
        KD2 = part(2, 2 * T)
        KG = part(2 * T)
        VM = part(4, 256)
        VD = part(4, 256)
        VG = part(4, 128)
        QM = part(4, T)
        QD = part(2, T)
        QG = part(4, T)
        ZR = part(8, T)
        KPE = part(T)

        psum = [stack.enter_context(nc.psum_tensor(f"bank{b}", [P, 512], F32)) for b in range(8)]

        def half(b, j):
            return psum[b][:, j * T:(j + 1) * T]

        raw_in = [ev(f"raw_in{j}") for j in range(RING)]
        hi_done, lo_done, pack_used = ev("hi_done"), ev("lo_done"), ev("pack_used")

        block = stack.enter_context(nc.Block())

        def odd_heads():
            return [dict(h=h, row=64 * (h % 2), k=64, q=lambda c, h=h: OQ[64 * (h % 2):64 * (h % 2) + 64, h // 2, c * P:(c + 1) * P],
                         keys=lambda n, h=h: OK[64 * (h % 2):64 * (h % 2) + 64, h // 2, 0:n],
                         v=lambda s, h=h: OV[:, s, h * 64:(h + 1) * 64],
                         out=(6 + (h // 2) % 2, 64 * (h % 2), 0), last=h % 2 == 1, tile=h // 2) for h in range(C_HEADS)]

        def block2_heads(k0, n_tiles):
            t0 = k0 // P
            kk = slice(k0, k0 + n_tiles * P)
            heads = []
            for h in range(4):
                heads.append(dict(q=lambda c, h=h: QM[0:MLA_QK, h, c * P:(c + 1) * P], keys=lambda n, h=h: KM[0:MLA_QK, h, kk],
                                  v=lambda s, h=h: VM[:, t0 + s, h * 64:(h + 1) * 64],
                                  out=(6 + (h // 2) % 2, 64 * (h % 2), 0), last=h % 2 == 1, tile=h // 2, kind="mla"))
            for pair in range(2):
                for j in (2 * pair, 2 * pair + 1):
                    for w in range(2):
                        h = 2 * j + w
                        r = 32 * (h % 4)
                        heads.append(dict(q=lambda c, h=h, r=r: QD[r:r + 32, h // 4, c * P:(c + 1) * P],
                                          keys=lambda n, h=h, r=r: KD2[r:r + 32, h // 4, kk],
                                          v=lambda s, j=j: VD[:, t0 + s, j * 64:(j + 1) * 64],
                                          out=(6 + pair, 64 * (j % 2), w), last=j % 2 == 1 and w == 1, tile=2 + pair,
                                          kind="diff"))
            for h in range(8):
                r = 64 * (h // 4)
                heads.append(dict(q=lambda c, h=h, r=r: QG[r:r + 64, h % 4, c * P:(c + 1) * P],
                                  keys=lambda n, r=r: KG[r:r + 64, kk],
                                  v=lambda s, h=h: VG[:, t0 + s, (h // 4) * 64:(h // 4) * 64 + 64],
                                  out=(6 + (h // 2) % 2, 64 * (h % 2), 0), last=h % 2 == 1, tile=4 + h // 2, kind="gqa"))
            return heads

        def heads_and_keys(kind):
            if kind == "odd":
                return odd_heads(), lambda c: c + 1
            if kind == "context":
                return block2_heads(T, 2), lambda c: 2
            return block2_heads(0, 4), lambda c: 4

        ROPED = [("rot_mla", "cos_mla", "sin_mla", MLA_QK, QM[0:MLA_QK, 0:2, :]),
                 ("rot_mla", "cos_mla", "sin_mla", MLA_QK, QM[0:MLA_QK, 2:4, :]),
                 ("rot_mla", "cos_mla", "sin_mla", MLA_QK, KPE[0:MLA_QK].unsqueeze(1)),
                 ("rot_diff", "cos_diff", "sin_diff", P, QD),
                 ("rot_diff", "cos_diff", "sin_diff", P, KD2[:, :, 0:T]),
                 ("rot_gqa", "cos_gqa", "sin_gqa", P, QG[:, 0:2, :]),
                 ("rot_gqa", "cos_gqa", "sin_gqa", P, QG[:, 2:4, :]),
                 ("rot_gqa", "cos_gqa", "sin_gqa", P, KG[:, 0:T].unsqueeze(1))]

        @block.sync
        def _(sp):
            sp.dma_start(vec[:], vecs).then_inc(ev("vec_in"), 16)
            n = 0
            split = 0

            def load(first, c, it, slot, wait):
                if wait:
                    sp.wait_ge(lo_done, c)
                sp.dma_start(raw[:, slot, :], w_packs[it]).then_inc(raw_in[slot], 16)

            for first, count in stream_order():
                done = 0
                while done < count:
                    loops = (count - done) // RING
                    if n >= RING and loops > 1:
                        with sp.Fori(0, loops) as i:
                            for j in range(RING):
                                load(first, i * RING + (n + j - RING + 1), i * RING + (first + done + j), (n + j) % RING, True)
                        n += loops * RING
                        done += loops * RING
                    else:
                        load(first, n - RING + 1, first + done, n % RING, n >= RING)
                        n += 1
                        done += 1
                    if n == RING:
                        sp.dma_start(mat[:], mats).then_inc(ev("mat_in"), 16)
                        sp.dma_start(lat[:].rearrange("p k t -> p (k t)"), x_t).then_inc(ev("lat_in"), 16)
                        sp.dma_start(con[:].rearrange("p k t -> p (k t)"), ctx_t).then_inc(ev("con_in"), 16)
                        sp.dma_start(WS.rearrange("p a b -> p (a b)"), w_s_t).then_inc(ev("ws_in"), 16)
                        sp.dma_start(BS.rearrange("p a b -> p (a b)"), b_s_row.partition_broadcast(P)).then_inc(ev("bs_in"), 16)
                        sp.dma_start(LNG, ln_g_row.partition_broadcast(P)).then_inc(ev("lng_in"), 16)
                        sp.dma_start(LNB, ln_b_row.partition_broadcast(P)).then_inc(ev("lnb_in"), 16)
                        sp.dma_start(GUP, gate_up).then_inc(ev("gup_in"), 16)
            assert n == TOTAL
            sp.wait_ge(ev("out_ready"), 1)
            sp.dma_start(out_t, lat[:].rearrange("p k t -> p (k t)")).then_inc(ev("stored"), 16)
            sp.wait_ge(ev("stored"), 16)

        @block.tensor
        def _(pe):
            seen = Seen()
            pos = [0]
            lin = [0]

            def mm3(out, a_hi, a_lo, first, last, w_slot, cols, swap=False, check=False):
                hi, lo = w_hi[:, w_slot, cols], w_lo[:, w_slot, cols]
                for n, (x, y) in enumerate(((hi, a_hi), (hi, a_lo), (lo, a_hi))):
                    if swap:
                        x, y = y, x
                    ins = pe.matmul(out, x, y, start=first and n == 0, stop=last and n == 2, skip_group_check=check)
                return ins

            def linear(kt=KT, tokens=False, rhs=(h_hi, h_lo)):
                s = pos[0] % RING
                pe.wait_ge(lo_done, pos[0] + 1)
                if lin[0] >= 2:
                    pe.wait_ge(ev("lin_read"), lin[0] - 1)
                b = 4 + lin[0] % 2
                if tokens:
                    for tk in range(2):
                        for k in range(kt):
                            ins = mm3(psum[b][:, tk * P:(tk + 1) * P], rhs[0][:, k, tk * P:(tk + 1) * P],
                                      rhs[1][:, k, tk * P:(tk + 1) * P], k == 0, k == kt - 1, s,
                                      slice(k * P, (k + 1) * P), swap=True)
                else:
                    for k in range(kt):
                        ins = mm3(half(b, 0), rhs[0][:, k, :], rhs[1][:, k, :], k == 0, k == kt - 1, s,
                                  slice(k * P, (k + 1) * P))
                ins.then_inc(pack_used, 1)
                pos[0] += 1
                lin[0] += 1

            def lin_all_read():
                pe.wait_ge(ev("lin_read"), lin[0])

            def norm_sum(tiles=KT):
                for k in range(tiles):
                    if k % 2 == 0:
                        pe.wait_ge(ev("squares"), seen.next(ev("squares")))
                    ins = pe.matmul(half(6, 0), M("ones"), sq[:, k, :], start=k == 0, stop=k == tiles - 1)
                ins.then_inc(ev("sum_ready"), 1)

            def ffn(steps):
                base = pos[0]
                up_base = seen.now(ev("act_ready"))

                def up(s, par, p):
                    if not isinstance(s, int) or up_base + s >= 2:
                        pe.wait_ge(ev("act_ready"), up_base + s - 1)
                    for w in range(2):
                        pe.wait_ge(lo_done, p + w + 1)
                        slot = (base + (3 * par[1] - 1 if par[1] else 0) + w) % RING
                        for k in range(KT):
                            ins = mm3(half(4 + par[0], w), h_hi[:, k, :], h_lo[:, k, :], k == 0, k == KT - 1,
                                      slot, slice(k * P, (k + 1) * P))
                        ins.then_inc(pack_used, 1)

                def down(s, par, p, first=False, last=False):
                    pe.wait_ge(lo_done, p + 1)
                    pe.wait_ge(ev("act_ready"), up_base + s + 1)
                    slot = (base + par[1]) % RING
                    for m in range(KT):
                        ins = mm3(half(m // 2, m % 2), f_hi[:, par[0], :], f_lo[:, par[0], :],
                                  first and m % 2 == 0, last, slot, slice(m * P, (m + 1) * P), check=True)
                    ins.then_inc(pack_used, 1)

                up(0, (0, 0), base)
                up(1, (1, 1), base + 2)
                down(0, (0, 4), base + 4, first=True)
                assert (steps - 2) % 2 == 0
                with pe.Fori(0, (steps - 2) // 2) as i:
                    for j in range(2):
                        up(i * 2 + (2 + j), (j, 2 + j), i * 6 + (base + 5 + 3 * j))
                        down(i * 2 + (1 + j), ((1 + j) % 2, 7 + 3 * j), i * 6 + (base + 7 + 3 * j))
                down(steps - 1, ((steps - 1) % 2, 3 * steps - 1), base + 3 * steps - 1, last=True)
                pos[0] = base + 3 * steps
                seen.next(ev("act_ready"), steps)

            def attention(kind):
                heads, n_keys = heads_and_keys(kind)
                units = [(i, c) for i in range(len(heads)) for c in range(2)]
                lin_all_read()
                pe.wait_ge(ev("qk_ready"), seen.next(ev("qk_ready")))

                def scores(u):
                    i, c = units[u]
                    hd, n = heads[i], n_keys(c) * P
                    if u >= 2:
                        pe.wait_ge(ev("exp_done"), seen.now(ev("exp_done")) + u - 1)
                    out = psum[u % 2][:, 0:n]
                    if kind == "odd":
                        hh = hd["h"]
                        pick = M("head_id")[0:C_HEADS, hh:hh + 1]
                        pe.matmul(out, hd["q"](c), hd["keys"](n), start=True, stop=False)
                        pe.matmul(out, OC[0:C_HEADS, c * P:(c + 1) * P], pick.to_broadcast([C_HEADS, n]), start=False, stop=False)
                        pe.matmul(out, pick.to_broadcast([C_HEADS, P]), ONC[0:C_HEADS, 0:n], start=False, stop=True)\
                          .then_inc(ev("scores_done"), 1)
                    else:
                        pe.matmul(out, hd["q"](c), hd["keys"](n), start=True, stop=True).then_inc(ev("scores_done"), 1)

                def turn(u):
                    i, c = units[u]
                    pe.wait_ge(ev("prob_ready"), seen.now(ev("prob_ready")) + u + 1)
                    if u >= 2:
                        pe.wait_ge(ev("prob_t_ready"), seen.now(ev("prob_t_ready")) + u - 1)
                    for s in range(n_keys(c)):
                        ins = pe.transpose(psum[2 + u % 2][:, s * P:(s + 1) * P], prob[:, u % 2, s * P:(s + 1) * P], M("ident"))
                    ins.then_inc(ev("turned"), 1)

                def values(i):
                    hd = heads[i]
                    bank, row, w = hd["out"]
                    pe.wait_ge(ev("prob_t_ready"), seen.now(ev("prob_t_ready")) + 2 * i + 2)
                    pair = sum(h["last"] for h in heads[:i])
                    if pair >= 2:
                        pe.wait_ge(ev("pair_read"), seen.now(ev("pair_read")) + pair - 1)
                    pt = prob_t[:, i % 2, :].rearrange("p (s t) -> p s t", t=T)
                    ns = n_keys(1)
                    for s in range(ns):
                        c0 = 0 if n_keys(0) > s else 1
                        ins = pe.matmul(psum[bank][row:row + 64, w * T + c0 * P:(w + 1) * T], hd["v"](s), pt[:, s, c0 * P:T],
                                        start=s == 0, stop=s == ns - 1)
                    ins.then_inc(ev("value_done"), 1)

                scores(0)
                for u in range(len(units)):
                    if u + 1 < len(units):
                        scores(u + 1)
                    turn(u)
                    if u % 2 == 0 and u >= 2:
                        values(u // 2 - 1)
                values(len(heads) - 1)
                seen.next(ev("exp_done"), len(units))
                seen.next(ev("prob_ready"), len(units))
                seen.next(ev("prob_t_ready"), len(units))
                seen.next(ev("pair_read"), sum(h["last"] for h in heads))

            pe.wait_ge(ev("cond_ready"), seen.next(ev("cond_ready")))

            def ada(j, p, col):
                pe.wait_ge(lo_done, p + 1)
                for k in range(KT):
                    ins = mm3(psum[7][:, col], cond_hi[:, k, :], cond_lo[:, k, :], k == 0, k == KT - 1, j,
                              slice(k * P, (k + 1) * P))
                ins.then_inc(pack_used, 1)

            with pe.Fori(0, 2 * N_ADA // RING) as i:
                for j in range(RING):
                    ada(j, i * RING + j, bass.ds(i * (2 * RING) + 2 * j, 2))
            pos[0] = 2 * N_ADA
            pe.wait_ge(ev("mat_in"), 16)
            pe.wait_ge(ev("lam_prod"), seen.next(ev("lam_prod")))
            pe.matmul(psum[6][:, 0:4], M("ones")[0:32, :], small[0:32, 0:4], start=True, stop=True).then_inc(ev("lam_sum"), 1)

            norm_sum()
            pe.wait_ge(ev("h_ready"), seen.next(ev("h_ready"), KT))
            for n in range(N_EVEN_IN):
                linear(tokens=5 <= n < 13)
            lin_all_read()
            pe.wait_ge(ev("gup_in"), 16)
            for t in range(2):
                ins = pe.matmul(half(6, t), GUP[:, t * P:(t + 1) * P], GLR[0:RANK, :], start=True, stop=True)
            ins.then_inc(ev("gate_done"), 1)
            pe.wait_ge(ev("vn_ready"), 1)
            pe.wait_ge(ev("ws_ready"), 1)
            for g in range(4):
                for c in range(2):
                    ins = pe.matmul(psum[2 + g // 2][:, (g % 2) * T + c * P:(g % 2) * T + (c + 1) * P],
                                    VN[:, c, g * P:(g + 1) * P], WS[:, g, :], start=True, stop=True)
            ins.then_inc(ev("spatial_done"), 1)
            pe.wait_ge(ev("decays_ready"), 1)
            for t in range(2):
                ins = pe.transpose(psum[7][:, t * P:(t + 1) * P], KD[:, t, :], M("ident"))
            ins.then_inc(ev("kd_turned"), 1)
            for par in range(2):
                r = 64 * par
                for t in range(2):
                    for c in range(2):
                        for i in range(4):
                            ins = pe.matmul(psum[par][:, (t * 2 + c) * P + i * SUB:(t * 2 + c) * P + (i + 1) * SUB],
                                            EK[r:r + 64, t, c * 4 + i, :], QQ[r:r + 64, t, c * P + i * SUB:c * P + (i + 1) * SUB],
                                            start=True, stop=True)
            ins.then_inc(ev("gla_scores"), 1)
            pe.wait_ge(ev("kdt_ready"), 1)
            for h in range(4):
                r = 64 * (h % 2)
                ins = pe.matmul(psum[6][r:r + 64, (h // 2) * P:(h // 2 + 1) * P], KDT[:, h // 2, r:r + 64], VB[:, 0, h * P:(h + 1) * P],
                                start=True, stop=True)
            ins.then_inc(ev("state_done"), 1)
            pe.wait_ge(ev("state_ready"), 1)
            pe.wait_ge(ev("ats_ready"), 1)
            for h in range(4):
                r = 64 * (h % 2)
                for c in range(2):
                    o = psum[4 + h % 2][:, (h // 2) * T + c * P:(h // 2) * T + (c + 1) * P]
                    ins = pe.matmul(o, VB[:, c, h * P:(h + 1) * P], ATS[:, h % 2, (h // 2) * 2 + c, :], start=True, stop=c == 0)
                    if c == 1:
                        ins = pe.matmul(o, ST[r:r + 64, h // 2, :], QI[r:r + 64, h // 2, :], start=False, stop=True)
            ins.then_inc(ev("gla_out"), 1)
            pe.wait_ge(ev("squares"), seen.next(ev("squares")))
            for b in range(2):
                ins = pe.matmul(psum[b][:, :], M("ones"), sq[:, 2 * b:2 * b + 2, :], start=True, stop=True)
            ins.then_inc(ev("sum_ready"), 1)
            pe.wait_ge(ev("h_ready"), seen.next(ev("h_ready"), KT))
            for m in range(KT):
                linear()
            norm_sum()
            pe.wait_ge(ev("h_ready"), seen.next(ev("h_ready"), KT))
            lin_all_read()
            ffn(FF_STEPS)
            norm_sum()
            pe.wait_ge(ev("h_ready"), seen.next(ev("h_ready"), KT))
            for n in range(N_ODD_IN):
                linear(tokens=17 <= n < 25)
            for _ in range(2):
                pe.wait_ge(ev("squares"), seen.next(ev("squares")))
                for k in range(8):
                    ins = pe.matmul(half(k // 2, k % 2), M("block64"), sq[:, k, :], start=True, stop=True)
                ins.then_inc(ev("sum_ready"), 1)
            attention("odd")
            pe.wait_ge(ev("h_ready"), seen.next(ev("h_ready"), KT))
            for m in range(KT):
                linear()
            norm_sum()
            pe.wait_ge(ev("h_ready"), seen.next(ev("h_ready"), KT))
            linear(tokens=True)
            pe.wait_ge(ev("gates_ready"), 1)
            for t in range(2):
                ins = pe.transpose(psum[7][0:N_EXP, t * P:(t + 1) * P], GATE[:, t, :], M("ident"))
            ins.then_inc(ev("gates_turned"), 1)
            pe.wait_ge(ev("gt_ready"), 1)
            for e in range(N_EXP):
                ins = pe.matmul(half(e // 2, e % 2), M("pick")[0:N_EXP, e * P:(e + 1) * P], GT[0:N_EXP, :], start=True, stop=True)
            ins.then_inc(ev("gates_spread"), 1)
            pe.wait_ge(ev("gb_ready"), 1)
            lin_all_read()
            ffn(MOE_STEPS)
            norm_sum()
            for l in range(2):
                for stream in ("context", "latents"):
                    only_kv = l == 1 and stream == "context"
                    norm_sum()
                    pe.wait_ge(ev("h_ready"), seen.next(ev("h_ready"), KT))
                    for n in range(N_IN_KV if only_kv else N_IN):
                        linear(tokens=5 <= n < 8)
                    pe.wait_ge(ev("squares"), seen.next(ev("squares")))
                    pe.matmul(half(0, 0), M("ones"), sq[:, 0, :], start=True, stop=True)
                    ins = pe.matmul(half(1, 0), M("block64"), sq[:, 1, :], start=True, stop=True)
                    if not only_kv:
                        for k in range(4):
                            pe.matmul(half(2 + k // 2, k % 2), M("block64"), sq[:, 2 + k, :], start=True, stop=True)
                        pe.matmul(half(0, 1), M("ones"), sq[:, 6, :], start=True, stop=False)
                        ins = pe.matmul(half(0, 1), M("ones"), sq[:, 7, :], start=False, stop=True)
                    ins.then_inc(ev("sum_ready"), 1)
                    pe.wait_ge(ev("latent_split"), seen.next(ev("latent_split")))
                    lin_all_read()
                    pe.wait_ge(lo_done, pos[0] + 1)
                    s = pos[0] % RING
                    for h in range(4):
                        mm3(half(h // 2, h % 2), h_hi[:, 0, :], h_lo[:, 0, :], True, True, s, slice(h * P, (h + 1) * P))
                    vh = w_hi[:, s, 0:512].rearrange("p (h c) -> p h c", h=4)[:, :, 64:128]
                    vl = w_lo[:, s, 0:512].rearrange("p (h c) -> p h c", h=4)[:, :, 64:128]
                    for tk in range(2):
                        tt = slice(tk * P, (tk + 1) * P)
                        pe.matmul(half(6, tk), h_hi[:, 0, tt], vh, start=True, stop=False)
                        pe.matmul(half(6, tk), h_lo[:, 0, tt], vh, start=False, stop=False)
                        ins = pe.matmul(half(6, tk), h_hi[:, 0, tt], vl, start=False, stop=True)
                    ins.then_inc(pack_used, 1)
                    pos[0] += 1
                    if not only_kv:
                        pe.wait_ge(lo_done, pos[0] + 1)
                        s = pos[0] % RING
                        for h in range(4):
                            for k in range(2):
                                ins = mm3(half(2 + h // 2, h % 2), h_hi[:, 1 + k, :], h_lo[:, 1 + k, :], k == 0, k == 1, s,
                                          slice((2 * h + k) * P, (2 * h + k + 1) * P))
                        ins.then_inc(pack_used, 1)
                        pos[0] += 1
                    if stream == "latents":
                        pe.wait_ge(ev("rope_in"), seen.next(ev("rope_in")))
                        for n, (rot, _, _, rows, x) in enumerate(ROPED):
                            if n >= 2:
                                pe.wait_ge(ev("rope_out"), seen.now(ev("rope_out")) + n - 1)
                            width = x.shape[1] * T
                            pe.matmul(psum[4 + n % 2][0:rows, 0:width], M(rot)[0:rows, 0:rows], x, start=True, stop=True)\
                              .then_inc(ev("rotated"), 1)
                        seen.next(ev("rope_out"), len(ROPED))
                    if only_kv:
                        continue
                    attention(stream)
                    pe.wait_ge(ev("squares"), seen.next(ev("squares")))
                    pe.matmul(psum[0][:, :], M("block64"), sq[:, 0:2, :], start=True, stop=True).then_inc(ev("sum_ready"), 1)
                    pe.wait_ge(ev("h_ready"), seen.next(ev("h_ready"), KT))
                    for m in range(KT):
                        linear()
                    norm_sum()
                    norm_sum()
                    pe.wait_ge(ev("h_ready"), seen.next(ev("h_ready"), KT))
                    lin_all_read()
                    ffn(FF_STEPS)
                    norm_sum()
            assert pos[0] == TOTAL

        @block.scalar
        def _(act):
            seen = Seen()
            steps = [0]
            nsplit = [0]
            nlin = [0]

            def A(out, in_, func, **kw):
                return act.activation(out, in_, func, **kw)

            def step(ins):
                steps[0] += 1
                ins.then_inc(ev("act_step"), 1)

            def settle():
                act.wait_ge(ev("act_step"), steps[0])

            def wait(name, n=1):
                act.wait_ge(ev(name), seen.next(ev(name), n))

            def split_at(p, slot, turn, reuse):
                act.wait_ge(raw_in[slot], 16 * turn + 16)
                if reuse:
                    act.wait_ge(pack_used, p - RING + 1)
                    act.wait_ge(lo_done, p - RING + 1)
                A(w_hi[:, slot, :], raw[:, slot, :], ACT.Copy).then_inc(hi_done, 1)

            def split_to(p):
                while nsplit[0] < min(p, TOTAL):
                    n = nsplit[0]
                    split_at(n, n % RING, n // RING, n >= RING)
                    nsplit[0] += 1

            def lin_wait():
                split_to(2 * N_ADA + nlin_pos[0] + AHEAD)
                nlin_pos[0] += 1
                act.wait_ge(pack_used, 2 * N_ADA + nlin_pos[0])
                b = 4 + nlin[0] % 2
                nlin[0] += 1
                return b

            nlin_pos = [0]
            nffn = [0]

            def fm(out, func=ACT.Copy, **kw):
                b = lin_wait()
                A(out, half(b, 0), func, **kw).then_inc(ev("lin_read"), 1)

            def tm(out, func=ACT.Copy, **kw):
                b = lin_wait()
                A(out, half(b, 0).rearrange("p (a b) -> p a b", a=2), func, **kw).then_inc(ev("lin_read"), 1)

            def rsqrt_of(out, in_, scale, bias, sem):
                step(A(out, in_, ACT.Ln, scale=scale, bias=bias))
                settle()
                A(out, out, ACT.Exp, scale=-0.5).then_inc(sem, 1)

            def norm(x, shift=None):
                for k in range(0, KT, 2):
                    A(sq[:, k:k + 2, :], x[:, k:k + 2, :], ACT.Square).then_inc(ev("squares"), 1)
                wait("sum_ready")
                rsqrt_of(rs[:], half(6, 0), 1.0 / D, V("eps"), ev("rs_ready"))
                if shift is not None:
                    for k in range(KT):
                        wait("scaled")
                        A(h_hi[:, k, :], tmp[:, k, :], ACT.Identity, bias=shift(k)).then_inc(ev("h_hi_ready"), 1)

            def split_tmp():
                for k in range(KT):
                    wait("scaled")
                    A(h_hi[:, k, :], tmp[:, k, :], ACT.Copy).then_inc(ev("h_hi_ready"), 1)

            def skip_linears(n):
                for _ in range(n):
                    split_to(2 * N_ADA + nlin_pos[0] + AHEAD)
                    nlin_pos[0] += 1
                    nlin[0] += 1

            def ffn(n_steps):
                base = nffn[0]
                first = 2 * N_ADA + nlin_pos[0]
                split_to(first + AHEAD)
                p0 = nsplit[0]

                def one(s, par, off, it):
                    act.wait_ge(pack_used, first + 2 if isinstance(s, int) and s == 0 else s * 3 + (first + 1))
                    if not isinstance(s, int) or base + s >= 2:
                        act.wait_ge(ev("act_ready"), base + s - 1)
                    A(sg[:, par, :], half(4 + par, 0), ACT.Silu).then_inc(ev("silu_done"), 1)
                    for j in range(3):
                        p = p0 + off + j
                        if isinstance(s, int) and p >= TOTAL:
                            continue
                        slot = p % RING
                        split_at(it * RING + p if it is not None else p, slot,
                                 (it + p // RING) if it is not None else p // RING, True)

                last = p0 + 3 * n_steps >= TOTAL
                head, tail = 2, 4 if last else 0
                for s in range(head):
                    one(s, s % 2, 3 * s, None)
                with act.Fori(0, (n_steps - head - tail) // 2) as i:
                    for j in range(2):
                        one(i * 2 + (head + j), j, 3 * (head + j), i)
                for s in range(n_steps - tail, n_steps):
                    one(s, s % 2, 3 * s, None)
                nffn[0] += n_steps
                nsplit[0] = min(p0 + 3 * n_steps, TOTAL)
                nlin_pos[0] += 3 * n_steps

            def attention(kind):
                heads, n_keys = heads_and_keys(kind)
                for u in range(2 * len(heads) + 1):
                    if u < 2 * len(heads):
                        n = n_keys(u % 2) * P
                        wait("max_ready")
                        src = logit[:, u % 2, 0:n] if kind == "odd" else psum[u % 2][:, 0:n]
                        A(prob[:, u % 2, 0:n], src, ACT.Exp, bias=small[:, 8 + u % 2:9 + u % 2],
                          accum_out=small[:, 10 + u % 2:11 + u % 2]).then_inc(ev("exp_done"), 1)
                    if u >= 1:
                        v = u - 1
                        c, i = v % 2, v // 2
                        ns = n_keys(c)
                        wait("turned")
                        if i >= 2:
                            act.wait_ge(ev("value_done"), seen.now(ev("value_done")) + i - 1)
                        out = prob_t[:, i % 2, :].rearrange("p (s t) -> p s t", t=T)[:, 0:ns, c * P:(c + 1) * P]
                        A(out, psum[2 + v % 2][:, 0:ns * P].rearrange("p (s t) -> p s t", t=P), ACT.Copy)\
                            .then_inc(ev("prob_t_ready"), 1)
                seen.next(ev("value_done"), len(heads))

            act.wait_ge(ev("vec_in"), 16)
            A(cond_s[:].rearrange("p k s -> p (k s)"), V("cond"), ACT.Silu).then_inc(ev("cond_silu"), 1)
            split_to(RING)
            with act.Fori(0, (2 * N_ADA - RING) // RING) as i:
                for j in range(RING):
                    split_at(i * RING + (RING + j), j, i + 1, True)
            nsplit[0] = 2 * N_ADA
            split_to(2 * N_ADA + AHEAD)
            wait("lam_sum")
            A(small[:, 4:8], psum[6][:, 0:4], ACT.Exp).then_inc(ev("lam_exp"), 1)
            act.wait_ge(ev("lat_in"), 16)
            norm(lat, lambda k: V("zero"))
            fm(GLR)
            for t in range(2):
                fm(QT[:, t, :], scale=0.125)
            for t in range(2):
                fm(KTT[:, t, :])
            for t in range(4):
                tm(VB[:, :, t * P:(t + 1) * P])
            for t in range(4):
                tm(VA[:, :, t * P:(t + 1) * P], ACT.Gelu_apprx_tanh)
            for t in range(4):
                fm(U[:, t, :], ACT.Gelu_apprx_tanh)
            for t in range(4):
                fm(OG[:, t, :], ACT.Silu)
            wait("gate_done")
            for t in range(2):
                A(GX[:, t, :], half(6, t), ACT.Identity, bias=V("gate_bias", t)).then_inc(ev("gx_ready"), 1)
            wait("abs_ready")
            step(A(QQ, QQ, ACT.Exp))
            settle()
            A(QQ, QQ, ACT.Ln, bias=V("one")).then_inc(ev("softplus_ready"), 1)
            wait("var_ready")
            step(A(small[:, 16:18], small[:, 16:18], ACT.Ln, bias=V("eps")))
            settle()
            A(small[:, 16:18], small[:, 16:18], ACT.Exp, scale=-0.5).then_inc(ev("rstd_ready"), 1)
            wait("diffs_ready")
            A(EK, EK, ACT.Exp, scale=-1.0 / 16).then_inc(ev("exps_ready"), 1)
            A(QQ, QQ, ACT.Exp, scale=1.0 / 16).then_inc(ev("exps_ready"), 1)
            A(QI, G[:, :, P:2 * P], ACT.Exp, scale=1.0 / 16).then_inc(ev("exps_ready"), 1)
            A(KD, KD, ACT.Exp, scale=-1.0 / 16).then_inc(ev("exps_ready"), 1)
            wait("gla_out")
            for b in range(2):
                ins = A(sq[:, b:4:2, :], psum[4 + b][:, :].rearrange("p (a t) -> p a t", a=2), ACT.Square)
                if b == 1:
                    ins.then_inc(ev("squares"), 1)
            for b in range(2):
                step(A(tmp[:, b:4:2, :], psum[4 + b][:, :].rearrange("p (a t) -> p a t", a=2), ACT.Copy))
            settle()
            wait("sum_ready")
            for b in range(2):
                step(A(sq[:, 4 + 2 * b:6 + 2 * b, :], psum[b][:, :].rearrange("p (a t) -> p a t", a=2), ACT.Ln,
                       scale=1.0 / P, bias=V("eps")))
            settle()
            A(sq[:, 4:8, :], sq[:, 4:8, :], ACT.Exp, scale=-0.5).then_inc(ev("rs_ready"), 1)
            split_tmp()
            skip_linears(KT)
            wait("x_ready")
            norm(lat, lambda k: V("zero"))
            ffn(FF_STEPS)
            wait("x_ready")
            norm(lat, lambda k: V("zero"))
            fm(OF)
            for t in range(8):
                fm(OQ[:, t, :])
            for t in range(8):
                fm(OK[:, t, :])
            for t in range(8):
                tm(OV[:, :, t * P:(t + 1) * P])
            for t in range(8):
                fm(OO[:, t, :], ACT.Sigmoid)
            act.wait_ge(ev("lin_read"), nlin[0])
            A(OF[0:C_HEADS], OF[0:C_HEADS], ACT.Identity, bias=V("forget_bias")[0:C_HEADS]).then_inc(ev("f_ready"), 1)
            wait("abs_ready")
            step(A(ONC[0:C_HEADS], ONC[0:C_HEADS], ACT.Exp))
            settle()
            A(ONC[0:C_HEADS], ONC[0:C_HEADS], ACT.Ln, bias=V("one")[0:C_HEADS]).then_inc(ev("softplus_ready"), 1)
            for which, x in enumerate((OQ, OK)):
                if which:
                    wait("qk_scaled")
                A(sq[:], x, ACT.Square).then_inc(ev("squares"), 1)
                wait("sum_ready")
                for b in range(4):
                    step(A(sq[:, 2 * b:2 * b + 2, :], psum[b][:, :].rearrange("p (a t) -> p a t", a=2), ACT.Ln,
                           scale=1.0 if which == 0 else 1.0 / 64, bias=V("eps64") if which == 0 else V("eps")))
                settle()
                A(sq[:], sq[:], ACT.Exp, scale=-0.5).then_inc(ev("rs_ready"), 1)
            attention("odd")
            split_tmp()
            skip_linears(KT)
            wait("x_ready")
            norm(lat, lambda k: V("zero"))
            tm(RL)
            wait("top_diff")
            A(small[:, 24:26], small[:, 24:26], ACT.Exp).then_inc(ev("top_exp"), 1)
            ffn(MOE_STEPS)
            wait("x_ready")
            norm(lat)
            for l in range(2):
                for s, (stream, x) in enumerate((("context", con), ("latents", lat))):
                    only_kv = l == 1 and stream == "context"
                    k0 = T if stream == "context" else 0
                    col = 1 - s
                    if (l, s) == (0, 0):
                        act.wait_ge(ev("con_in"), 16)
                        wait("x_ready")
                    norm(x, lambda k: mod[:, l, k, col:col + 1])
                    fm(ZR[:, 0, :])
                    fm(KPE)
                    for t in range(2):
                        fm(KD2[:, t, k0:k0 + T])
                    fm(ZR[:, 1, :])
                    for t in range(2):
                        tm(VD[:, k0 // P:k0 // P + 2, t * P:(t + 1) * P])
                    tm(VG[:, k0 // P:k0 // P + 2, :])
                    if not only_kv:
                        for t in range(2):
                            fm(ZR[:, 6 + t, :])
                        for t in range(2):
                            fm(QD[:, t, :], scale=DIFF_SCALE)
                        for t in range(4):
                            fm(ZR[:, 2 + t, :])
                    act.wait_ge(ev("lin_read"), nlin[0])
                    n = 2 if only_kv else 8
                    A(sq[:, 0:n, :], ZR[:, 0:n, :], ACT.Square).then_inc(ev("squares"), 1)
                    wait("sum_ready")
                    step(A(sq[:, 0, :], half(0, 0), ACT.Ln, scale=1.0 / 128, bias=V("eps")))
                    step(A(sq[:, 1, :], half(1, 0), ACT.Ln, scale=1.0 / 64, bias=V("eps")))
                    if not only_kv:
                        for b in range(2):
                            step(A(sq[:, 2 + 2 * b:4 + 2 * b, :], psum[2 + b][:, :].rearrange("p (a t) -> p a t", a=2),
                                   ACT.Ln, scale=1.0, bias=V("eps64")))
                        step(A(sq[:, 6, :], half(0, 1), ACT.Ln, scale=1.0 / 256, bias=V("eps")))
                    settle()
                    n = 2 if only_kv else 7
                    A(sq[:, 0:n, :], sq[:, 0:n, :], ACT.Exp, scale=-0.5).then_inc(ev("rs_ready"), 1)
                    wait("latents_normed")
                    n = 1 if only_kv else 3
                    A(h_hi[:, 0:n, :], tmp[:, 0:n, :], ACT.Copy).then_inc(ev("latents_hi"), 1)
                    split_to(2 * N_ADA + nlin_pos[0] + AHEAD)
                    nlin_pos[0] += 1
                    act.wait_ge(pack_used, 2 * N_ADA + nlin_pos[0])
                    for b in range(2):
                        A(KM[0:64, 2 * b:2 * b + 2, k0:k0 + T], psum[b][0:64, :].rearrange("p (a t) -> p a t", a=2), ACT.Copy)\
                            .then_inc(ev("km_ready"), 1)
                    A(VM[:, k0 // P:k0 // P + 2, :], psum[6][:, :].rearrange("p (a t) -> p a t", a=2), ACT.Copy)\
                        .then_inc(ev("km_ready"), 1)
                    if not only_kv:
                        split_to(2 * N_ADA + nlin_pos[0] + AHEAD)
                        nlin_pos[0] += 1
                        act.wait_ge(pack_used, 2 * N_ADA + nlin_pos[0])
                        for b in range(2):
                            A(QM[0:MLA_QK, 2 * b:2 * b + 2, :], psum[2 + b][0:MLA_QK, :].rearrange("p (a t) -> p a t", a=2),
                              ACT.Copy, scale=MLA_SCALE).then_inc(ev("qm_ready"), 1)
                    if only_kv:
                        wait("context_keys_ready")
                        continue
                    attention(stream)
                    wait("diff_ready")
                    A(sq[:, 0:2, :], tmp[:, 2:4, :], ACT.Square).then_inc(ev("squares"), 1)
                    wait("sum_ready")
                    step(A(sq[:, 2:4, :], psum[0][:, :].rearrange("p (a t) -> p a t", a=2), ACT.Ln, scale=1.0 / 64, bias=V("eps")))
                    settle()
                    A(sq[:, 2:4, :], sq[:, 2:4, :], ACT.Exp, scale=-0.5).then_inc(ev("rs_ready"), 1)
                    split_tmp()
                    for m in range(KT):
                        fm(ZR[:, m, :])
                    act.wait_ge(ev("lin_read"), nlin[0])
                    norm(ZR)
                    wait("x_ready")
                    norm(x, lambda k: mod[:, l, 24 + k, col:col + 1])
                    ffn(FF_STEPS)
                    act.wait_ge(pack_used, 2 * N_ADA + nlin_pos[0])
                    for b in range(4):
                        step(A(ZR[:, 2 * b:2 * b + 2, :], psum[b][:, :].rearrange("p (a t) -> p a t", a=2), ACT.Copy))
                    settle()
                    norm(ZR)
                    wait("x_ready")

        @block.vector
        def _(v):
            seen = Seen()
            steps = [0]
            nsplit = [0]
            npos = [0]
            nlin = [0]

            def step(ins):
                steps[0] += 1
                ins.then_inc(ev("dve_step"), 1)

            def settle():
                v.wait_ge(ev("dve_step"), steps[0])

            def link(ins):
                step(ins)
                settle()

            def wait(name, n=1):
                v.wait_ge(ev(name), seen.next(ev(name), n))

            def split_at(p, slot, reuse):
                v.wait_ge(hi_done, p + 1)
                if reuse:
                    v.wait_ge(pack_used, p - RING + 1)
                v.tensor_tensor(w_lo[:, slot, :], raw[:, slot, :], w_hi[:, slot, :].bitcast(F32), ALU.subtract)\
                    .then_inc(lo_done, 1)

            def split_to(p):
                while nsplit[0] < min(p, TOTAL):
                    n = nsplit[0]
                    split_at(n, n % RING, n >= RING)
                    nsplit[0] += 1

            def norm(x, gain, shift=None, out=None):
                wait("rs_ready")
                out = tmp if out is None else out
                for k in range(KT):
                    ins = v.scalar_tensor_tensor(out[:, k, :], x[:, k, :], gain(k), rs[:], ALU.mult, ALU.mult)
                    if shift is not None:
                        ins.then_inc(ev("scaled"), 1)
                    else:
                        step(ins)
                if shift is None:
                    settle()
                    return
                for k in range(KT):
                    wait("h_hi_ready")
                    v.scalar_tensor_tensor(h_lo[:, k, :], tmp[:, k, :], shift(k), h_hi[:, k, :].bitcast(F32), ALU.add,
                                           ALU.subtract).then_inc(ev("h_ready"), 1)

            def low_part(k):
                wait("h_hi_ready")
                v.tensor_tensor(h_lo[:, k, :], tmp[:, k, :], h_hi[:, k, :].bitcast(F32), ALU.subtract)\
                    .then_inc(ev("h_ready"), 1)

            def others_read(n):
                for _ in range(n):
                    split_to(2 * N_ADA + npos[0] + AHEAD)
                    npos[0] += 1
                    nlin[0] += 1

            def add_linears(x):
                for m in range(KT):
                    split_to(2 * N_ADA + npos[0] + AHEAD)
                    npos[0] += 1
                    v.wait_ge(pack_used, 2 * N_ADA + npos[0])
                    b = 4 + nlin[0] % 2
                    nlin[0] += 1
                    v.tensor_tensor(x[:, m, :], x[:, m, :], half(b, 0), ALU.add).then_inc(ev("lin_read"), 1)
                v.wait_ge(ev("lin_read"), nlin[0])
                v.sem_inc(ev("x_ready"), 1)

            def ffn(n_steps, gated=False):
                base = seen.now(ev("silu_done"))
                start = 2 * N_ADA + npos[0]
                split_to(2 * N_ADA + npos[0] + AHEAD)
                p0 = nsplit[0]

                def one(s, par, off, it, e=None):
                    v.wait_ge(ev("silu_done"), base + s + 1)
                    if not isinstance(s, int) or base + s >= 2:
                        v.wait_ge(pack_used, s * 3 + (start - 1))
                    v.tensor_tensor(prod[:, par, :], sg[:, par, :], half(4 + par, 1), ALU.mult).then_inc(ev("prod_done"), 1)
                    v.wait_ge(ev("prod_done"), base + s + 1)
                    if e is not None:
                        v.tensor_tensor(prod[:, par, :], prod[:, par, :], GB[:, e, :], ALU.mult).then_inc(ev("gated"), 1)
                        v.wait_ge(ev("gated"), base - FF_STEPS + s + 1)
                    v.tensor_copy(f_hi[:, par, :], prod[:, par, :]).then_inc(ev("f_hi_done"), 1)
                    v.wait_ge(ev("f_hi_done"), base + s + 1)
                    v.tensor_tensor(f_lo[:, par, :], prod[:, par, :], f_hi[:, par, :].bitcast(F32), ALU.subtract)\
                        .then_inc(ev("act_ready"), 1)
                    for j in range(3):
                        p = p0 + off + j
                        if isinstance(s, int) and p >= TOTAL:
                            continue
                        split_at(p if it is None else it * RING + p, p % RING, True)

                if gated:
                    with v.Fori(0, N_EXP) as e:
                        with v.Fori(0, EXP_STEPS // 2) as i:
                            for j in range(2):
                                it = e * (EXP_STEPS // 2) + i
                                one(it * 2 + j, j, 3 * j, it, e)
                else:
                    last = p0 + 3 * n_steps >= TOTAL
                    head, tail = 2, 4 if last else 0
                    for s in range(head):
                        one(s, s % 2, 3 * s, None)
                    with v.Fori(0, (n_steps - head - tail) // 2) as i:
                        for j in range(2):
                            one(i * 2 + (head + j), j, 3 * (head + j), i)
                    for s in range(n_steps - tail, n_steps):
                        one(s, s % 2, 3 * s, None)
                seen.next(ev("silu_done"), n_steps)
                nsplit[0] = min(p0 + 3 * n_steps, TOTAL)
                npos[0] += 3 * n_steps

            def log_sigmoid(x, t, out, n):
                v.scalar_tensor_tensor(t, x, -1.0, x, ALU.mult, ALU.min).then_inc(ev("abs_ready"), 1)
                wait("softplus_ready")
                link(v.scalar_tensor_tensor(out, x, 0.0, t, ALU.min, ALU.subtract))

            def attention(kind, pair_done):
                heads, n_keys = heads_and_keys(kind)
                pair = 0
                total = 2 * len(heads)

                def merged(i):
                    v.wait_ge(ev("value_done"), seen.now(ev("value_done")) + i + 1)
                    pair_done(heads[i])

                for u in range(total + 3):
                    if u < total:
                        c = u % 2
                        n = n_keys(c) * P
                        wait("scores_done")
                        src = psum[u % 2][:, 0:n]
                        if kind == "odd":
                            if u >= 2:
                                v.wait_ge(ev("exp_done"), seen.now(ev("exp_done")) + u - 1)
                            d = c * P
                            if c:
                                step(v.tensor_copy(logit[:, 1, 0:P], psum[u % 2][:, 0:P]))
                            link(v.tensor_tensor(logit[:, c, d:d + P], psum[u % 2][:, d:d + P], M("mask_add"), ALU.add))
                            src = logit[:, c, 0:n]
                        elif u >= 2:
                            v.wait_ge(ev("exp_done"), seen.now(ev("exp_done")) + u - 1)
                        v.tensor_reduce(small[:, 8 + u % 2:9 + u % 2], src, AX.X, ALU.max, negate=True).then_inc(ev("max_ready"), 1)
                    if 1 <= u <= total:
                        w = u - 1
                        n = n_keys(w % 2) * P
                        v.wait_ge(ev("exp_done"), seen.now(ev("exp_done")) + w + 1)
                        link(v.reciprocal(small[:, 12 + w % 2:13 + w % 2], small[:, 10 + w % 2:11 + w % 2]))
                        v.tensor_scalar(prob[:, w % 2, 0:n], prob[:, w % 2, 0:n], small[:, 12 + w % 2:13 + w % 2], None, ALU.mult)\
                            .then_inc(ev("prob_ready"), 1)
                    if u >= 4 and u % 2 == 0 and heads[u // 2 - 2]["last"]:
                        merged(u // 2 - 2)
                seen.next(ev("exp_done"), total)
                seen.next(ev("value_done"), len(heads))

            wait("cond_silu")
            link(v.tensor_copy(cond_hi[:], cond_s[:]))
            v.tensor_tensor(cond_lo[:], cond_s[:], cond_hi[:].bitcast(F32), ALU.subtract).then_inc(ev("cond_ready"), 1)
            v.wait_ge(ev("vec_in"), 16)
            for l in range(2):
                lam = V(f"lambdas{l}")
                ins = v.tensor_tensor(small[0:32, 2 * l:2 * l + 2], lam[0:32, 0:2], lam[0:32, 2:4], ALU.mult)
                if l == 1:
                    ins.then_inc(ev("lam_prod"), 1)
            split_to(RING)
            with v.Fori(0, (2 * N_ADA - RING) // RING) as i:
                for j in range(RING):
                    split_at(i * RING + (RING + j), j, True)
            nsplit[0] = 2 * N_ADA
            split_to(2 * N_ADA + AHEAD)
            wait("lam_exp")
            for l in range(2):
                link(v.tensor_tensor(neg_lam[:, l:l + 1], small[:, 4 + 2 * l + 1:6 + 2 * l], small[:, 4 + 2 * l:5 + 2 * l], ALU.subtract))
                link(v.tensor_scalar(neg_lam[:, l:l + 1], neg_lam[:, l:l + 1], -LAMBDA_INIT[l], None, ALU.add))
                link(v.tensor_scalar(g_sub[:, l:l + 1], V(f"g_sub{l}"), 1.0 - LAMBDA_INIT[l], None, ALU.mult))
                v.wait_ge(pack_used, 2 * N_ADA)
                src = psum[7][:, l * 96:(l + 1) * 96].rearrange("p (m s) -> p m s", s=2)
                link(v.tensor_tensor(mod[:, l, :, :], src, V(f"b_ada{l}").unsqueeze(2).to_broadcast([P, N_ADA, 2]), ALU.add))

                def g(name):
                    return V(name).unsqueeze(2).to_broadcast([P, KT, 2])
                link(v.scalar_tensor_tensor(gains[:, l, 0], mod[:, l, 8:16, :], 1.0, g(f"g_attn_pre{l}"), ALU.add, ALU.mult))
                link(v.tensor_tensor(gains[:, l, 1], mod[:, l, 16:24, :], g(f"g_attn_post{l}"), ALU.mult))
                link(v.scalar_tensor_tensor(gains[:, l, 2], mod[:, l, 32:40, :], 1.0, g(f"g_ffn_pre{l}"), ALU.add, ALU.mult))
                link(v.tensor_tensor(gains[:, l, 3], mod[:, l, 40:48, :], g(f"g_ffn_post{l}"), ALU.mult))
            v.wait_ge(ev("mat_in"), 16)
            v.wait_ge(ev("ws_in"), 16)
            v.tensor_tensor(WS, WS, M("mask01").unsqueeze(1).to_broadcast([P, 4, P]), ALU.mult).then_inc(ev("ws_ready"), 1)
            norm(lat, lambda k: V("g_even_mix", k), lambda k: V("zero"))
            others_read(N_EVEN_IN)
            v.wait_ge(ev("lin_read"), nlin[0])
            for c in range(2):
                link(v.bn_stats(small[:, 32 + 6 * c:38 + 6 * c], VA[:, c, :]))
                link(v.bn_aggr(small[:, 48 + 2 * c:50 + 2 * c], small[:, 32 + 6 * c:38 + 6 * c]))
            v.tensor_copy(small[:, 16:18], small[:, 49:52:2]).then_inc(ev("var_ready"), 1)
            wait("gx_ready", 2)
            log_sigmoid(GX, QQ, GX, T)
            link(v.memset(sq[:, 0, :], 1.0))
            for t in range(2):
                for c in range(2):
                    cc = slice(c * P, (c + 1) * P)
                    step(v.tensor_tensor_scan(G[:, t, cc], sq[:, 0, cc], GX[:, t, cc], 0.0, ALU.mult, ALU.add))
            link(v.memset(small[:, 32:48], 0.0))
            ref = small[:, 32:48].rearrange("p (t c i) -> p t c i", t=2, c=2)
            for t in range(2):
                for c in range(2):
                    step(v.tensor_copy(ref[:, t, c, 1:4], G[:, t, c * P + SUB - 1:c * P + 3 * SUB:SUB]))
            settle()
            for t in range(2):
                for c in range(2):
                    g3 = G[:, t, c * P:(c + 1) * P].unsqueeze(1).to_broadcast([P, 4, P])
                    r3 = ref[:, t, c, :].unsqueeze(2).to_broadcast([P, 4, P])
                    step(v.tensor_tensor(EK[:, t, 4 * c:4 * c + 4, :], g3, r3, ALU.subtract))
            for t in range(2):
                g3 = G[:, t, :].rearrange("p (i s) -> p i s", s=SUB)
                r3 = small[:, 32 + 8 * t:40 + 8 * t].unsqueeze(2).to_broadcast([P, 8, SUB])
                step(v.tensor_tensor(QQ[:, t, :].rearrange("p (i s) -> p i s", s=SUB), g3, r3, ALU.subtract))
                step(v.tensor_scalar(KD[:, t, :], G[:, t, 0:P], G[:, t, P - 1:P], None, ALU.subtract))
            settle()
            v.tensor_scalar(EK, EK, -16.0 * CLAMP, None, ALU.max).then_inc(ev("diffs_ready"), 1)
            wait("rstd_ready")
            for c in range(2):
                step(v.tensor_scalar(VN[:, c, :], VA[:, c, :], small[:, 48 + 2 * c:49 + 2 * c], small[:, 16 + c:17 + c],
                                     ALU.subtract, ALU.mult))
            settle()
            v.wait_ge(ev("lng_in"), 16)
            v.wait_ge(ev("lnb_in"), 16)
            link(v.tensor_tensor(VN, VN, LNG.unsqueeze(1).to_broadcast([P, 2, A_W]), ALU.mult))
            v.tensor_tensor(VN, VN, LNB.unsqueeze(1).to_broadcast([P, 2, A_W]), ALU.add).then_inc(ev("vn_ready"), 1)
            wait("exps_ready", 4)
            for t in range(2):
                for c in range(2):
                    k3 = KTT[:, t, c * P:(c + 1) * P].unsqueeze(1).to_broadcast([P, 4, P])
                    step(v.tensor_tensor(EK[:, t, 4 * c:4 * c + 4, :], EK[:, t, 4 * c:4 * c + 4, :], k3, ALU.mult))
            step(v.tensor_tensor(QQ, QQ, QT, ALU.mult))
            step(v.tensor_tensor(QI, QI, QT[:, :, P:2 * P], ALU.mult))
            step(v.tensor_tensor(KD, KD, KTT[:, :, 0:P], ALU.mult))
            settle()
            v.sem_inc(ev("decays_ready"), 1)
            v.wait_ge(ev("bs_in"), 16)
            wait("spatial_done")
            for b in range(2):
                for g in range(2):
                    src = half(2 + b, g).rearrange("p (c s) -> p c s", c=2)
                    step(v.tensor_tensor(sq[:, 4 + 2 * b + g, :].rearrange("p (c s) -> p c s", c=2), src,
                                         BS[:, 2 * b + g, :].unsqueeze(1).to_broadcast([P, 2, P]), ALU.add))
            settle()
            link(v.tensor_tensor(U, U, sq[:, 4:8, :], ALU.mult))
            wait("kd_turned")
            v.tensor_copy(KDT, psum[7][:, 0:2 * P].rearrange("p (a b) -> p a b", a=2)).then_inc(ev("kdt_ready"), 1)
            wait("gla_scores")
            for par in range(2):
                ins = v.tensor_tensor(ATS[:, par], psum[par][:, :].rearrange("p (a b) -> p a b", a=4),
                                      M("mask01").unsqueeze(1).to_broadcast([P, 4, P]), ALU.mult)
            ins.then_inc(ev("ats_ready"), 1)
            wait("state_done")
            v.tensor_copy(ST, psum[6][:, 0:2 * P].rearrange("p (a b) -> p a b", a=2)).then_inc(ev("state_ready"), 1)
            wait("rs_ready")
            link(v.tensor_tensor(tmp[:, 0:4, :], tmp[:, 0:4, :], sq[:, 4:8, :], ALU.mult))
            for h in range(4):
                step(v.scalar_tensor_tensor(OG[:, h, :], tmp[:, h, :], V("head_g", h), OG[:, h, :], ALU.mult, ALU.mult))
            settle()
            for k in range(KT):
                src = U[:, k, :] if k < 4 else OG[:, k - 4, :]
                v.tensor_copy(tmp[:, k, :], src).then_inc(ev("scaled"), 1)
            for k in range(KT):
                low_part(k)
            add_linears(lat)
            norm(lat, lambda k: V("g_even_ffn", k), lambda k: V("zero"))
            ffn(FF_STEPS)

            def add_down():
                v.wait_ge(pack_used, 2 * N_ADA + npos[0])
                for b in range(4):
                    step(v.tensor_tensor(lat[:, 2 * b:2 * b + 2, :], lat[:, 2 * b:2 * b + 2, :],
                                         psum[b][:, :].rearrange("p (a t) -> p a t", a=2), ALU.add))
                settle()
                v.sem_inc(ev("x_ready"), 1)

            add_down()
            norm(lat, lambda k: V("g_odd_mix", k), lambda k: V("zero"))
            others_read(N_ODD_IN)
            wait("f_ready")
            log_sigmoid(OF[0:C_HEADS], ONC[0:C_HEADS], OF[0:C_HEADS], T)
            link(v.memset(rs[:], 1.0))
            link(v.tensor_tensor_scan(OC[0:C_HEADS], rs[0:C_HEADS, :], OF[0:C_HEADS], 0.0, ALU.mult, ALU.add))
            link(v.tensor_scalar(ONC[0:C_HEADS], OC[0:C_HEADS], -1.0, None, ALU.mult))
            wait("rs_ready")
            v.scalar_tensor_tensor(OQ, OQ, V("odd_q_g"), sq[:], ALU.mult, ALU.mult).then_inc(ev("qk_scaled"), 1)
            wait("rs_ready")
            v.scalar_tensor_tensor(OK, OK, V("odd_k_g"), sq[:], ALU.mult, ALU.mult).then_inc(ev("qk_ready"), 1)

            def odd_pair(hd):
                t = hd["tile"]
                v.tensor_tensor(tmp[:, t, :], half(hd["out"][0], 0), OO[:, t, :], ALU.mult).then_inc(ev("pair_read"), 1)

            attention("odd", odd_pair)
            v.wait_ge(ev("pair_read"), seen.next(ev("pair_read"), 8))

            def hand_on():
                for k in range(KT):
                    v.sem_inc(ev("scaled"), 1)
                for k in range(KT):
                    low_part(k)

            hand_on()
            add_linears(lat)
            norm(lat, lambda k: V("g_odd_ffn", k), lambda k: V("zero"))
            others_read(1)
            v.wait_ge(ev("lin_read"), nlin[0])
            for t in range(2):
                link(v.max(small[:, 32 + 8 * t:40 + 8 * t], RL[:, t, 0:N_EXP]))
                link(v.max_index(GATE2[:, t, :].bitcast(U32), small[:, 32 + 8 * t:40 + 8 * t], RL[:, t, 0:N_EXP]))
                link(v.tensor_copy(small[:, 16 + 2 * t:18 + 2 * t], GATE2[:, t, 0:2].bitcast(U32)))
            top = small[:, 32:48].rearrange("p (t n) -> p t n", t=2)
            v.tensor_tensor(small[:, 24:26].unsqueeze(2), top[:, :, 1:2], top[:, :, 0:1], ALU.subtract).then_inc(ev("top_diff"), 1)
            wait("top_exp")
            link(v.tensor_scalar(small[:, 26:28], small[:, 24:26], 1.0, None, ALU.add))
            link(v.reciprocal(small[:, 26:28], small[:, 26:28]))
            link(v.tensor_tensor(small[:, 28:30], small[:, 26:28], small[:, 24:26], ALU.mult))
            for t in range(2):
                link(v.tensor_scalar(GATE[:, t, :], M("iota"), small[:, 16 + 2 * t:17 + 2 * t], small[:, 26 + t:27 + t],
                                     ALU.is_equal, ALU.mult))
                link(v.tensor_scalar(GATE2[:, t, :], M("iota"), small[:, 17 + 2 * t:18 + 2 * t], small[:, 28 + t:29 + t],
                                     ALU.is_equal, ALU.mult))
            v.tensor_tensor(GATE, GATE, GATE2, ALU.add).then_inc(ev("gates_ready"), 1)
            wait("gates_turned")
            v.tensor_copy(GT[0:N_EXP, :], psum[7][0:N_EXP, 0:T]).then_inc(ev("gt_ready"), 1)
            wait("gates_spread")
            for b in range(4):
                step(v.tensor_copy(GB[:, 2 * b:2 * b + 2, :], psum[b][:, :].rearrange("p (a t) -> p a t", a=2)))
            settle()
            v.sem_inc(ev("gb_ready"), 1)
            ffn(MOE_STEPS, gated=True)
            add_down()
            norm(lat, lambda k: V("g_final", k), out=lat)
            v.sem_inc(ev("x_ready"), 1)
            for l in range(2):
                for s, (stream, x) in enumerate((("context", con), ("latents", lat))):
                    only_kv = l == 1 and stream == "context"
                    k0 = T if stream == "context" else 0
                    col = 1 - s
                    norm(x, lambda k: gains[:, l, 0, k, col:col + 1], lambda k: mod[:, l, k, col:col + 1])
                    others_read(N_IN_KV if only_kv else N_IN)
                    wait("rs_ready")
                    step(v.scalar_tensor_tensor(tmp[:, 0, :], ZR[:, 0, :], V(f"g_mla_kv{l}"), sq[:, 0, :], ALU.mult, ALU.mult))
                    if not only_kv:
                        for k in range(2):
                            step(v.scalar_tensor_tensor(tmp[:, 1 + k, :], ZR[:, 6 + k, :], V(f"g_mla_q{l}", k), sq[:, 6, :],
                                                        ALU.mult, ALU.mult))
                    settle()
                    v.sem_inc(ev("latents_normed"), 1)
                    n = 1 if only_kv else 3
                    wait("latents_hi")
                    v.tensor_tensor(h_lo[:, 0:n, :], tmp[:, 0:n, :], h_hi[:, 0:n, :].bitcast(F32), ALU.subtract)\
                        .then_inc(ev("latent_split"), 1)
                    split_to(2 * N_ADA + npos[0] + AHEAD)
                    npos[0] += 1
                    step(v.scalar_tensor_tensor(KG[:, k0:k0 + T], ZR[:, 1, :], V(f"g_gqa_k{l}"), sq[:, 1, :], ALU.mult, ALU.mult))
                    if not only_kv:
                        step(v.scalar_tensor_tensor(QG, ZR[:, 2:6, :], V(f"g_gqa_q{l}"), sq[:, 2:6, :], ALU.mult, ALU.mult))
                        split_to(2 * N_ADA + npos[0] + AHEAD)
                        npos[0] += 1
                        wait("qm_ready", 2)
                    settle()
                    if stream == "latents":
                        v.sem_inc(ev("rope_in"), 1)
                        for n, (_, cos, sin, rows, z) in enumerate(ROPED):
                            w = z.shape[1]
                            wait("rotated")
                            src = psum[4 + n % 2][0:rows, 0:w * T].rearrange("p (a t) -> p a t", a=w)
                            t = sq[0:rows, 0:w, :]
                            v.tensor_tensor(t, src, M(sin)[0:rows].unsqueeze(1).to_broadcast([rows, w, T]), ALU.mult)\
                                .then_inc(ev("rope_out"), 1)
                            v.wait_ge(ev("rope_out"), seen.next(ev("rope_out")))
                            link(v.tensor_tensor(z, z, M(cos)[0:rows].unsqueeze(1).to_broadcast([rows, w, T]), ALU.mult))
                            link(v.tensor_tensor(z, z, t, ALU.add))
                    wait("km_ready", 3)
                    link(v.tensor_copy(KM[64:MLA_QK, :, k0:k0 + T], KPE[64:MLA_QK].unsqueeze(1).to_broadcast([32, 4, T])))
                    if only_kv:
                        v.sem_inc(ev("context_keys_ready"), 1)
                        continue
                    v.sem_inc(ev("qk_ready"), 1)

                    def pair(hd):
                        t, b = hd["tile"], hd["out"][0]
                        if hd["kind"] == "diff":
                            link(v.tensor_scalar(sq[:, 4 + t, :], half(b, 1), neg_lam[:, l:l + 1], None, ALU.mult))
                            v.tensor_tensor(tmp[:, t, :], half(b, 0), sq[:, 4 + t, :], ALU.add).then_inc(ev("pair_read"), 1)
                        else:
                            v.tensor_copy(tmp[:, t, :], half(b, 0)).then_inc(ev("pair_read"), 1)

                    attention(stream, pair)
                    v.wait_ge(ev("pair_read"), seen.next(ev("pair_read"), 8))
                    v.sem_inc(ev("diff_ready"), 1)
                    wait("rs_ready")
                    link(v.scalar_tensor_tensor(tmp[:, 2:4, :], tmp[:, 2:4, :], g_sub[:, l:l + 1], sq[:, 2:4, :], ALU.mult, ALU.mult))
                    hand_on()
                    others_read(KT)

                    def post(which):
                        norm(ZR, lambda k: gains[:, l, which, k, col:col + 1])
                        link(v.tensor_tensor(x[:], x[:], tmp[:], ALU.add))
                        v.sem_inc(ev("x_ready"), 1)
                    post(1)
                    norm(x, lambda k: gains[:, l, 2, k, col:col + 1], lambda k: mod[:, l, 24 + k, col:col + 1])
                    ffn(FF_STEPS)
                    post(3)
            v.sem_inc(ev("out_ready"), 1)


def _column_packs(w):
    k, n = w.shape
    pad = -n % P
    if pad:
        w = np.concatenate([w, np.zeros((k, pad), w.dtype)], axis=1)
    return w.reshape(KT, P, -1, P).transpose(2, 1, 0, 3).reshape(-1, P, PACK)


def _fill_ffn(out, w1, w3, w2):
    up = [[a.reshape(-1, KT, P, a.shape[-1] // P, P) for a in (w1, w3)]][0]
    n_exp, per = up[0].shape[0], up[0].shape[3]
    n = n_exp * per
    dest = out.reshape(-1, P, KT, P)
    for w in range(2):
        for e in range(n_exp):
            src = up[w][e].transpose(2, 1, 0, 3)
            for f in range(per):
                s = e * per + f
                at = w if s == 0 else 3 * s - 1 + w
                dest[at] = src[f]
    rows = w2.reshape(-1, P, D)
    for s in range(n):
        out[3 * s + 4 if s < n - 1 else 3 * n - 1] = rows[s]


def _weight_packs(a):
    packs = np.zeros((N_PACKS, P, PACK), np.float32)

    def put(name, values):
        packs[START[name]:START[name] + values.shape[0]] = values

    for l in range(2):
        put(f"ada{l}", _column_packs(a["w_ada_2"][l]))
    w = a["even_w_in"][0]
    u, v, q, k, g, vb, og = np.split(w, np.cumsum([A_W, A_W, B_QK, B_QK, RANK, B_V])[:6], axis=1)
    put("even_in", np.concatenate([_column_packs(x) for x in (g, q, k, vb, v, u, og)]))
    put("even_o", _column_packs(a["even_w_o"][0]))
    w = a["odd_w_in"][0]
    q, k, v, og, f = np.split(w, [D, 2 * D, 3 * D, 4 * D], axis=1)
    put("odd_in", np.concatenate([_column_packs(x) for x in (f, q, k, v, og)]))
    put("odd_o", _column_packs(a["odd_w_o"][0]))
    put("router", _column_packs(a["odd_router"][0]))

    def ffn(name, w1, w3, w2):
        _fill_ffn(packs[START[name]:START[name] + COUNT[name]], w1, w3, w2)

    ffn("even_ffn", a["even_ffn_w1"][0], a["even_ffn_w3"][0], a["even_ffn_w2"][0])
    ffn("moe", a["odd_exp_w1"][0], a["odd_exp_w3"][0], a["odd_exp_w2"][0])
    for l in range(2):
        w = a["w_in_2"][l]
        qa, kva, dq, dk, dv, gq, gk, gv = np.split(w, np.cumsum([256, 160, 256, 256, 256, 512, 128])[:7], axis=1)
        ckv, kpe = kva[:, :128], kva[:, 128:]
        kpe = np.concatenate([np.zeros((D, 64), w.dtype), kpe], axis=1)
        gq = gq.reshape(D, 2, 4, 64).transpose(0, 2, 1, 3).reshape(D, 512)
        put(f"in{l}", np.concatenate([_column_packs(x) for x in (ckv, kpe, dk, gk, dv, gv, qa, dq, gq)]))
        packs[START[f"kvb{l}"], :, 0:512] = a["w_mla_kvb_2"][l]
        qb = a["w_mla_qb_2"][l].reshape(2, P, 4, MLA_QK).transpose(1, 2, 0, 3)
        packs[START[f"qb{l}"]].reshape(P, 4, 2, P)[..., 0:MLA_QK] = qb
        put(f"out{l}", _column_packs(a["w_out_2"][l]))
        ffn(f"ffn{l}", a["w_ffn_gate_2"][l], a["w_ffn_up_2"][l], a["w_ffn_down_2"][l])
    return packs


def _vectors(a):
    vec = np.zeros((P, N_VEC), np.float32)

    def put(name, values):
        at, n = VEC[name]
        values = np.asarray(values).reshape(-1)
        rows = values.size // n
        vec[0:rows, at:at + n] = values.reshape(n, rows).T

    vec[:, VEC["one"][0]] = 1.0
    vec[:, VEC["eps"][0]] = EPS
    vec[:, VEC["eps64"][0]] = 64 * EPS
    put("g_even_mix", a["even_norm_mix"][0])
    put("g_even_ffn", a["even_norm_ffn"][0])
    put("g_odd_mix", a["odd_norm_mix"][0])
    put("g_odd_ffn", a["odd_norm_ffn"][0])
    put("g_final", a["final_norm"])
    put("head_g", a["even_head_g"][0])
    put("gate_bias", a["even_gate_bias"][0])
    put("odd_q_g", np.tile(a["odd_q_g"][0], 2))
    put("odd_k_g", np.tile(a["odd_k_g"][0], 2))
    put("forget_bias", a["odd_forget_bias"][0])
    put("cond", np.stack([a["c_2"][0], a["c_ctx_2"]]).reshape(2, KT, P).transpose(1, 0, 2))
    for l in range(2):
        for name, key in (("g_attn_pre", "g_attn_pre_2"), ("g_attn_post", "g_attn_post_2"), ("g_ffn_pre", "g_ffn_pre_2"),
                          ("g_ffn_post", "g_ffn_post_2"), ("b_ada", "b_ada_2"), ("g_mla_q", "g_mla_q_2"), ("g_mla_kv", "g_mla_kv_2")):
            put(f"{name}{l}", a[key][l])
        for name, key in (("g_gqa_q", "g_gqa_q_2"), ("g_gqa_k", "g_gqa_k_2"), ("g_sub", "g_diff_sub_2")):
            put(f"{name}{l}", np.tile(a[key][l], 2))
        put(f"lambdas{l}", np.stack([a[f"lambda_{n}_2"][l] for n in ("q1", "q2", "k1", "k2")]))
    return vec


def _matrices():
    mat = np.zeros((P, N_MAT), np.float32)

    def put(name, values):
        at, n = MAT[name]
        mat[0:values.shape[0], at:at + values.shape[1]] = values

    r = np.arange(P)
    put("ident", np.eye(P))
    put("ones", np.ones((P, P)))
    put("block64", (r[:, None] // 64 == r[None, :] // 64).astype(np.float32))
    put("mask01", (r[:, None] <= r[None, :]).astype(np.float32))
    put("mask_add", np.where(r[None, :] <= r[:, None], 0.0, -1e30))
    token = np.arange(T)
    for name, dim, first in (("mla", 32, 64), ("diff", 32, 0), ("gqa", 64, 0)):
        h = dim // 2
        rot = np.zeros((P, P))
        quarter = dim // 4
        inv = (np.float32(ROPE_THETA) ** (-np.arange(quarter, dtype=np.float32) / np.float32(quarter))).astype(np.float32)
        row, col = (token // GRID_W).astype(np.float32), (token % GRID_W).astype(np.float32)
        angle = np.concatenate([row[:, None] * inv, col[:, None] * inv], axis=1).T
        cos, sin = np.ones((P, T)), np.zeros((P, T))
        for b in range(first, MLA_QK if name == "mla" else P, dim):
            for i in range(h):
                rot[b + h + i, b + i] = -1.0
                rot[b + i, b + h + i] = 1.0
            cos[b:b + h] = cos[b + h:b + dim] = np.cos(angle)
            sin[b:b + h] = sin[b + h:b + dim] = np.sin(angle)
        put("rot_" + name, rot)
        put("cos_" + name, cos)
        put("sin_" + name, sin)
    pick = np.zeros((N_EXP, N_EXP * P))
    for e in range(N_EXP):
        pick[e, e * P:(e + 1) * P] = 1.0
    put("pick", pick)
    put("iota", np.tile(np.arange(N_EXP), (P, 1)))
    put("head_id", np.eye(C_HEADS))
    return mat


def _feature_major(x):
    return np.ascontiguousarray(x.T.reshape(KT, P, T).transpose(1, 0, 2)).reshape(P, KT * T)


def kernel(**inputs):
    import concourse.bacc as bacc
    from concourse.bass_utils import run_bass_kernel_spmd

    a = {k: np.asarray(v) for k, v in inputs.items()}
    arrays = {
        "w_packs": _weight_packs(a),
        "vecs": _vectors(a),
        "mats": _matrices(),
        "x_t": _feature_major(a["x"][0]),
        "ctx_t": _feature_major(a["ctx_2"][0]),
        "w_s_t": np.ascontiguousarray(a["even_w_s"][0].transpose(2, 0, 1)).reshape(P, 4 * P),
        "b_s_row": np.ascontiguousarray(a["even_b_s"][0]).reshape(4 * P),
        "ln_g_row": np.ascontiguousarray(a["even_ln_g"][0]),
        "ln_b_row": np.ascontiguousarray(a["even_ln_b"][0]),
        "gate_up": np.ascontiguousarray(a["even_gate_up"][0]),
    }
    nc = bacc.Bacc("TRN2", target_bir_lowering=False, num_devices=1)
    args = [nc.dram_tensor(n, x.shape, F32, kind="ExternalInput").ap() for n, x in arrays.items()]
    out = nc.dram_tensor("out_t", (P, KT * T), F32, kind="ExternalOutput").ap()
    build(nc, *args, out)
    r = run_bass_kernel_spmd(nc, [arrays], core_ids=[0])
    y = r.results[0]["out_t"].reshape(P, KT, T).transpose(1, 0, 2).reshape(D, T).T
    return np.ascontiguousarray(y)[None]
```

```python
from contextlib import ExitStack

import numpy as np

import concourse.bass as bass
from concourse import mybir

ALU = mybir.AluOpType
ACT = mybir.ActivationFunctionType
AX = mybir.AxisListType
F32 = mybir.dt.float32
F32R = mybir.dt.float32r
U32 = mybir.dt.uint32
I32 = mybir.dt.int32

P = 128
D = 1024
KT = D // P
T = 256
CHUNK = 128
EPS = 1e-6
PACK = KT * P

A_W, B_QK, B_V, RANK = 512, 256, 512, 16
CLAMP = 70.0
SUB = 32
C_HEADS = 16
FF = 2816
FF_STEPS = FF // P
N_EXP, FF_EXP = 8, 3584
WIDE = 512
GROUPS = FF_EXP // WIDE
EXP_PACKS = 12 * GROUPS

GRID_W = 64
ROPE_THETA = 10000.0
MLA_QK = 96
MLA_SCALE = 96.0 ** -0.5
DIFF_SCALE = 32.0 ** -0.5
LAMBDA_INIT = [0.8 - 0.6 * float(np.exp(-0.3 * l)) for l in range(2)]

RING = 6
AHEAD = 5

N_EVEN_IN, N_ODD_IN, N_IN, N_IN_KV, N_ADA = 21, 33, 16, 8, 48
SECTIONS = [("ada0", N_ADA), ("ada1", N_ADA), ("even_in", N_EVEN_IN), ("even_o", 8), ("even_ffn", 3 * FF_STEPS),
            ("odd_in", N_ODD_IN), ("odd_o", 8), ("router", 1), ("moe", N_EXP * EXP_PACKS)]
for _l in range(2):
    SECTIONS += [(f"in{_l}", N_IN), (f"kvb{_l}", 1), (f"qb{_l}", 1), (f"out{_l}", 8), (f"ffn{_l}", 3 * FF_STEPS)]
START, _n = {}, 0
for _name, _count in SECTIONS:
    START[_name] = _n
    _n += _count
N_PACKS = _n
ADA_GROUPS = 2 * N_ADA // 4
COUNT = dict(SECTIONS)


def stream_order():
    def all_of(*names):
        return [(START[n], COUNT[n]) for n in names]
    order = all_of("ada0", "ada1", "even_in", "even_o", "even_ffn", "odd_in", "odd_o", "router", "moe")
    for _ in ("context", "latents"):
        order += all_of("in0", "kvb0", "qb0", "out0", "ffn0")
    order += [(START["in1"], N_IN_KV), (START["kvb1"], 1)]
    order += all_of("in1", "kvb1", "qb1", "out1", "ffn1")
    merged = []
    for s, n in order:
        if merged and sum(merged[-1]) == s:
            merged[-1] = (merged[-1][0], merged[-1][1] + n)
        else:
            merged.append((s, n))
    return merged


TOTAL = sum(n for _, n in stream_order())

VEC = {}
_n = 0
for _name, _count in ([("zero", 1), ("one", 1), ("eps", 1), ("eps64", 1),
                       ("g_even_mix", 8), ("g_even_ffn", 8), ("g_odd_mix", 8), ("g_odd_ffn", 8), ("g_final", 8),
                       ("head_g", 4), ("gate_bias", 2), ("odd_q_g", 1), ("odd_k_g", 1), ("forget_bias", 1),
                       ("cond", 16)]
                      + [(f"{n}{l}", c) for l in range(2) for n, c in
                         (("g_attn_pre", 8), ("g_attn_post", 8), ("g_ffn_pre", 8), ("g_ffn_post", 8), ("b_ada", 48),
                          ("g_mla_q", 2), ("g_mla_kv", 1), ("g_gqa_q", 1), ("g_gqa_k", 1), ("g_sub", 1),
                          ("lambdas", 4))]):
    VEC[_name] = (_n, _count)
    _n += _count
N_VEC = _n

MAT = {}
_n = 0
for _name, _count in [("ident", P), ("ones", P), ("block64", P), ("mask01", P), ("mask_add", P),
                      ("rot_mla", P), ("rot_diff", P), ("rot_gqa", P),
                      ("cos_mla", T), ("sin_mla", T), ("cos_diff", T), ("sin_diff", T), ("cos_gqa", T),
                      ("sin_gqa", T), ("pick", N_EXP * P), ("iota", P), ("head_id", C_HEADS)]:
    MAT[_name] = (_n, _count)
    _n += _count
N_MAT = _n


class Seen:

    def __init__(self):
        self.count = {}

    def next(self, sem, n=1):
        self.count[sem.name] = self.count.get(sem.name, 0) + n
        return self.count[sem.name]

    def now(self, sem):
        return self.count.get(sem.name, 0)


def build(nc, w_packs, vecs, mats, x_t, ctx_t, w_s_t, b_s_row, ln_g_row, ln_b_row, gate_up, out_t):
    with ExitStack() as stack:
        def sb(name, shape, dt=F32):
            return stack.enter_context(nc.sbuf_tensor(name, shape, dt))

        made = {}

        def ev(name):
            if name not in made:
                made[name] = stack.enter_context(nc.semaphore(name))
            return made[name]

        raw = sb("raw", [P, RING, PACK])
        w_hi = sb("w_hi", [P, RING, PACK], F32R)
        w_lo = sb("w_lo", [P, RING, PACK], F32R)
        lat = sb("lat", [P, KT, T])
        con = sb("con", [P, KT, T])
        h_hi = sb("h_hi", [P, KT, T], F32R)
        h_lo = sb("h_lo", [P, KT, T], F32R)
        tmp = sb("tmp", [P, KT, T])
        sq = sb("sq", [P, KT, T])
        vec = sb("vec", [P, N_VEC])
        mat = sb("mat", [P, N_MAT])
        rs = sb("rs", [P, T])
        prob = sb("prob", [P, 2, 512])
        prob_t = sb("prob_t", [P, 2, 4 * T])
        logit_sg = sb("logit_sg_prod", [P, 6 * T])
        logit, sg, prod = (logit_sg[:, n * 2 * T:(n + 1) * 2 * T].rearrange("p (a t) -> p a t", t=T) for n in range(3))
        f_hi = sb("f_hi", [P, 2, T], F32R)
        f_lo = sb("f_lo", [P, 2, T], F32R)
        mod = sb("mod", [P, 2, N_ADA, 2])
        gains = sb("gains", [P, 2, 4, KT, 2])
        small = sb("small", [P, 64])
        cond_s = sb("cond_s", [P, KT, 2])
        ada_rows = logit_sg[0:2, :].rearrange("p (g c) -> p g c", c=512)
        neg_lam = sb("neg_lam", [P, 2])
        g_sub = sb("g_sub", [P, 2])
        choice_t = sb("choice_t", [P, T], F32R)
        fullest = sb("fullest", [P, 2], I32)
        arena = sb("arena", [P, 11264])

        def V(name, j=None):
            a, n = VEC[name]
            return vec[:, a:a + n] if j is None else vec[:, a + j:a + j + 1]

        def M(name):
            a, n = MAT[name]
            return mat[:, a:a + n]

        at = [0]

        def part(*shape, start=None):
            if start is not None:
                at[0] = start
            n = int(np.prod(shape))
            a = arena[:, at[0]:at[0] + n]
            at[0] += n
            assert at[0] <= 11264
            if len(shape) == 2:
                a = a.rearrange("p (a b) -> p a b", b=shape[1])
            if len(shape) == 3:
                a = a.rearrange("p (a b c) -> p a b c", b=shape[1], c=shape[2])
            return a

        cond_hi, cond_lo = (h[:].rearrange("p k t -> p (k t)")[:, 0:KT * P].rearrange("p (k m) -> p k m", m=P)
                            for h in (h_hi, h_lo))
        U = part(4, T, start=0)
        VA = part(2, A_W)
        VN = part(2, A_W)
        QT = part(2, T)
        KTT = part(2, T)
        VB = part(2, B_V)
        OG = part(4, T)
        G = part(2, T)
        GX = part(2, T)
        EK = part(2, 8, P)
        QQ = part(2, T)
        QI = part(2, P)
        KD = part(2, P)
        WS = part(4, P)
        BS = part(4, P)
        LNG, LNB = prob_t[:, 0, 0:A_W], prob_t[:, 0, A_W:2 * A_W]
        ATS = prob_t[:, 1, :].rearrange("p (a b c) -> p a b c", a=2, b=4)
        KDT = prob[:, 0, 0:2 * P].rearrange("p (a b) -> p a b", a=2)
        ST = prob[:, 0, 2 * P:4 * P].rearrange("p (a b) -> p a b", a=2)
        GUP = prob[0:RANK, 1, 0:B_QK]
        GLR = logit[:, 0, :]
        OQ = part(8, T, start=0)
        OK = part(8, T)
        OV = part(2, D)
        OO = part(8, T)
        OC = part(T)
        ONC = part(T)
        OF = part(T)
        GB = part(8, T, start=0)
        RL = part(2, P, start=2048)
        GATE = part(2, N_EXP + 1)
        SLOT = part(2, N_EXP + 1)
        SEL = part(2, N_EXP)
        GATE2 = part(2, N_EXP)
        GT = part(T)
        HT = part(2, D)
        CHOICE = part(2, P)
        CUR_SLOT, CUR_GATE = small[:, 48:50], small[:, 50:52]
        SLOT_GATE = small[:, 52:53]
        KM = part(4, 2 * T, start=0)
        KD2 = part(2, 2 * T)
        KG = part(2 * T)
        VM = part(4, 256)
        VD = part(4, 256)
        VG = part(4, 128)
        QM = part(4, T)
        QD = part(2, T)
        QG = part(4, T)
        ZR = part(8, T)
        KPE = part(T)

        psum = [stack.enter_context(nc.psum_tensor(f"bank{b}", [P, 512], F32)) for b in range(8)]

        def half(b, j):
            return psum[b][:, j * T:(j + 1) * T]

        SG_WIDE = sg.rearrange("p a t -> p (a t)")
        PROD_WIDE = prod.rearrange("p a t -> p (a t)")
        F_HI, F_LO = (f[:].rearrange("p a t -> p (a t)").rearrange("p (j s) -> p j s", s=P) for f in (f_hi, f_lo))
        X_HI, X_LO = h_hi[:, :, 0:P], h_lo[:, :, 0:P]
        Y_HI, Y_LO = h_hi[:, :, P:2 * P], h_lo[:, :, P:2 * P]
        SCATTER_BANKS = (5, 6, 7, 4)

        def group_at(g):
            return 0 if g == 0 else 12 * g - 4

        raw_in = [ev(f"raw_in{j}") for j in range(RING)]
        hi_done, lo_done, pack_used = ev("hi_done"), ev("lo_done"), ev("pack_used")

        block = stack.enter_context(nc.Block())

        def odd_heads():
            return [dict(h=h, row=64 * (h % 2), k=64, q=lambda c, h=h: OQ[64 * (h % 2):64 * (h % 2) + 64, h // 2, c * P:(c + 1) * P],
                         keys=lambda n, h=h: OK[64 * (h % 2):64 * (h % 2) + 64, h // 2, 0:n],
                         v=lambda s, h=h: OV[:, s, h * 64:(h + 1) * 64],
                         out=(6 + (h // 2) % 2, 64 * (h % 2), 0), last=h % 2 == 1, tile=h // 2) for h in range(C_HEADS)]

        def block2_heads(k0, n_tiles):
            t0 = k0 // P
            kk = slice(k0, k0 + n_tiles * P)
            heads = []
            for h in range(4):
                heads.append(dict(q=lambda c, h=h: QM[0:MLA_QK, h, c * P:(c + 1) * P], keys=lambda n, h=h: KM[0:MLA_QK, h, kk],
                                  v=lambda s, h=h: VM[:, t0 + s, h * 64:(h + 1) * 64],
                                  out=(6 + (h // 2) % 2, 64 * (h % 2), 0), last=h % 2 == 1, tile=h // 2, kind="mla"))
            for pair in range(2):
                for j in (2 * pair, 2 * pair + 1):
                    for w in range(2):
                        h = 2 * j + w
                        r = 32 * (h % 4)
                        heads.append(dict(q=lambda c, h=h, r=r: QD[r:r + 32, h // 4, c * P:(c + 1) * P],
                                          keys=lambda n, h=h, r=r: KD2[r:r + 32, h // 4, kk],
                                          v=lambda s, j=j: VD[:, t0 + s, j * 64:(j + 1) * 64],
                                          out=(6 + pair, 64 * (j % 2), w), last=j % 2 == 1 and w == 1, tile=2 + pair,
                                          kind="diff"))
            for h in range(8):
                r = 64 * (h // 4)
                heads.append(dict(q=lambda c, h=h, r=r: QG[r:r + 64, h % 4, c * P:(c + 1) * P],
                                  keys=lambda n, r=r: KG[r:r + 64, kk],
                                  v=lambda s, h=h: VG[:, t0 + s, (h // 4) * 64:(h // 4) * 64 + 64],
                                  out=(6 + (h // 2) % 2, 64 * (h % 2), 0), last=h % 2 == 1, tile=4 + h // 2, kind="gqa"))
            return heads

        def heads_and_keys(kind):
            if kind == "odd":
                return odd_heads(), lambda c: c + 1
            if kind == "context":
                return block2_heads(T, 2), lambda c: 2
            return block2_heads(0, 4), lambda c: 4

        ROPED = [("rot_mla", "cos_mla", "sin_mla", MLA_QK, QM[0:MLA_QK, 0:2, :]),
                 ("rot_mla", "cos_mla", "sin_mla", MLA_QK, QM[0:MLA_QK, 2:4, :]),
                 ("rot_mla", "cos_mla", "sin_mla", MLA_QK, KPE[0:MLA_QK].unsqueeze(1)),
                 ("rot_diff", "cos_diff", "sin_diff", P, QD),
                 ("rot_diff", "cos_diff", "sin_diff", P, KD2[:, :, 0:T]),
                 ("rot_gqa", "cos_gqa", "sin_gqa", P, QG[:, 0:2, :]),
                 ("rot_gqa", "cos_gqa", "sin_gqa", P, QG[:, 2:4, :]),
                 ("rot_gqa", "cos_gqa", "sin_gqa", P, KG[:, 0:T].unsqueeze(1))]

        @block.sync
        def _(sp):
            sp.dma_start(vec[:], vecs).then_inc(ev("vec_in"), 16)
            n = 0
            split = 0

            def load(first, c, it, slot, wait):
                if wait:
                    sp.wait_ge(lo_done, c)
                sp.dma_start(raw[:, slot, :], w_packs[it]).then_inc(raw_in[slot], 16)

            for first, count in stream_order():
                done = 0
                while done < count:
                    loops = (count - done) // RING
                    if n >= RING and loops > 1:
                        with sp.Fori(0, loops) as i:
                            for j in range(RING):
                                load(first, i * RING + (n + j - RING + 1), i * RING + (first + done + j), (n + j) % RING, True)
                        n += loops * RING
                        done += loops * RING
                    else:
                        load(first, n - RING + 1, first + done, n % RING, n >= RING)
                        n += 1
                        done += 1
                    if n == RING:
                        sp.dma_start(mat[:], mats).then_inc(ev("mat_in"), 16)
                        sp.dma_start(lat[:].rearrange("p k t -> p (k t)"), x_t).then_inc(ev("lat_in"), 16)
                        sp.dma_start(con[:].rearrange("p k t -> p (k t)"), ctx_t).then_inc(ev("con_in"), 16)
                        sp.dma_start(WS.rearrange("p a b -> p (a b)"), w_s_t).then_inc(ev("ws_in"), 16)
                        sp.dma_start(BS.rearrange("p a b -> p (a b)"), b_s_row.partition_broadcast(P)).then_inc(ev("bs_in"), 16)
                        sp.dma_start(LNG, ln_g_row.partition_broadcast(P)).then_inc(ev("lng_in"), 16)
                        sp.dma_start(LNB, ln_b_row.partition_broadcast(P)).then_inc(ev("lnb_in"), 16)
                        sp.dma_start(GUP, gate_up).then_inc(ev("gup_in"), 16)
            assert n == TOTAL
            sp.wait_ge(ev("out_ready"), 1)
            sp.dma_start(out_t, lat[:].rearrange("p k t -> p (k t)")).then_inc(ev("stored"), 16)
            sp.wait_ge(ev("stored"), 16)

        @block.tensor
        def _(pe):
            seen = Seen()
            pos = [0]
            lin = [0]

            def mm3(out, a_hi, a_lo, first, last, w_slot, cols, swap=False, check=False):
                hi, lo = w_hi[:, w_slot, cols], w_lo[:, w_slot, cols]
                for n, (x, y) in enumerate(((hi, a_hi), (hi, a_lo), (lo, a_hi))):
                    if swap:
                        x, y = y, x
                    ins = pe.matmul(out, x, y, start=first and n == 0, stop=last and n == 2, skip_group_check=check)
                return ins

            def linear(kt=KT, tokens=False, rhs=(h_hi, h_lo)):
                s = pos[0] % RING
                pe.wait_ge(lo_done, pos[0] + 1)
                if lin[0] >= 2:
                    pe.wait_ge(ev("lin_read"), lin[0] - 1)
                b = 4 + lin[0] % 2
                if tokens:
                    for tk in range(2):
                        for k in range(kt):
                            ins = mm3(psum[b][:, tk * P:(tk + 1) * P], rhs[0][:, k, tk * P:(tk + 1) * P],
                                      rhs[1][:, k, tk * P:(tk + 1) * P], k == 0, k == kt - 1, s,
                                      slice(k * P, (k + 1) * P), swap=True)
                else:
                    for k in range(kt):
                        ins = mm3(half(b, 0), rhs[0][:, k, :], rhs[1][:, k, :], k == 0, k == kt - 1, s,
                                  slice(k * P, (k + 1) * P))
                ins.then_inc(pack_used, 1)
                pos[0] += 1
                lin[0] += 1

            def lin_all_read():
                pe.wait_ge(ev("lin_read"), lin[0])

            def norm_sum(tiles=KT):
                for k in range(tiles):
                    if k % 2 == 0:
                        pe.wait_ge(ev("squares"), seen.next(ev("squares")))
                    ins = pe.matmul(half(6, 0), M("ones"), sq[:, k, :], start=k == 0, stop=k == tiles - 1)
                ins.then_inc(ev("sum_ready"), 1)

            def ffn(steps):
                base = pos[0]
                up_base = seen.now(ev("act_ready"))

                def up(s, par, p):
                    if not isinstance(s, int) or up_base + s >= 2:
                        pe.wait_ge(ev("act_ready"), up_base + s - 1)
                    for w in range(2):
                        pe.wait_ge(lo_done, p + w + 1)
                        slot = (base + (3 * par[1] - 1 if par[1] else 0) + w) % RING
                        for k in range(KT):
                            ins = mm3(half(4 + par[0], w), h_hi[:, k, :], h_lo[:, k, :], k == 0, k == KT - 1,
                                      slot, slice(k * P, (k + 1) * P))
                        ins.then_inc(pack_used, 1)

                def down(s, par, p, first=False, last=False):
                    pe.wait_ge(lo_done, p + 1)
                    pe.wait_ge(ev("act_ready"), up_base + s + 1)
                    slot = (base + par[1]) % RING
                    for m in range(KT):
                        ins = mm3(half(m // 2, m % 2), f_hi[:, par[0], :], f_lo[:, par[0], :],
                                  first and m % 2 == 0, last, slot, slice(m * P, (m + 1) * P), check=True)
                    ins.then_inc(pack_used, 1)

                up(0, (0, 0), base)
                up(1, (1, 1), base + 2)
                down(0, (0, 4), base + 4, first=True)
                assert (steps - 2) % 2 == 0
                with pe.Fori(0, (steps - 2) // 2) as i:
                    for j in range(2):
                        up(i * 2 + (2 + j), (j, 2 + j), i * 6 + (base + 5 + 3 * j))
                        down(i * 2 + (1 + j), ((1 + j) % 2, 7 + 3 * j), i * 6 + (base + 7 + 3 * j))
                down(steps - 1, ((steps - 1) % 2, 3 * steps - 1), base + 3 * steps - 1, last=True)
                pos[0] = base + 3 * steps
                seen.next(ev("act_ready"), steps)

            def attention(kind):
                heads, n_keys = heads_and_keys(kind)
                units = [(i, c) for i in range(len(heads)) for c in range(2)]
                lin_all_read()
                pe.wait_ge(ev("qk_ready"), seen.next(ev("qk_ready")))

                def scores(u):
                    i, c = units[u]
                    hd, n = heads[i], n_keys(c) * P
                    if u >= 2:
                        pe.wait_ge(ev("exp_done"), seen.now(ev("exp_done")) + u - 1)
                    out = psum[u % 2][:, 0:n]
                    if kind == "odd":
                        hh = hd["h"]
                        pick = M("head_id")[0:C_HEADS, hh:hh + 1]
                        pe.matmul(out, hd["q"](c), hd["keys"](n), start=True, stop=False)
                        pe.matmul(out, OC[0:C_HEADS, c * P:(c + 1) * P], pick.to_broadcast([C_HEADS, n]), start=False, stop=False)
                        pe.matmul(out, pick.to_broadcast([C_HEADS, P]), ONC[0:C_HEADS, 0:n], start=False, stop=True)\
                          .then_inc(ev("scores_done"), 1)
                    else:
                        pe.matmul(out, hd["q"](c), hd["keys"](n), start=True, stop=True).then_inc(ev("scores_done"), 1)

                def turn(u):
                    i, c = units[u]
                    pe.wait_ge(ev("prob_ready"), seen.now(ev("prob_ready")) + u + 1)
                    if u >= 2:
                        pe.wait_ge(ev("prob_t_ready"), seen.now(ev("prob_t_ready")) + u - 1)
                    for s in range(n_keys(c)):
                        ins = pe.transpose(psum[2 + u % 2][:, s * P:(s + 1) * P], prob[:, u % 2, s * P:(s + 1) * P], M("ident"))
                    ins.then_inc(ev("turned"), 1)

                def values(i):
                    hd = heads[i]
                    bank, row, w = hd["out"]
                    pe.wait_ge(ev("prob_t_ready"), seen.now(ev("prob_t_ready")) + 2 * i + 2)
                    pair = sum(h["last"] for h in heads[:i])
                    if pair >= 2:
                        pe.wait_ge(ev("pair_read"), seen.now(ev("pair_read")) + pair - 1)
                    pt = prob_t[:, i % 2, :].rearrange("p (s t) -> p s t", t=T)
                    ns = n_keys(1)
                    for s in range(ns):
                        c0 = 0 if n_keys(0) > s else 1
                        ins = pe.matmul(psum[bank][row:row + 64, w * T + c0 * P:(w + 1) * T], hd["v"](s), pt[:, s, c0 * P:T],
                                        start=s == 0, stop=s == ns - 1)
                    ins.then_inc(ev("value_done"), 1)

                scores(0)
                for u in range(len(units)):
                    if u + 1 < len(units):
                        scores(u + 1)
                    turn(u)
                    if u % 2 == 0 and u >= 2:
                        values(u // 2 - 1)
                values(len(heads) - 1)
                seen.next(ev("exp_done"), len(units))
                seen.next(ev("prob_ready"), len(units))
                seen.next(ev("prob_t_ready"), len(units))
                seen.next(ev("pair_read"), sum(h["last"] for h in heads))

            def sparse_experts(base):
                def up(bank, p, at):
                    for q in range(4):
                        pe.wait_ge(lo_done, p + (q + 1))
                        for t in range(2):
                            k = 2 * q + t
                            ins = mm3(psum[bank][:, :], X_HI[:, k, :], X_LO[:, k, :], k == 0, k == KT - 1, (at + q) % RING,
                                      slice(t * WIDE, (t + 1) * WIDE), swap=True)
                        ins.then_inc(pack_used, 1)

                def ups(g, p, at):
                    pe.wait_ge(ev("m_silu"), g)
                    up(0, p, at)

                def turn(g):
                    pe.wait_ge(ev("m_prod"), g + 1)
                    for j in range(4):
                        ins = pe.transpose(psum[4][:, j * P:(j + 1) * P], PROD_WIDE[:, j * P:(j + 1) * P], M("ident"))
                    ins.then_inc(ev("m_turned"), 1)

                def down(g, p, at, first, last):
                    pe.wait_ge(ev("m_split"), g + 1)
                    for q in range(4):
                        pe.wait_ge(lo_done, p + (q + 1))
                        for c in range(2):
                            ins = mm3(psum[2 + c][:, :], F_HI[:, q, :], F_LO[:, q, :], first and q == 0, last and q == 3,
                                      (at + q) % RING, slice(c * 512, (c + 1) * 512), swap=True)
                        ins.then_inc(pack_used, 1)

                def gather(n):
                    pe.wait_ge(ev("m_choice"), n + 1)
                    for k in range(KT):
                        for t in range(2):
                            ins = pe.matmul(psum[5 + k // 4][:, (k % 4) * P:(k % 4 + 1) * P], HT[:, t, k * P:(k + 1) * P],
                                            CHOICE[:, t, :], start=t == 0, stop=t == 1)
                    ins.then_inc(ev("m_gathered"), 1)

                def scatter(n):
                    pe.wait_ge(ev("m_y_split"), n + 1)
                    pe.wait_ge(ev("m_choice_t"), n + 1)
                    for m in range(KT):
                        out = half(SCATTER_BANKS[m // 2], m % 2)
                        pe.matmul(out, Y_HI[:, m, :], choice_t[:], start=True, stop=False)
                        ins = pe.matmul(out, Y_LO[:, m, :], choice_t[:], start=False, stop=True)
                    ins.then_inc(ev("m_scattered"), 1)

                for t in range(2):
                    for k in range(KT):
                        ins = pe.transpose(psum[2 * t + k // 4][:, (k % 4) * P:(k % 4 + 1) * P], tmp[:, k, t * P:(t + 1) * P],
                                           M("ident"))
                ins.then_inc(ev("m_h_turned"), 1)
                pe.wait_ge(ev("m_h_t"), 1)
                gather(0)
                with pe.Fori(0, N_EXP) as e:
                    p = e * EXP_PACKS + base
                    g = e * GROUPS
                    pe.wait_ge(ev("m_x_split"), e + 1)
                    ups(g, p, base)
                    up(1, p + 4, base + 4)
                    scatter(e)
                    at = base + group_at(1)
                    ups(g + 1, p + group_at(1), at)
                    pe.wait_ge(ev("m_added"), e + 1)
                    turn(g)
                    up(1, p + (group_at(1) + 4), at + 4)
                    down(g, p + (group_at(1) + 8), at + 8, True, False)
                    for t in range(2):
                        pe.transpose(psum[7][:, t * P:(t + 1) * P], CHOICE[:, t, :], M("ident"))
                    for t in range(2):
                        ins = pe.matmul(psum[7][:, T:T + 1], CHOICE[:, t, :], CUR_GATE[:, t:t + 1], start=t == 0, stop=t == 1)
                    ins.then_inc(ev("m_choice_turned"), 1)
                    with pe.Fori(0, GROUPS - 2) as i:
                        at = base + group_at(2)
                        p2 = e * EXP_PACKS + i * 12 + at
                        g2 = e * GROUPS + i
                        ups(g2 + 2, p2, at)
                        turn(g2 + 1)
                        up(1, p2 + 4, at + 4)
                        down(g2 + 1, p2 + 8, at + 8, False, False)
                    gather(e + 1)
                    turn(g + (GROUPS - 1))
                    down(g + (GROUPS - 1), p + (EXP_PACKS - 4), base + EXP_PACKS - 4, False, True)
                scatter(N_EXP)

            def dense_experts(base):
                for t in range(2):
                    ins = pe.transpose(psum[7][0:N_EXP, t * P:(t + 1) * P], GATE[:, t, 0:N_EXP], M("ident"))
                ins.then_inc(ev("gates_turned"), 1)
                pe.wait_ge(ev("gt_ready"), 1)
                for e in range(N_EXP):
                    ins = pe.matmul(half(e // 2, e % 2), M("pick")[0:N_EXP, e * P:(e + 1) * P], GT[0:N_EXP, :], start=True, stop=True)
                ins.then_inc(ev("gates_spread"), 1)

                def up(bank, p, at):
                    for q in range(4):
                        pe.wait_ge(lo_done, p + (q + 1))
                        for t in range(2):
                            k = 2 * q + t
                            for j in range(4):
                                ins = mm3(half(bank + j // 2, j % 2), h_hi[:, k, :], h_lo[:, k, :], k == 0 and j % 2 == 0,
                                          k == KT - 1, (at + q) % RING, slice(t * WIDE + j * P, t * WIDE + (j + 1) * P), check=True)
                        ins.then_inc(pack_used, 1)

                def ups(g, p, at):
                    pe.wait_ge(ev("d_prod"), g)
                    up(4, p, at)
                    up(6, p + 4, at + 4)

                def down(g, p, at, first=False, last=False):
                    for q in range(4):
                        if q % 2 == 0:
                            pe.wait_ge(ev("d_split"), g * 2 + (q // 2 + 1))
                        pe.wait_ge(lo_done, p + (q + 1))
                        for m in range(KT):
                            ins = mm3(half(m // 2, m % 2), f_hi[:, q % 2, :], f_lo[:, q % 2, :], first and q == 0 and m % 2 == 0,
                                      last and q == 3, (at + q) % RING, slice(m * P, (m + 1) * P), check=True)
                        ins.then_inc(pack_used, 1)

                with pe.Fori(0, N_EXP) as e:
                    p = e * EXP_PACKS + base
                    g = e * GROUPS
                    ups(g, p, base)
                    ups(g + 1, p + group_at(1), base + group_at(1))
                    pe.wait_ge(ev("d_added"), e + 1)
                    down(g, p + (group_at(1) + 8), base + group_at(1) + 8, first=True)
                    with pe.Fori(0, GROUPS - 2) as i:
                        at = base + group_at(2)
                        p2 = e * EXP_PACKS + i * 12 + at
                        g2 = e * GROUPS + i
                        ups(g2 + 2, p2, at)
                        down(g2 + 1, p2 + 8, at + 8)
                    down(g + (GROUPS - 1), p + (EXP_PACKS - 4), base + EXP_PACKS - 4, last=True)

            pe.wait_ge(ev("cond_ready"), seen.next(ev("cond_ready")))

            def ada(g, j, p):
                if not isinstance(g, int) or g >= 3:
                    pe.wait_ge(ev("ada_row"), g - 2)
                for q in range(4):
                    pe.wait_ge(lo_done, p + q + 1)
                    for t in range(2):
                        k = 2 * q + t
                        ins = mm3(psum[4 + j % 3][:, :], cond_hi[:, k, :], cond_lo[:, k, :], k == 0, k == KT - 1, (4 * j + q) % RING,
                                  slice(t * 512, (t + 1) * 512), swap=True)
                    ins.then_inc(pack_used, 1)

            def ada_turn(g, j):
                pe.wait_ge(ev("ada_row"), g + 1)
                for q in range(4):
                    col = bass.ds(g * 8 + 2 * q, 2)
                    ins = pe.matmul(psum[7][:, col], ada_rows[0:2, j % 3, q * P:(q + 1) * P], M("ident")[0:2, 0:2],
                                    start=True, stop=True)
                ins.then_inc(ev("ada_turned"), 1)

            ada(0, 0, 0)
            pe.wait_ge(ev("mat_in"), 16)
            for g in (1, 2):
                ada(g, g, 4 * g)
                ada_turn(g - 1, g - 1)
            with pe.Fori(1, ADA_GROUPS // 3) as i:
                for j in range(3):
                    ada(i * 3 + j, j, i * 12 + 4 * j)
                    ada_turn(i * 3 + (j - 1), (j - 1) % 3)
            ada_turn(ADA_GROUPS - 1, 2)
            pos[0] = 2 * N_ADA
            pe.wait_ge(ev("lam_prod"), seen.next(ev("lam_prod")))
            pe.matmul(psum[6][:, 0:4], M("ones")[0:32, :], small[0:32, 0:4], start=True, stop=True).then_inc(ev("lam_sum"), 1)

            norm_sum()
            pe.wait_ge(ev("h_ready"), seen.next(ev("h_ready"), KT))
            for n in range(N_EVEN_IN):
                linear(tokens=5 <= n < 13)
            lin_all_read()
            pe.wait_ge(ev("gup_in"), 16)
            for t in range(2):
                ins = pe.matmul(half(6, t), GUP[:, t * P:(t + 1) * P], GLR[0:RANK, :], start=True, stop=True)
            ins.then_inc(ev("gate_done"), 1)
            pe.wait_ge(ev("vn_ready"), 1)
            pe.wait_ge(ev("ws_ready"), 1)
            for g in range(4):
                for c in range(2):
                    ins = pe.matmul(psum[2 + g // 2][:, (g % 2) * T + c * P:(g % 2) * T + (c + 1) * P],
                                    VN[:, c, g * P:(g + 1) * P], WS[:, g, :], start=True, stop=True)
            ins.then_inc(ev("spatial_done"), 1)
            pe.wait_ge(ev("decays_ready"), 1)
            for t in range(2):
                ins = pe.transpose(psum[7][:, t * P:(t + 1) * P], KD[:, t, :], M("ident"))
            ins.then_inc(ev("kd_turned"), 1)
            for par in range(2):
                r = 64 * par
                for t in range(2):
                    for c in range(2):
                        for i in range(4):
                            ins = pe.matmul(psum[par][:, (t * 2 + c) * P + i * SUB:(t * 2 + c) * P + (i + 1) * SUB],
                                            EK[r:r + 64, t, c * 4 + i, :], QQ[r:r + 64, t, c * P + i * SUB:c * P + (i + 1) * SUB],
                                            start=True, stop=True)
            ins.then_inc(ev("gla_scores"), 1)
            pe.wait_ge(ev("kdt_ready"), 1)
            for h in range(4):
                r = 64 * (h % 2)
                ins = pe.matmul(psum[6][r:r + 64, (h // 2) * P:(h // 2 + 1) * P], KDT[:, h // 2, r:r + 64], VB[:, 0, h * P:(h + 1) * P],
                                start=True, stop=True)
            ins.then_inc(ev("state_done"), 1)
            pe.wait_ge(ev("state_ready"), 1)
            pe.wait_ge(ev("ats_ready"), 1)
            for h in range(4):
                r = 64 * (h % 2)
                for c in range(2):
                    o = psum[4 + h % 2][:, (h // 2) * T + c * P:(h // 2) * T + (c + 1) * P]
                    ins = pe.matmul(o, VB[:, c, h * P:(h + 1) * P], ATS[:, h % 2, (h // 2) * 2 + c, :], start=True, stop=c == 0)
                    if c == 1:
                        ins = pe.matmul(o, ST[r:r + 64, h // 2, :], QI[r:r + 64, h // 2, :], start=False, stop=True)
            ins.then_inc(ev("gla_out"), 1)
            pe.wait_ge(ev("squares"), seen.next(ev("squares")))
            for b in range(2):
                ins = pe.matmul(psum[b][:, :], M("ones"), sq[:, 2 * b:2 * b + 2, :], start=True, stop=True)
            ins.then_inc(ev("sum_ready"), 1)
            pe.wait_ge(ev("h_ready"), seen.next(ev("h_ready"), KT))
            for m in range(KT):
                linear()
            norm_sum()
            pe.wait_ge(ev("h_ready"), seen.next(ev("h_ready"), KT))
            lin_all_read()
            ffn(FF_STEPS)
            norm_sum()
            pe.wait_ge(ev("h_ready"), seen.next(ev("h_ready"), KT))
            for n in range(N_ODD_IN):
                linear(tokens=17 <= n < 25)
            for _ in range(2):
                pe.wait_ge(ev("squares"), seen.next(ev("squares")))
                for k in range(8):
                    ins = pe.matmul(half(k // 2, k % 2), M("block64"), sq[:, k, :], start=True, stop=True)
                ins.then_inc(ev("sum_ready"), 1)
            attention("odd")
            pe.wait_ge(ev("h_ready"), seen.next(ev("h_ready"), KT))
            for m in range(KT):
                linear()
            norm_sum()
            pe.wait_ge(ev("h_ready"), seen.next(ev("h_ready"), KT))
            linear(tokens=True)
            lin_all_read()
            pe.wait_ge(ev("chosen"), 1)
            pe.matmul(psum[7][:, 0:N_EXP], M("mask01"), SEL[:, 0, :], start=True, stop=True)
            pe.matmul(psum[7][:, 8:8 + N_EXP], M("ones"), SEL[:, 0, :], start=True, stop=False)
            pe.matmul(psum[7][:, 8:8 + N_EXP], M("mask01"), SEL[:, 1, :], start=False, stop=True)
            for t in range(2):
                ins = pe.matmul(psum[7][:, 16:16 + N_EXP], M("ones"), SEL[:, t, :], start=t == 0, stop=t == 1)
            ins.then_inc(ev("slots_counted"), 1)
            pe.wait_ge(ev("routed"), 1)
            n = pe.value_load(fullest[0:1, 0:1], min_val=0, max_val=T)
            with pe.If(n > P):
                dense_experts(pos[0])
            with pe.Else():
                sparse_experts(pos[0])
            pos[0] += N_EXP * EXP_PACKS
            norm_sum()
            for l in range(2):
                for stream in ("context", "latents"):
                    only_kv = l == 1 and stream == "context"
                    norm_sum()
                    pe.wait_ge(ev("h_ready"), seen.next(ev("h_ready"), KT))
                    for n in range(N_IN_KV if only_kv else N_IN):
                        linear(tokens=5 <= n < 8)
                    pe.wait_ge(ev("squares"), seen.next(ev("squares")))
                    pe.matmul(half(0, 0), M("ones"), sq[:, 0, :], start=True, stop=True)
                    ins = pe.matmul(half(1, 0), M("block64"), sq[:, 1, :], start=True, stop=True)
                    if not only_kv:
                        for k in range(4):
                            pe.matmul(half(2 + k // 2, k % 2), M("block64"), sq[:, 2 + k, :], start=True, stop=True)
                        pe.matmul(half(0, 1), M("ones"), sq[:, 6, :], start=True, stop=False)
                        ins = pe.matmul(half(0, 1), M("ones"), sq[:, 7, :], start=False, stop=True)
                    ins.then_inc(ev("sum_ready"), 1)
                    pe.wait_ge(ev("latent_split"), seen.next(ev("latent_split")))
                    lin_all_read()
                    pe.wait_ge(lo_done, pos[0] + 1)
                    s = pos[0] % RING
                    for h in range(4):
                        mm3(half(h // 2, h % 2), h_hi[:, 0, :], h_lo[:, 0, :], True, True, s, slice(h * P, (h + 1) * P))
                    vh = w_hi[:, s, 0:512].rearrange("p (h c) -> p h c", h=4)[:, :, 64:128]
                    vl = w_lo[:, s, 0:512].rearrange("p (h c) -> p h c", h=4)[:, :, 64:128]
                    for tk in range(2):
                        tt = slice(tk * P, (tk + 1) * P)
                        pe.matmul(half(6, tk), h_hi[:, 0, tt], vh, start=True, stop=False)
                        pe.matmul(half(6, tk), h_lo[:, 0, tt], vh, start=False, stop=False)
                        ins = pe.matmul(half(6, tk), h_hi[:, 0, tt], vl, start=False, stop=True)
                    ins.then_inc(pack_used, 1)
                    pos[0] += 1
                    if not only_kv:
                        pe.wait_ge(lo_done, pos[0] + 1)
                        s = pos[0] % RING
                        for h in range(4):
                            for k in range(2):
                                ins = mm3(half(2 + h // 2, h % 2), h_hi[:, 1 + k, :], h_lo[:, 1 + k, :], k == 0, k == 1, s,
                                          slice((2 * h + k) * P, (2 * h + k + 1) * P))
                        ins.then_inc(pack_used, 1)
                        pos[0] += 1
                    if stream == "latents":
                        pe.wait_ge(ev("rope_in"), seen.next(ev("rope_in")))
                        for n, (rot, _, _, rows, x) in enumerate(ROPED):
                            if n >= 2:
                                pe.wait_ge(ev("rope_out"), seen.now(ev("rope_out")) + n - 1)
                            width = x.shape[1] * T
                            pe.matmul(psum[4 + n % 2][0:rows, 0:width], M(rot)[0:rows, 0:rows], x, start=True, stop=True)\
                              .then_inc(ev("rotated"), 1)
                        seen.next(ev("rope_out"), len(ROPED))
                    if only_kv:
                        continue
                    attention(stream)
                    pe.wait_ge(ev("squares"), seen.next(ev("squares")))
                    pe.matmul(psum[0][:, :], M("block64"), sq[:, 0:2, :], start=True, stop=True).then_inc(ev("sum_ready"), 1)
                    pe.wait_ge(ev("h_ready"), seen.next(ev("h_ready"), KT))
                    for m in range(KT):
                        linear()
                    norm_sum()
                    norm_sum()
                    pe.wait_ge(ev("h_ready"), seen.next(ev("h_ready"), KT))
                    lin_all_read()
                    ffn(FF_STEPS)
                    norm_sum()
            assert pos[0] == TOTAL

        @block.scalar
        def _(act):
            seen = Seen()
            steps = [0]
            nsplit = [0]
            nlin = [0]

            def A(out, in_, func, **kw):
                return act.activation(out, in_, func, **kw)

            def step(ins):
                steps[0] += 1
                ins.then_inc(ev("act_step"), 1)

            def settle():
                act.wait_ge(ev("act_step"), steps[0])

            def wait(name, n=1):
                act.wait_ge(ev(name), seen.next(ev(name), n))

            def split_at(p, slot, turn, reuse):
                act.wait_ge(raw_in[slot], 16 * turn + 16)
                if reuse:
                    act.wait_ge(pack_used, p - RING + 1)
                    act.wait_ge(lo_done, p - RING + 1)
                A(w_hi[:, slot, :], raw[:, slot, :], ACT.Copy).then_inc(hi_done, 1)

            def split_to(p):
                while nsplit[0] < min(p, TOTAL):
                    n = nsplit[0]
                    split_at(n, n % RING, n // RING, n >= RING)
                    nsplit[0] += 1

            def lin_wait():
                split_to(2 * N_ADA + nlin_pos[0] + AHEAD)
                nlin_pos[0] += 1
                act.wait_ge(pack_used, 2 * N_ADA + nlin_pos[0])
                b = 4 + nlin[0] % 2
                nlin[0] += 1
                return b

            nlin_pos = [0]
            nffn = [0]

            def fm(out, func=ACT.Copy, **kw):
                b = lin_wait()
                A(out, half(b, 0), func, **kw).then_inc(ev("lin_read"), 1)

            def tm(out, func=ACT.Copy, **kw):
                b = lin_wait()
                A(out, half(b, 0).rearrange("p (a b) -> p a b", a=2), func, **kw).then_inc(ev("lin_read"), 1)

            def rsqrt_of(out, in_, scale, bias, sem):
                step(A(out, in_, ACT.Ln, scale=scale, bias=bias))
                settle()
                A(out, out, ACT.Exp, scale=-0.5).then_inc(sem, 1)

            def norm(x, shift=None):
                for k in range(0, KT, 2):
                    A(sq[:, k:k + 2, :], x[:, k:k + 2, :], ACT.Square).then_inc(ev("squares"), 1)
                wait("sum_ready")
                rsqrt_of(rs[:], half(6, 0), 1.0 / D, V("eps"), ev("rs_ready"))
                if shift is not None:
                    for k in range(KT):
                        wait("scaled")
                        A(h_hi[:, k, :], tmp[:, k, :], ACT.Identity, bias=shift(k)).then_inc(ev("h_hi_ready"), 1)

            def split_tmp():
                for k in range(KT):
                    wait("scaled")
                    A(h_hi[:, k, :], tmp[:, k, :], ACT.Copy).then_inc(ev("h_hi_ready"), 1)

            def skip_linears(n):
                for _ in range(n):
                    split_to(2 * N_ADA + nlin_pos[0] + AHEAD)
                    nlin_pos[0] += 1
                    nlin[0] += 1

            def ffn(n_steps):
                base = nffn[0]
                first = 2 * N_ADA + nlin_pos[0]
                split_to(first + AHEAD)
                p0 = nsplit[0]

                def one(s, par, off, it):
                    act.wait_ge(pack_used, first + 2 if isinstance(s, int) and s == 0 else s * 3 + (first + 1))
                    if not isinstance(s, int) or base + s >= 2:
                        act.wait_ge(ev("act_ready"), base + s - 1)
                    A(sg[:, par, :], half(4 + par, 0), ACT.Silu).then_inc(ev("silu_done"), 1)
                    for j in range(3):
                        p = p0 + off + j
                        if isinstance(s, int) and p >= TOTAL:
                            continue
                        slot = p % RING
                        split_at(it * RING + p if it is not None else p, slot,
                                 (it + p // RING) if it is not None else p // RING, True)

                last = p0 + 3 * n_steps >= TOTAL
                head, tail = 2, 4 if last else 0
                for s in range(head):
                    one(s, s % 2, 3 * s, None)
                with act.Fori(0, (n_steps - head - tail) // 2) as i:
                    for j in range(2):
                        one(i * 2 + (head + j), j, 3 * (head + j), i)
                for s in range(n_steps - tail, n_steps):
                    one(s, s % 2, 3 * s, None)
                nffn[0] += n_steps
                nsplit[0] = min(p0 + 3 * n_steps, TOTAL)
                nlin_pos[0] += 3 * n_steps

            def attention(kind):
                heads, n_keys = heads_and_keys(kind)
                for u in range(2 * len(heads) + 1):
                    if u < 2 * len(heads):
                        n = n_keys(u % 2) * P
                        wait("max_ready")
                        src = logit[:, u % 2, 0:n] if kind == "odd" else psum[u % 2][:, 0:n]
                        A(prob[:, u % 2, 0:n], src, ACT.Exp, bias=small[:, 8 + u % 2:9 + u % 2],
                          accum_out=small[:, 10 + u % 2:11 + u % 2]).then_inc(ev("exp_done"), 1)
                    if u >= 1:
                        v = u - 1
                        c, i = v % 2, v // 2
                        ns = n_keys(c)
                        wait("turned")
                        if i >= 2:
                            act.wait_ge(ev("value_done"), seen.now(ev("value_done")) + i - 1)
                        out = prob_t[:, i % 2, :].rearrange("p (s t) -> p s t", t=T)[:, 0:ns, c * P:(c + 1) * P]
                        A(out, psum[2 + v % 2][:, 0:ns * P].rearrange("p (s t) -> p s t", t=P), ACT.Copy)\
                            .then_inc(ev("prob_t_ready"), 1)
                seen.next(ev("value_done"), len(heads))

            def experts(sparse):
                base = 2 * N_ADA + nlin_pos[0]

                class Ahead:
                    n = AHEAD

                def split(n, e, i=None):
                    while Ahead.n < n:
                        c = base + Ahead.n
                        p, turn = e * EXP_PACKS + c, e * (EXP_PACKS // RING) + c // RING
                        if i is not None:
                            p, turn = i * 12 + p, i * (12 // RING) + turn
                        split_at(p, c % RING, turn, True)
                        Ahead.n += 1

                def silu(g, p):
                    act.wait_ge(pack_used, p + 4)
                    if sparse:
                        act.wait_ge(ev("m_prod"), g)
                        A(SG_WIDE, psum[0][:, :], ACT.Silu).then_inc(ev("m_silu"), 1)
                    else:
                        A(sq[:, 0:2, :], psum[4][:, :].rearrange("p (a t) -> p a t", a=2), ACT.Silu)
                        A(sq[:, 2:4, :], psum[5][:, :].rearrange("p (a t) -> p a t", a=2), ACT.Silu).then_inc(ev("d_silu"), 1)

                def high(g):
                    if sparse:
                        act.wait_ge(ev("m_turned"), g + 1)
                        A(F_HI, psum[4][:, :].rearrange("p (j s) -> p j s", s=P), ACT.Copy).then_inc(ev("m_f_hi"), 1)

                def gathered(n):
                    act.wait_ge(ev("m_gathered"), n + 1)
                    for c in range(2):
                        ins = A(X_HI[:, 4 * c:4 * c + 4, :], psum[5 + c][:, :].rearrange("p (k s) -> p k s", s=P), ACT.Copy)
                    ins.then_inc(ev("m_x_hi"), 1)

                if sparse:
                    act.wait_ge(ev("m_h_turned"), 1)
                    for c in range(2):
                        ins = A(HT[:, 0, c * 512:(c + 1) * 512], psum[c][:, :], ACT.Copy)
                    ins.then_inc(ev("m_h_t0"), 1)
                    gathered(0)
                with act.Fori(0, N_EXP) as e:
                    Ahead.n = AHEAD
                    for n in (0, 1):
                        at = group_at(n)
                        split(at + 4 + AHEAD, e)
                        silu(e * GROUPS + n, e * EXP_PACKS + (base + at))
                        if n:
                            high(e * GROUPS)
                        split(at + 8 + AHEAD, e)
                    split(group_at(2) + AHEAD, e)
                    if sparse:
                        act.wait_ge(ev("m_choice_turned"), e + 1)
                        A(choice_t[:], half(7, 0), ACT.Copy)
                        A(SLOT_GATE, psum[7][:, T:T + 1], ACT.Copy).then_inc(ev("m_choice_t"), 1)
                    with act.Fori(0, GROUPS - 2) as i:
                        at = group_at(2)
                        split(at + 4 + AHEAD, e, i)
                        silu(e * GROUPS + i + 2, e * EXP_PACKS + i * 12 + (base + at))
                        high(e * GROUPS + i + 1)
                        split(at + 12 + AHEAD, e, i)
                    Ahead.n = group_at(GROUPS) + AHEAD
                    if sparse:
                        gathered(e + 1)
                        high(e * GROUPS + (GROUPS - 1))
                    split(EXP_PACKS + AHEAD, e)
                    if sparse:
                        act.wait_ge(pack_used, e * EXP_PACKS + (base + EXP_PACKS))
                        act.wait_ge(ev("m_choice_t"), e + 2)
                        for c in range(2):
                            ins = A(Y_HI[:, 4 * c:4 * c + 4, :], psum[2 + c][:, :].rearrange("p (k s) -> p k s", s=P), ACT.Copy,
                                    scale=SLOT_GATE)
                        ins.then_inc(ev("m_y_hi"), 1)

            act.wait_ge(ev("vec_in"), 16)
            A(cond_s[:].rearrange("p k s -> p (k s)"), V("cond"), ACT.Silu).then_inc(ev("cond_silu"), 1)
            split_to(RING)

            def ada_row(g, j):
                act.wait_ge(pack_used, g * 4 + 4)
                if not isinstance(g, int) or g >= 3:
                    act.wait_ge(ev("ada_turned"), g - 2)
                A(ada_rows[0:2, j, :], psum[4 + j][0:2, :], ACT.Copy).then_inc(ev("ada_row"), 1)

            for g in range(3):
                split_to(4 * g + 4 + AHEAD)
                ada_row(g, g)
            with act.Fori(0, ADA_GROUPS // 3 - 1) as i:
                for j in range(3):
                    for q in range(4):
                        n = 12 + AHEAD + 4 * j + q
                        split_at(i * 12 + n, n % RING, i * 2 + n // RING, True)
                    ada_row(i * 3 + (3 + j), j)
            nsplit[0] = 2 * N_ADA + AHEAD
            wait("lam_sum")
            A(small[:, 4:8], psum[6][:, 0:4], ACT.Exp).then_inc(ev("lam_exp"), 1)
            act.wait_ge(ev("lat_in"), 16)
            norm(lat, lambda k: V("zero"))
            fm(GLR)
            for t in range(2):
                fm(QT[:, t, :], scale=0.125)
            for t in range(2):
                fm(KTT[:, t, :])
            for t in range(4):
                tm(VB[:, :, t * P:(t + 1) * P])
            for t in range(4):
                tm(VA[:, :, t * P:(t + 1) * P], ACT.Gelu_apprx_tanh)
            for t in range(4):
                fm(U[:, t, :], ACT.Gelu_apprx_tanh)
            for t in range(4):
                fm(OG[:, t, :], ACT.Silu)
            wait("gate_done")
            for t in range(2):
                A(GX[:, t, :], half(6, t), ACT.Identity, bias=V("gate_bias", t)).then_inc(ev("gx_ready"), 1)
            wait("abs_ready")
            step(A(QQ, QQ, ACT.Exp))
            settle()
            A(QQ, QQ, ACT.Ln, bias=V("one")).then_inc(ev("softplus_ready"), 1)
            wait("var_ready")
            step(A(small[:, 16:18], small[:, 16:18], ACT.Ln, bias=V("eps")))
            settle()
            A(small[:, 16:18], small[:, 16:18], ACT.Exp, scale=-0.5).then_inc(ev("rstd_ready"), 1)
            wait("diffs_ready")
            A(EK, EK, ACT.Exp, scale=-1.0 / 16).then_inc(ev("exps_ready"), 1)
            A(QQ, QQ, ACT.Exp, scale=1.0 / 16).then_inc(ev("exps_ready"), 1)
            A(QI, G[:, :, P:2 * P], ACT.Exp, scale=1.0 / 16).then_inc(ev("exps_ready"), 1)
            A(KD, KD, ACT.Exp, scale=-1.0 / 16).then_inc(ev("exps_ready"), 1)
            wait("gla_out")
            for b in range(2):
                ins = A(sq[:, b:4:2, :], psum[4 + b][:, :].rearrange("p (a t) -> p a t", a=2), ACT.Square)
                if b == 1:
                    ins.then_inc(ev("squares"), 1)
            for b in range(2):
                step(A(tmp[:, b:4:2, :], psum[4 + b][:, :].rearrange("p (a t) -> p a t", a=2), ACT.Copy))
            settle()
            wait("sum_ready")
            for b in range(2):
                step(A(sq[:, 4 + 2 * b:6 + 2 * b, :], psum[b][:, :].rearrange("p (a t) -> p a t", a=2), ACT.Ln,
                       scale=1.0 / P, bias=V("eps")))
            settle()
            A(sq[:, 4:8, :], sq[:, 4:8, :], ACT.Exp, scale=-0.5).then_inc(ev("rs_ready"), 1)
            split_tmp()
            skip_linears(KT)
            wait("x_ready")
            norm(lat, lambda k: V("zero"))
            ffn(FF_STEPS)
            wait("x_ready")
            norm(lat, lambda k: V("zero"))
            fm(OF)
            for t in range(8):
                fm(OQ[:, t, :])
            for t in range(8):
                fm(OK[:, t, :])
            for t in range(8):
                tm(OV[:, :, t * P:(t + 1) * P])
            for t in range(8):
                fm(OO[:, t, :], ACT.Sigmoid)
            act.wait_ge(ev("lin_read"), nlin[0])
            A(OF[0:C_HEADS], OF[0:C_HEADS], ACT.Identity, bias=V("forget_bias")[0:C_HEADS]).then_inc(ev("f_ready"), 1)
            wait("abs_ready")
            step(A(ONC[0:C_HEADS], ONC[0:C_HEADS], ACT.Exp))
            settle()
            A(ONC[0:C_HEADS], ONC[0:C_HEADS], ACT.Ln, bias=V("one")[0:C_HEADS]).then_inc(ev("softplus_ready"), 1)
            for which, x in enumerate((OQ, OK)):
                if which:
                    wait("qk_scaled")
                A(sq[:], x, ACT.Square).then_inc(ev("squares"), 1)
                wait("sum_ready")
                for b in range(4):
                    step(A(sq[:, 2 * b:2 * b + 2, :], psum[b][:, :].rearrange("p (a t) -> p a t", a=2), ACT.Ln,
                           scale=1.0 if which == 0 else 1.0 / 64, bias=V("eps64") if which == 0 else V("eps")))
                settle()
                A(sq[:], sq[:], ACT.Exp, scale=-0.5).then_inc(ev("rs_ready"), 1)
            attention("odd")
            split_tmp()
            skip_linears(KT)
            wait("x_ready")
            norm(lat, lambda k: V("zero"))
            tm(RL)
            wait("top_diff")
            A(small[:, 24:26], small[:, 24:26], ACT.Exp).then_inc(ev("top_exp"), 1)
            split_to(2 * N_ADA + nlin_pos[0] + AHEAD)
            act.wait_ge(ev("routed"), 1)
            n = act.value_load(fullest[0:1, 0:1], min_val=0, max_val=T)
            with act.If(n > P):
                experts(sparse=False)
            with act.Else():
                experts(sparse=True)
            nlin_pos[0] += N_EXP * EXP_PACKS
            nsplit[0] += N_EXP * EXP_PACKS
            wait("x_ready")
            norm(lat)
            for l in range(2):
                for s, (stream, x) in enumerate((("context", con), ("latents", lat))):
                    only_kv = l == 1 and stream == "context"
                    k0 = T if stream == "context" else 0
                    col = 1 - s
                    if (l, s) == (0, 0):
                        act.wait_ge(ev("con_in"), 16)
                        wait("x_ready")
                    norm(x, lambda k: mod[:, l, k, col:col + 1])
                    fm(ZR[:, 0, :])
                    fm(KPE)
                    for t in range(2):
                        fm(KD2[:, t, k0:k0 + T])
                    fm(ZR[:, 1, :])
                    for t in range(2):
                        tm(VD[:, k0 // P:k0 // P + 2, t * P:(t + 1) * P])
                    tm(VG[:, k0 // P:k0 // P + 2, :])
                    if not only_kv:
                        for t in range(2):
                            fm(ZR[:, 6 + t, :])
                        for t in range(2):
                            fm(QD[:, t, :], scale=DIFF_SCALE)
                        for t in range(4):
                            fm(ZR[:, 2 + t, :])
                    act.wait_ge(ev("lin_read"), nlin[0])
                    n = 2 if only_kv else 8
                    A(sq[:, 0:n, :], ZR[:, 0:n, :], ACT.Square).then_inc(ev("squares"), 1)
                    wait("sum_ready")
                    step(A(sq[:, 0, :], half(0, 0), ACT.Ln, scale=1.0 / 128, bias=V("eps")))
                    step(A(sq[:, 1, :], half(1, 0), ACT.Ln, scale=1.0 / 64, bias=V("eps")))
                    if not only_kv:
                        for b in range(2):
                            step(A(sq[:, 2 + 2 * b:4 + 2 * b, :], psum[2 + b][:, :].rearrange("p (a t) -> p a t", a=2),
                                   ACT.Ln, scale=1.0, bias=V("eps64")))
                        step(A(sq[:, 6, :], half(0, 1), ACT.Ln, scale=1.0 / 256, bias=V("eps")))
                    settle()
                    n = 2 if only_kv else 7
                    A(sq[:, 0:n, :], sq[:, 0:n, :], ACT.Exp, scale=-0.5).then_inc(ev("rs_ready"), 1)
                    wait("latents_normed")
                    n = 1 if only_kv else 3
                    A(h_hi[:, 0:n, :], tmp[:, 0:n, :], ACT.Copy).then_inc(ev("latents_hi"), 1)
                    split_to(2 * N_ADA + nlin_pos[0] + AHEAD)
                    nlin_pos[0] += 1
                    act.wait_ge(pack_used, 2 * N_ADA + nlin_pos[0])
                    for b in range(2):
                        A(KM[0:64, 2 * b:2 * b + 2, k0:k0 + T], psum[b][0:64, :].rearrange("p (a t) -> p a t", a=2), ACT.Copy)\
                            .then_inc(ev("km_ready"), 1)
                    A(VM[:, k0 // P:k0 // P + 2, :], psum[6][:, :].rearrange("p (a t) -> p a t", a=2), ACT.Copy)\
                        .then_inc(ev("km_ready"), 1)
                    if not only_kv:
                        split_to(2 * N_ADA + nlin_pos[0] + AHEAD)
                        nlin_pos[0] += 1
                        act.wait_ge(pack_used, 2 * N_ADA + nlin_pos[0])
                        for b in range(2):
                            A(QM[0:MLA_QK, 2 * b:2 * b + 2, :], psum[2 + b][0:MLA_QK, :].rearrange("p (a t) -> p a t", a=2),
                              ACT.Copy, scale=MLA_SCALE).then_inc(ev("qm_ready"), 1)
                    if only_kv:
                        wait("context_keys_ready")
                        continue
                    attention(stream)
                    wait("diff_ready")
                    A(sq[:, 0:2, :], tmp[:, 2:4, :], ACT.Square).then_inc(ev("squares"), 1)
                    wait("sum_ready")
                    step(A(sq[:, 2:4, :], psum[0][:, :].rearrange("p (a t) -> p a t", a=2), ACT.Ln, scale=1.0 / 64, bias=V("eps")))
                    settle()
                    A(sq[:, 2:4, :], sq[:, 2:4, :], ACT.Exp, scale=-0.5).then_inc(ev("rs_ready"), 1)
                    split_tmp()
                    for m in range(KT):
                        fm(ZR[:, m, :])
                    act.wait_ge(ev("lin_read"), nlin[0])
                    norm(ZR)
                    wait("x_ready")
                    norm(x, lambda k: mod[:, l, 24 + k, col:col + 1])
                    ffn(FF_STEPS)
                    act.wait_ge(pack_used, 2 * N_ADA + nlin_pos[0])
                    for b in range(4):
                        step(A(ZR[:, 2 * b:2 * b + 2, :], psum[b][:, :].rearrange("p (a t) -> p a t", a=2), ACT.Copy))
                    settle()
                    norm(ZR)
                    wait("x_ready")

        @block.vector
        def _(v):
            seen = Seen()
            steps = [0]
            nsplit = [0]
            npos = [0]
            nlin = [0]

            def step(ins):
                steps[0] += 1
                ins.then_inc(ev("dve_step"), 1)

            def settle():
                v.wait_ge(ev("dve_step"), steps[0])

            def link(ins):
                step(ins)
                settle()

            def wait(name, n=1):
                v.wait_ge(ev(name), seen.next(ev(name), n))

            def split_at(p, slot, reuse):
                v.wait_ge(hi_done, p + 1)
                if reuse:
                    v.wait_ge(pack_used, p - RING + 1)
                v.tensor_tensor(w_lo[:, slot, :], raw[:, slot, :], w_hi[:, slot, :].bitcast(F32), ALU.subtract)\
                    .then_inc(lo_done, 1)

            def split_to(p):
                while nsplit[0] < min(p, TOTAL):
                    n = nsplit[0]
                    split_at(n, n % RING, n >= RING)
                    nsplit[0] += 1

            def norm(x, gain, shift=None, out=None):
                wait("rs_ready")
                out = tmp if out is None else out
                for k in range(KT):
                    ins = v.scalar_tensor_tensor(out[:, k, :], x[:, k, :], gain(k), rs[:], ALU.mult, ALU.mult)
                    if shift is not None:
                        ins.then_inc(ev("scaled"), 1)
                    else:
                        step(ins)
                if shift is None:
                    settle()
                    return
                for k in range(KT):
                    wait("h_hi_ready")
                    v.scalar_tensor_tensor(h_lo[:, k, :], tmp[:, k, :], shift(k), h_hi[:, k, :].bitcast(F32), ALU.add,
                                           ALU.subtract).then_inc(ev("h_ready"), 1)

            def low_part(k):
                wait("h_hi_ready")
                v.tensor_tensor(h_lo[:, k, :], tmp[:, k, :], h_hi[:, k, :].bitcast(F32), ALU.subtract)\
                    .then_inc(ev("h_ready"), 1)

            def others_read(n):
                for _ in range(n):
                    split_to(2 * N_ADA + npos[0] + AHEAD)
                    npos[0] += 1
                    nlin[0] += 1

            def add_linears(x):
                for m in range(KT):
                    split_to(2 * N_ADA + npos[0] + AHEAD)
                    npos[0] += 1
                    v.wait_ge(pack_used, 2 * N_ADA + npos[0])
                    b = 4 + nlin[0] % 2
                    nlin[0] += 1
                    v.tensor_tensor(x[:, m, :], x[:, m, :], half(b, 0), ALU.add).then_inc(ev("lin_read"), 1)
                v.wait_ge(ev("lin_read"), nlin[0])
                v.sem_inc(ev("x_ready"), 1)

            def ffn(n_steps):
                base = seen.now(ev("silu_done"))
                start = 2 * N_ADA + npos[0]
                split_to(2 * N_ADA + npos[0] + AHEAD)
                p0 = nsplit[0]

                def one(s, par, off, it):
                    v.wait_ge(ev("silu_done"), base + s + 1)
                    if not isinstance(s, int) or base + s >= 2:
                        v.wait_ge(pack_used, s * 3 + (start - 1))
                    v.tensor_tensor(prod[:, par, :], sg[:, par, :], half(4 + par, 1), ALU.mult).then_inc(ev("prod_done"), 1)
                    v.wait_ge(ev("prod_done"), base + s + 1)
                    v.tensor_copy(f_hi[:, par, :], prod[:, par, :]).then_inc(ev("f_hi_done"), 1)
                    v.wait_ge(ev("f_hi_done"), base + s + 1)
                    v.tensor_tensor(f_lo[:, par, :], prod[:, par, :], f_hi[:, par, :].bitcast(F32), ALU.subtract)\
                        .then_inc(ev("act_ready"), 1)
                    for j in range(3):
                        p = p0 + off + j
                        if isinstance(s, int) and p >= TOTAL:
                            continue
                        split_at(p if it is None else it * RING + p, p % RING, True)

                last = p0 + 3 * n_steps >= TOTAL
                head, tail = 2, 4 if last else 0
                for s in range(head):
                    one(s, s % 2, 3 * s, None)
                with v.Fori(0, (n_steps - head - tail) // 2) as i:
                    for j in range(2):
                        one(i * 2 + (head + j), j, 3 * (head + j), i)
                for s in range(n_steps - tail, n_steps):
                    one(s, s % 2, 3 * s, None)
                seen.next(ev("silu_done"), n_steps)
                nsplit[0] = min(p0 + 3 * n_steps, TOTAL)
                npos[0] += 3 * n_steps

            def experts(sparse):
                base = 2 * N_ADA + npos[0]

                class Ahead:
                    n = AHEAD

                def split(n, e, i=None):
                    while Ahead.n < n:
                        c = base + Ahead.n
                        split_at(e * EXP_PACKS + c if i is None else e * EXP_PACKS + i * 12 + c, c % RING, True)
                        Ahead.n += 1

                def product(g, p):
                    v.wait_ge(ev("m_silu"), g + 1)
                    v.wait_ge(pack_used, p)
                    v.tensor_tensor(PROD_WIDE, SG_WIDE, psum[1][:, :], ALU.mult).then_inc(ev("m_prod"), 1)

                def product_all(g, p, e):
                    v.wait_ge(ev("d_silu"), g + 1)
                    v.wait_ge(pack_used, p)
                    v.wait_ge(ev("d_split"), g * 2)
                    for b in range(2):
                        ins = v.tensor_tensor(sq[:, 4 + 2 * b:6 + 2 * b, :], sq[:, 2 * b:2 * b + 2, :],
                                              psum[6 + b][:, :].rearrange("p (a t) -> p a t", a=2), ALU.mult)
                        ins.then_inc(ev("d_mul"), 1)
                    v.wait_ge(ev("d_mul"), g * 2 + 2)
                    v.tensor_tensor(sq[:, 4:8, :], sq[:, 4:8, :], GB[:, bass.ds(e, 1), :].to_broadcast([P, 4, T]), ALU.mult)\
                        .then_inc(ev("d_prod"), 1)

                def pair_parts(g, n):
                    v.wait_ge(ev("d_prod"), g + 1)
                    src = sq[:, 4 + 2 * n:6 + 2 * n, :]
                    v.tensor_copy(f_hi[:], src).then_inc(ev("d_f_hi"), 1)
                    v.wait_ge(ev("d_f_hi"), g * 2 + (n + 1))
                    v.tensor_tensor(f_lo[:], src, f_hi[:].bitcast(F32), ALU.subtract).then_inc(ev("d_split"), 1)

                def low(g):
                    v.wait_ge(ev("m_f_hi"), g + 1)
                    v.tensor_tensor(F_LO, psum[4][:, :].rearrange("p (j s) -> p j s", s=P), F_HI.bitcast(F32), ALU.subtract)\
                        .then_inc(ev("m_split"), 1)

                def choose(n):
                    v.tensor_copy(CUR_SLOT.unsqueeze(2), SLOT[:, :, bass.ds(n, 1)]).then_inc(ev("m_columns"), 1)
                    v.tensor_copy(CUR_GATE.unsqueeze(2), GATE[:, :, bass.ds(n, 1)]).then_inc(ev("m_columns"), 1)
                    v.wait_ge(ev("m_columns"), n * 2 + 2)
                    for t in range(2):
                        ins = v.tensor_scalar(CHOICE[:, t, :], M("iota"), CUR_SLOT[:, t:t + 1], None, ALU.is_equal)
                    ins.then_inc(ev("m_choice"), 1)

                def gathered(n):
                    v.wait_ge(ev("m_x_hi"), n + 1)
                    for c in range(2):
                        ins = v.tensor_tensor(X_LO[:, 4 * c:4 * c + 4, :], psum[5 + c][:, :].rearrange("p (k s) -> p k s", s=P),
                                              X_HI[:, 4 * c:4 * c + 4, :].bitcast(F32), ALU.subtract)
                    ins.then_inc(ev("m_x_split"), 1)

                def add(n):
                    v.wait_ge(ev("m_scattered"), n + 1)
                    for b in range(4):
                        ins = v.tensor_tensor(lat[:, 2 * b:2 * b + 2, :], lat[:, 2 * b:2 * b + 2, :],
                                              psum[SCATTER_BANKS[b]][:, :].rearrange("p (a t) -> p a t", a=2), ALU.add)
                    ins.then_inc(ev("m_added"), 1)

                def sparse_expert(e):
                    g, p = e * GROUPS, e * EXP_PACKS + base
                    split(8 + AHEAD, e)
                    product(g, p + 8)
                    add(e)
                    at = group_at(1)
                    split(at + 4 + AHEAD, e)
                    low(g)
                    split(at + 8 + AHEAD, e)
                    product(g + 1, p + (at + 8))
                    split(at + 12 + AHEAD, e)
                    v.wait_ge(ev("m_choice_turned"), e + 1)
                    choose(e + 1)
                    with v.Fori(0, GROUPS - 2) as i:
                        at = group_at(2)
                        g2, p2 = e * GROUPS + i + 1, e * EXP_PACKS + i * 12 + (base + at + 8)
                        split(at + 4 + AHEAD, e, i)
                        low(g2)
                        split(at + 8 + AHEAD, e, i)
                        product(g2 + 1, p2)
                        split(at + 12 + AHEAD, e, i)
                    Ahead.n = group_at(GROUPS) + AHEAD
                    gathered(e + 1)
                    low(g + (GROUPS - 1))
                    split(EXP_PACKS + AHEAD, e)
                    v.wait_ge(ev("m_y_hi"), e + 1)
                    for c in range(2):
                        ins = v.scalar_tensor_tensor(Y_LO[:, 4 * c:4 * c + 4, :], psum[2 + c][:, :].rearrange("p (k s) -> p k s", s=P),
                                                     SLOT_GATE, Y_HI[:, 4 * c:4 * c + 4, :].bitcast(F32), ALU.mult, ALU.subtract)
                    ins.then_inc(ev("m_y_split"), 1)

                def dense_expert(e):
                    g, p = e * GROUPS, e * EXP_PACKS + base
                    split(8 + AHEAD, e)
                    product_all(g, p + 8, e)
                    pair_parts(g, 0)

                    def group(at, g, p, i=None):
                        split(at + 10 + AHEAD, e, i)
                        v.wait_ge(pack_used, p + 10)
                        pair_parts(g - 1, 1)
                        split(at + 12 + AHEAD, e, i)
                        product_all(g, p + 12, e)
                        pair_parts(g, 0)

                    group(group_at(1), g + 1, p + group_at(1))
                    with v.Fori(0, GROUPS - 2) as i:
                        group(group_at(2), e * GROUPS + i + 2, e * EXP_PACKS + i * 12 + (base + group_at(2)), i)
                    Ahead.n = group_at(GROUPS) + AHEAD
                    split(EXP_PACKS - 2 + AHEAD, e)
                    v.wait_ge(pack_used, p + (EXP_PACKS - 2))
                    pair_parts(g + (GROUPS - 1), 1)
                    split(EXP_PACKS + AHEAD, e)
                    v.wait_ge(pack_used, p + EXP_PACKS)
                    for b in range(4):
                        ins = v.tensor_tensor(lat[:, 2 * b:2 * b + 2, :], lat[:, 2 * b:2 * b + 2, :],
                                              psum[b][:, :].rearrange("p (a t) -> p a t", a=2), ALU.add)
                    ins.then_inc(ev("d_added"), 1)

                if sparse:
                    v.wait_ge(ev("m_h_turned"), 1)
                    for c in range(2):
                        v.tensor_copy(HT[:, 1, c * 512:(c + 1) * 512], psum[2 + c][:, :]).then_inc(ev("m_h_t1"), 1)
                    v.wait_ge(ev("m_h_t1"), 2)
                    v.wait_ge(ev("m_h_t0"), 1)
                    v.sem_inc(ev("m_h_t"), 1)
                    choose(0)
                    zero = V("zero")
                    for a in (Y_HI, Y_LO):
                        v.tensor_copy(a, zero.unsqueeze(2).to_broadcast([P, KT, P])).then_inc(ev("m_zeroed"), 1)
                    v.tensor_copy(choice_t[:], zero.to_broadcast([P, T])).then_inc(ev("m_zeroed"), 1)
                    v.wait_ge(ev("m_zeroed"), 3)
                    v.sem_inc(ev("m_y_split"), 1)
                    v.sem_inc(ev("m_choice_t"), 1)
                    gathered(0)
                    with v.Fori(0, N_EXP) as e:
                        Ahead.n = AHEAD
                        sparse_expert(e)
                    add(N_EXP)
                    v.wait_ge(ev("m_added"), N_EXP + 1)
                else:
                    wait("gates_turned")
                    v.tensor_copy(GT[0:N_EXP, :], psum[7][0:N_EXP, 0:T]).then_inc(ev("gt_ready"), 1)
                    wait("gates_spread")
                    for b in range(4):
                        v.tensor_copy(GB[:, 2 * b:2 * b + 2, :], psum[b][:, :].rearrange("p (a t) -> p a t", a=2))\
                            .then_inc(ev("d_gates"), 1)
                    v.wait_ge(ev("d_gates"), 4)
                    v.sem_inc(ev("d_added"), 1)
                    with v.Fori(0, N_EXP) as e:
                        Ahead.n = AHEAD
                        dense_expert(e)
                    v.wait_ge(ev("d_added"), N_EXP + 1)

            def log_sigmoid(x, t, out, n):
                v.scalar_tensor_tensor(t, x, -1.0, x, ALU.mult, ALU.min).then_inc(ev("abs_ready"), 1)
                wait("softplus_ready")
                link(v.scalar_tensor_tensor(out, x, 0.0, t, ALU.min, ALU.subtract))

            def attention(kind, pair_done):
                heads, n_keys = heads_and_keys(kind)
                pair = 0
                total = 2 * len(heads)

                def merged(i):
                    v.wait_ge(ev("value_done"), seen.now(ev("value_done")) + i + 1)
                    pair_done(heads[i])

                for u in range(total + 3):
                    if u < total:
                        c = u % 2
                        n = n_keys(c) * P
                        wait("scores_done")
                        src = psum[u % 2][:, 0:n]
                        if kind == "odd":
                            if u >= 2:
                                v.wait_ge(ev("exp_done"), seen.now(ev("exp_done")) + u - 1)
                            d = c * P
                            if c:
                                step(v.tensor_copy(logit[:, 1, 0:P], psum[u % 2][:, 0:P]))
                            link(v.tensor_tensor(logit[:, c, d:d + P], psum[u % 2][:, d:d + P], M("mask_add"), ALU.add))
                            src = logit[:, c, 0:n]
                        elif u >= 2:
                            v.wait_ge(ev("exp_done"), seen.now(ev("exp_done")) + u - 1)
                        v.tensor_reduce(small[:, 8 + u % 2:9 + u % 2], src, AX.X, ALU.max, negate=True).then_inc(ev("max_ready"), 1)
                    if 1 <= u <= total:
                        w = u - 1
                        n = n_keys(w % 2) * P
                        v.wait_ge(ev("exp_done"), seen.now(ev("exp_done")) + w + 1)
                        link(v.reciprocal(small[:, 12 + w % 2:13 + w % 2], small[:, 10 + w % 2:11 + w % 2]))
                        v.tensor_scalar(prob[:, w % 2, 0:n], prob[:, w % 2, 0:n], small[:, 12 + w % 2:13 + w % 2], None, ALU.mult)\
                            .then_inc(ev("prob_ready"), 1)
                    if u >= 4 and u % 2 == 0 and heads[u // 2 - 2]["last"]:
                        merged(u // 2 - 2)
                seen.next(ev("exp_done"), total)
                seen.next(ev("value_done"), len(heads))

            wait("cond_silu")
            cond = cond_s[:].unsqueeze(2).to_broadcast([P, KT, P // 2, 2])
            hi, lo = (a.rearrange("p k (r s) -> p k r s", s=2) for a in (cond_hi, cond_lo))
            link(v.tensor_copy(hi, cond))
            v.tensor_tensor(lo, cond, hi.bitcast(F32), ALU.subtract).then_inc(ev("cond_ready"), 1)
            v.wait_ge(ev("vec_in"), 16)
            for l in range(2):
                lam = V(f"lambdas{l}")
                ins = v.tensor_tensor(small[0:32, 2 * l:2 * l + 2], lam[0:32, 0:2], lam[0:32, 2:4], ALU.mult)
                if l == 1:
                    ins.then_inc(ev("lam_prod"), 1)
            split_to(RING)
            with v.Fori(0, (2 * N_ADA - RING) // RING) as i:
                for j in range(RING):
                    split_at(i * RING + (RING + j), j, True)
            nsplit[0] = 2 * N_ADA
            split_to(2 * N_ADA + AHEAD)
            wait("lam_exp")
            for l in range(2):
                link(v.tensor_tensor(neg_lam[:, l:l + 1], small[:, 4 + 2 * l + 1:6 + 2 * l], small[:, 4 + 2 * l:5 + 2 * l], ALU.subtract))
                link(v.tensor_scalar(neg_lam[:, l:l + 1], neg_lam[:, l:l + 1], -LAMBDA_INIT[l], None, ALU.add))
                link(v.tensor_scalar(g_sub[:, l:l + 1], V(f"g_sub{l}"), 1.0 - LAMBDA_INIT[l], None, ALU.mult))
                v.wait_ge(ev("ada_turned"), ADA_GROUPS)
                src = psum[7][:, l * 96:(l + 1) * 96].rearrange("p (m s) -> p m s", s=2)
                link(v.tensor_tensor(mod[:, l, :, :], src, V(f"b_ada{l}").unsqueeze(2).to_broadcast([P, N_ADA, 2]), ALU.add))

                def g(name):
                    return V(name).unsqueeze(2).to_broadcast([P, KT, 2])
                link(v.scalar_tensor_tensor(gains[:, l, 0], mod[:, l, 8:16, :], 1.0, g(f"g_attn_pre{l}"), ALU.add, ALU.mult))
                link(v.tensor_tensor(gains[:, l, 1], mod[:, l, 16:24, :], g(f"g_attn_post{l}"), ALU.mult))
                link(v.scalar_tensor_tensor(gains[:, l, 2], mod[:, l, 32:40, :], 1.0, g(f"g_ffn_pre{l}"), ALU.add, ALU.mult))
                link(v.tensor_tensor(gains[:, l, 3], mod[:, l, 40:48, :], g(f"g_ffn_post{l}"), ALU.mult))
            v.wait_ge(ev("mat_in"), 16)
            v.wait_ge(ev("ws_in"), 16)
            v.tensor_tensor(WS, WS, M("mask01").unsqueeze(1).to_broadcast([P, 4, P]), ALU.mult).then_inc(ev("ws_ready"), 1)
            norm(lat, lambda k: V("g_even_mix", k), lambda k: V("zero"))
            others_read(N_EVEN_IN)
            v.wait_ge(ev("lin_read"), nlin[0])
            for c in range(2):
                link(v.bn_stats(small[:, 32 + 6 * c:38 + 6 * c], VA[:, c, :]))
                link(v.bn_aggr(small[:, 48 + 2 * c:50 + 2 * c], small[:, 32 + 6 * c:38 + 6 * c]))
            v.tensor_copy(small[:, 16:18], small[:, 49:52:2]).then_inc(ev("var_ready"), 1)
            wait("gx_ready", 2)
            log_sigmoid(GX, QQ, GX, T)
            link(v.memset(sq[:, 0, :], 1.0))
            for t in range(2):
                for c in range(2):
                    cc = slice(c * P, (c + 1) * P)
                    step(v.tensor_tensor_scan(G[:, t, cc], sq[:, 0, cc], GX[:, t, cc], 0.0, ALU.mult, ALU.add))
            link(v.memset(small[:, 32:48], 0.0))
            ref = small[:, 32:48].rearrange("p (t c i) -> p t c i", t=2, c=2)
            for t in range(2):
                for c in range(2):
                    step(v.tensor_copy(ref[:, t, c, 1:4], G[:, t, c * P + SUB - 1:c * P + 3 * SUB:SUB]))
            settle()
            for t in range(2):
                for c in range(2):
                    g3 = G[:, t, c * P:(c + 1) * P].unsqueeze(1).to_broadcast([P, 4, P])
                    r3 = ref[:, t, c, :].unsqueeze(2).to_broadcast([P, 4, P])
                    step(v.tensor_tensor(EK[:, t, 4 * c:4 * c + 4, :], g3, r3, ALU.subtract))
            for t in range(2):
                g3 = G[:, t, :].rearrange("p (i s) -> p i s", s=SUB)
                r3 = small[:, 32 + 8 * t:40 + 8 * t].unsqueeze(2).to_broadcast([P, 8, SUB])
                step(v.tensor_tensor(QQ[:, t, :].rearrange("p (i s) -> p i s", s=SUB), g3, r3, ALU.subtract))
                step(v.tensor_scalar(KD[:, t, :], G[:, t, 0:P], G[:, t, P - 1:P], None, ALU.subtract))
            settle()
            v.tensor_scalar(EK, EK, -16.0 * CLAMP, None, ALU.max).then_inc(ev("diffs_ready"), 1)
            wait("rstd_ready")
            for c in range(2):
                step(v.tensor_scalar(VN[:, c, :], VA[:, c, :], small[:, 48 + 2 * c:49 + 2 * c], small[:, 16 + c:17 + c],
                                     ALU.subtract, ALU.mult))
            settle()
            v.wait_ge(ev("lng_in"), 16)
            v.wait_ge(ev("lnb_in"), 16)
            link(v.tensor_tensor(VN, VN, LNG.unsqueeze(1).to_broadcast([P, 2, A_W]), ALU.mult))
            v.tensor_tensor(VN, VN, LNB.unsqueeze(1).to_broadcast([P, 2, A_W]), ALU.add).then_inc(ev("vn_ready"), 1)
            wait("exps_ready", 4)
            for t in range(2):
                for c in range(2):
                    k3 = KTT[:, t, c * P:(c + 1) * P].unsqueeze(1).to_broadcast([P, 4, P])
                    step(v.tensor_tensor(EK[:, t, 4 * c:4 * c + 4, :], EK[:, t, 4 * c:4 * c + 4, :], k3, ALU.mult))
            step(v.tensor_tensor(QQ, QQ, QT, ALU.mult))
            step(v.tensor_tensor(QI, QI, QT[:, :, P:2 * P], ALU.mult))
            step(v.tensor_tensor(KD, KD, KTT[:, :, 0:P], ALU.mult))
            settle()
            v.sem_inc(ev("decays_ready"), 1)
            v.wait_ge(ev("bs_in"), 16)
            wait("spatial_done")
            for b in range(2):
                for g in range(2):
                    src = half(2 + b, g).rearrange("p (c s) -> p c s", c=2)
                    step(v.tensor_tensor(sq[:, 4 + 2 * b + g, :].rearrange("p (c s) -> p c s", c=2), src,
                                         BS[:, 2 * b + g, :].unsqueeze(1).to_broadcast([P, 2, P]), ALU.add))
            settle()
            link(v.tensor_tensor(U, U, sq[:, 4:8, :], ALU.mult))
            wait("kd_turned")
            v.tensor_copy(KDT, psum[7][:, 0:2 * P].rearrange("p (a b) -> p a b", a=2)).then_inc(ev("kdt_ready"), 1)
            wait("gla_scores")
            for par in range(2):
                ins = v.tensor_tensor(ATS[:, par], psum[par][:, :].rearrange("p (a b) -> p a b", a=4),
                                      M("mask01").unsqueeze(1).to_broadcast([P, 4, P]), ALU.mult)
            ins.then_inc(ev("ats_ready"), 1)
            wait("state_done")
            v.tensor_copy(ST, psum[6][:, 0:2 * P].rearrange("p (a b) -> p a b", a=2)).then_inc(ev("state_ready"), 1)
            wait("rs_ready")
            link(v.tensor_tensor(tmp[:, 0:4, :], tmp[:, 0:4, :], sq[:, 4:8, :], ALU.mult))
            for h in range(4):
                step(v.scalar_tensor_tensor(OG[:, h, :], tmp[:, h, :], V("head_g", h), OG[:, h, :], ALU.mult, ALU.mult))
            settle()
            for k in range(KT):
                src = U[:, k, :] if k < 4 else OG[:, k - 4, :]
                v.tensor_copy(tmp[:, k, :], src).then_inc(ev("scaled"), 1)
            for k in range(KT):
                low_part(k)
            add_linears(lat)
            norm(lat, lambda k: V("g_even_ffn", k), lambda k: V("zero"))
            ffn(FF_STEPS)

            def add_down():
                v.wait_ge(pack_used, 2 * N_ADA + npos[0])
                for b in range(4):
                    step(v.tensor_tensor(lat[:, 2 * b:2 * b + 2, :], lat[:, 2 * b:2 * b + 2, :],
                                         psum[b][:, :].rearrange("p (a t) -> p a t", a=2), ALU.add))
                settle()
                v.sem_inc(ev("x_ready"), 1)

            add_down()
            norm(lat, lambda k: V("g_odd_mix", k), lambda k: V("zero"))
            others_read(N_ODD_IN)
            wait("f_ready")
            log_sigmoid(OF[0:C_HEADS], ONC[0:C_HEADS], OF[0:C_HEADS], T)
            link(v.memset(rs[:], 1.0))
            link(v.tensor_tensor_scan(OC[0:C_HEADS], rs[0:C_HEADS, :], OF[0:C_HEADS], 0.0, ALU.mult, ALU.add))
            link(v.tensor_scalar(ONC[0:C_HEADS], OC[0:C_HEADS], -1.0, None, ALU.mult))
            wait("rs_ready")
            v.scalar_tensor_tensor(OQ, OQ, V("odd_q_g"), sq[:], ALU.mult, ALU.mult).then_inc(ev("qk_scaled"), 1)
            wait("rs_ready")
            v.scalar_tensor_tensor(OK, OK, V("odd_k_g"), sq[:], ALU.mult, ALU.mult).then_inc(ev("qk_ready"), 1)

            def odd_pair(hd):
                t = hd["tile"]
                v.tensor_tensor(tmp[:, t, :], half(hd["out"][0], 0), OO[:, t, :], ALU.mult).then_inc(ev("pair_read"), 1)

            attention("odd", odd_pair)
            v.wait_ge(ev("pair_read"), seen.next(ev("pair_read"), 8))

            def hand_on():
                for k in range(KT):
                    v.sem_inc(ev("scaled"), 1)
                for k in range(KT):
                    low_part(k)

            hand_on()
            add_linears(lat)
            norm(lat, lambda k: V("g_odd_ffn", k), lambda k: V("zero"))
            others_read(1)
            v.wait_ge(ev("lin_read"), nlin[0])
            for t in range(2):
                link(v.max(small[:, 32 + 8 * t:40 + 8 * t], RL[:, t, 0:N_EXP]))
                link(v.max_index(GATE2[:, t, :].bitcast(U32), small[:, 32 + 8 * t:40 + 8 * t], RL[:, t, 0:N_EXP]))
                link(v.tensor_copy(small[:, 16 + 2 * t:18 + 2 * t], GATE2[:, t, 0:2].bitcast(U32)))
            top = small[:, 32:48].rearrange("p (t n) -> p t n", t=2)
            v.tensor_tensor(small[:, 24:26].unsqueeze(2), top[:, :, 1:2], top[:, :, 0:1], ALU.subtract).then_inc(ev("top_diff"), 1)
            wait("top_exp")
            link(v.tensor_scalar(small[:, 26:28], small[:, 24:26], 1.0, None, ALU.add))
            link(v.reciprocal(small[:, 26:28], small[:, 26:28]))
            link(v.tensor_tensor(small[:, 28:30], small[:, 26:28], small[:, 24:26], ALU.mult))
            link(v.memset(GATE, 0.0))
            link(v.memset(SLOT, 0.0))
            for t in range(2):
                first, second = (small[:, n + 2 * t:n + 1 + 2 * t] for n in (16, 17))
                ids = M("iota")[:, 0:N_EXP]
                step(v.tensor_scalar(GATE[:, t, 0:N_EXP], ids, first, small[:, 26 + t:27 + t], ALU.is_equal, ALU.mult))
                step(v.tensor_scalar(GATE2[:, t, :], ids, second, small[:, 28 + t:29 + t], ALU.is_equal, ALU.mult))
                link(v.tensor_scalar(SEL[:, t, :], ids, first, None, ALU.is_equal))
                step(v.scalar_tensor_tensor(SEL[:, t, :], ids, second, SEL[:, t, :], ALU.is_equal, ALU.add))
            settle()
            v.sem_inc(ev("chosen"), 1)
            step(v.tensor_tensor(GATE[:, :, 0:N_EXP], GATE[:, :, 0:N_EXP], GATE2, ALU.add))
            wait("slots_counted")
            step(v.tensor_tensor(SLOT[:, :, 0:N_EXP], psum[7][:, 0:2 * N_EXP].rearrange("p (t n) -> p t n", t=2), SEL, ALU.mult))
            link(v.tensor_reduce(small[:, 53:54], psum[7][:, 2 * N_EXP:3 * N_EXP], AX.X, ALU.max))
            step(v.tensor_scalar(SLOT, SLOT, -1.0, None, ALU.add))
            link(v.tensor_copy(fullest[:, 0:1], small[:, 53:54]))
            v.sem_inc(ev("routed"), 1)
            split_to(2 * N_ADA + npos[0] + AHEAD)
            n = v.value_load(fullest[0:1, 0:1], min_val=0, max_val=T)
            with v.If(n > P):
                experts(sparse=False)
            with v.Else():
                experts(sparse=True)
            npos[0] += N_EXP * EXP_PACKS
            nsplit[0] += N_EXP * EXP_PACKS
            v.sem_inc(ev("x_ready"), 1)
            norm(lat, lambda k: V("g_final", k), out=lat)
            v.sem_inc(ev("x_ready"), 1)
            for l in range(2):
                for s, (stream, x) in enumerate((("context", con), ("latents", lat))):
                    only_kv = l == 1 and stream == "context"
                    k0 = T if stream == "context" else 0
                    col = 1 - s
                    norm(x, lambda k: gains[:, l, 0, k, col:col + 1], lambda k: mod[:, l, k, col:col + 1])
                    others_read(N_IN_KV if only_kv else N_IN)
                    wait("rs_ready")
                    step(v.scalar_tensor_tensor(tmp[:, 0, :], ZR[:, 0, :], V(f"g_mla_kv{l}"), sq[:, 0, :], ALU.mult, ALU.mult))
                    if not only_kv:
                        for k in range(2):
                            step(v.scalar_tensor_tensor(tmp[:, 1 + k, :], ZR[:, 6 + k, :], V(f"g_mla_q{l}", k), sq[:, 6, :],
                                                        ALU.mult, ALU.mult))
                    settle()
                    v.sem_inc(ev("latents_normed"), 1)
                    n = 1 if only_kv else 3
                    wait("latents_hi")
                    v.tensor_tensor(h_lo[:, 0:n, :], tmp[:, 0:n, :], h_hi[:, 0:n, :].bitcast(F32), ALU.subtract)\
                        .then_inc(ev("latent_split"), 1)
                    split_to(2 * N_ADA + npos[0] + AHEAD)
                    npos[0] += 1
                    step(v.scalar_tensor_tensor(KG[:, k0:k0 + T], ZR[:, 1, :], V(f"g_gqa_k{l}"), sq[:, 1, :], ALU.mult, ALU.mult))
                    if not only_kv:
                        step(v.scalar_tensor_tensor(QG, ZR[:, 2:6, :], V(f"g_gqa_q{l}"), sq[:, 2:6, :], ALU.mult, ALU.mult))
                        split_to(2 * N_ADA + npos[0] + AHEAD)
                        npos[0] += 1
                        wait("qm_ready", 2)
                    settle()
                    if stream == "latents":
                        v.sem_inc(ev("rope_in"), 1)
                        for n, (_, cos, sin, rows, z) in enumerate(ROPED):
                            w = z.shape[1]
                            wait("rotated")
                            src = psum[4 + n % 2][0:rows, 0:w * T].rearrange("p (a t) -> p a t", a=w)
                            t = sq[0:rows, 0:w, :]
                            v.tensor_tensor(t, src, M(sin)[0:rows].unsqueeze(1).to_broadcast([rows, w, T]), ALU.mult)\
                                .then_inc(ev("rope_out"), 1)
                            v.wait_ge(ev("rope_out"), seen.next(ev("rope_out")))
                            link(v.tensor_tensor(z, z, M(cos)[0:rows].unsqueeze(1).to_broadcast([rows, w, T]), ALU.mult))
                            link(v.tensor_tensor(z, z, t, ALU.add))
                    wait("km_ready", 3)
                    link(v.tensor_copy(KM[64:MLA_QK, :, k0:k0 + T], KPE[64:MLA_QK].unsqueeze(1).to_broadcast([32, 4, T])))
                    if only_kv:
                        v.sem_inc(ev("context_keys_ready"), 1)
                        continue
                    v.sem_inc(ev("qk_ready"), 1)

                    def pair(hd):
                        t, b = hd["tile"], hd["out"][0]
                        if hd["kind"] == "diff":
                            link(v.tensor_scalar(sq[:, 4 + t, :], half(b, 1), neg_lam[:, l:l + 1], None, ALU.mult))
                            v.tensor_tensor(tmp[:, t, :], half(b, 0), sq[:, 4 + t, :], ALU.add).then_inc(ev("pair_read"), 1)
                        else:
                            v.tensor_copy(tmp[:, t, :], half(b, 0)).then_inc(ev("pair_read"), 1)

                    attention(stream, pair)
                    v.wait_ge(ev("pair_read"), seen.next(ev("pair_read"), 8))
                    v.sem_inc(ev("diff_ready"), 1)
                    wait("rs_ready")
                    link(v.scalar_tensor_tensor(tmp[:, 2:4, :], tmp[:, 2:4, :], g_sub[:, l:l + 1], sq[:, 2:4, :], ALU.mult, ALU.mult))
                    hand_on()
                    others_read(KT)

                    def post(which):
                        norm(ZR, lambda k: gains[:, l, which, k, col:col + 1])
                        link(v.tensor_tensor(x[:], x[:], tmp[:], ALU.add))
                        v.sem_inc(ev("x_ready"), 1)
                    post(1)
                    norm(x, lambda k: gains[:, l, 2, k, col:col + 1], lambda k: mod[:, l, 24 + k, col:col + 1])
                    ffn(FF_STEPS)
                    post(3)
            v.sem_inc(ev("out_ready"), 1)


def _column_packs(w):
    k, n = w.shape
    pad = -n % P
    if pad:
        w = np.concatenate([w, np.zeros((k, pad), w.dtype)], axis=1)
    return w.reshape(KT, P, -1, P).transpose(2, 1, 0, 3).reshape(-1, P, PACK)


def _wide_packs(w):
    return w.reshape(4, 2, P, -1, 512).transpose(3, 0, 2, 1, 4).reshape(-1, P, PACK)


def _fill_ffn(out, w1, w3, w2):
    n = w2.shape[0] // P
    for w, a in enumerate((w1, w3)):
        packs = _column_packs(a)
        for s in range(n):
            out[w if s == 0 else 3 * s - 1 + w] = packs[s]
    for s in range(n):
        out[3 * s + 4 if s < n - 1 else 3 * n - 1] = w2[s * P:(s + 1) * P]


def _fill_expert(out, w1, w3, w2):
    ups = [_wide_packs(a) for a in (w1, w3)]
    rows = w2.reshape(-1, P, D)
    for g in range(GROUPS):
        at = 0 if g == 0 else 12 * g - 4
        for w in range(2):
            out[at + 4 * w:at + 4 * w + 4] = ups[w][4 * g:4 * g + 4]
        down = 12 * g + 16 if g < GROUPS - 1 else EXP_PACKS - 4
        out[down:down + 4] = rows[4 * g:4 * g + 4]


def _weight_packs(a):
    packs = np.zeros((N_PACKS, P, PACK), np.float32)

    def put(name, values):
        packs[START[name]:START[name] + values.shape[0]] = values

    for l in range(2):
        put(f"ada{l}", _wide_packs(a["w_ada_2"][l]))
    w = a["even_w_in"][0]
    u, v, q, k, g, vb, og = np.split(w, np.cumsum([A_W, A_W, B_QK, B_QK, RANK, B_V])[:6], axis=1)
    put("even_in", np.concatenate([_column_packs(x) for x in (g, q, k, vb, v, u, og)]))
    put("even_o", _column_packs(a["even_w_o"][0]))
    w = a["odd_w_in"][0]
    q, k, v, og, f = np.split(w, [D, 2 * D, 3 * D, 4 * D], axis=1)
    put("odd_in", np.concatenate([_column_packs(x) for x in (f, q, k, v, og)]))
    put("odd_o", _column_packs(a["odd_w_o"][0]))
    put("router", _column_packs(a["odd_router"][0]))

    def ffn(name, w1, w3, w2):
        _fill_ffn(packs[START[name]:START[name] + COUNT[name]], w1, w3, w2)

    ffn("even_ffn", a["even_ffn_w1"][0], a["even_ffn_w3"][0], a["even_ffn_w2"][0])
    for e in range(N_EXP):
        _fill_expert(packs[START["moe"] + e * EXP_PACKS:START["moe"] + (e + 1) * EXP_PACKS],
                     a["odd_exp_w1"][0, e], a["odd_exp_w3"][0, e], a["odd_exp_w2"][0, e])
    for l in range(2):
        w = a["w_in_2"][l]
        qa, kva, dq, dk, dv, gq, gk, gv = np.split(w, np.cumsum([256, 160, 256, 256, 256, 512, 128])[:7], axis=1)
        ckv, kpe = kva[:, :128], kva[:, 128:]
        kpe = np.concatenate([np.zeros((D, 64), w.dtype), kpe], axis=1)
        gq = gq.reshape(D, 2, 4, 64).transpose(0, 2, 1, 3).reshape(D, 512)
        put(f"in{l}", np.concatenate([_column_packs(x) for x in (ckv, kpe, dk, gk, dv, gv, qa, dq, gq)]))
        packs[START[f"kvb{l}"], :, 0:512] = a["w_mla_kvb_2"][l]
        qb = a["w_mla_qb_2"][l].reshape(2, P, 4, MLA_QK).transpose(1, 2, 0, 3)
        packs[START[f"qb{l}"]].reshape(P, 4, 2, P)[..., 0:MLA_QK] = qb
        put(f"out{l}", _column_packs(a["w_out_2"][l]))
        ffn(f"ffn{l}", a["w_ffn_gate_2"][l], a["w_ffn_up_2"][l], a["w_ffn_down_2"][l])
    return packs


def _vectors(a):
    vec = np.zeros((P, N_VEC), np.float32)

    def put(name, values):
        at, n = VEC[name]
        values = np.asarray(values).reshape(-1)
        rows = values.size // n
        vec[0:rows, at:at + n] = values.reshape(n, rows).T

    vec[:, VEC["one"][0]] = 1.0
    vec[:, VEC["eps"][0]] = EPS
    vec[:, VEC["eps64"][0]] = 64 * EPS
    put("g_even_mix", a["even_norm_mix"][0])
    put("g_even_ffn", a["even_norm_ffn"][0])
    put("g_odd_mix", a["odd_norm_mix"][0])
    put("g_odd_ffn", a["odd_norm_ffn"][0])
    put("g_final", a["final_norm"])
    put("head_g", a["even_head_g"][0])
    put("gate_bias", a["even_gate_bias"][0])
    put("odd_q_g", np.tile(a["odd_q_g"][0], 2))
    put("odd_k_g", np.tile(a["odd_k_g"][0], 2))
    put("forget_bias", a["odd_forget_bias"][0])
    put("cond", np.stack([a["c_2"][0], a["c_ctx_2"]]).reshape(2, KT, P).transpose(1, 0, 2))
    for l in range(2):
        for name, key in (("g_attn_pre", "g_attn_pre_2"), ("g_attn_post", "g_attn_post_2"), ("g_ffn_pre", "g_ffn_pre_2"),
                          ("g_ffn_post", "g_ffn_post_2"), ("b_ada", "b_ada_2"), ("g_mla_q", "g_mla_q_2"), ("g_mla_kv", "g_mla_kv_2")):
            put(f"{name}{l}", a[key][l])
        for name, key in (("g_gqa_q", "g_gqa_q_2"), ("g_gqa_k", "g_gqa_k_2"), ("g_sub", "g_diff_sub_2")):
            put(f"{name}{l}", np.tile(a[key][l], 2))
        put(f"lambdas{l}", np.stack([a[f"lambda_{n}_2"][l] for n in ("q1", "q2", "k1", "k2")]))
    return vec


def _matrices():
    mat = np.zeros((P, N_MAT), np.float32)

    def put(name, values):
        at, n = MAT[name]
        mat[0:values.shape[0], at:at + values.shape[1]] = values

    r = np.arange(P)
    put("ident", np.eye(P))
    put("ones", np.ones((P, P)))
    put("block64", (r[:, None] // 64 == r[None, :] // 64).astype(np.float32))
    put("mask01", (r[:, None] <= r[None, :]).astype(np.float32))
    put("mask_add", np.where(r[None, :] <= r[:, None], 0.0, -1e30))
    token = np.arange(T)
    for name, dim, first in (("mla", 32, 64), ("diff", 32, 0), ("gqa", 64, 0)):
        h = dim // 2
        rot = np.zeros((P, P))
        quarter = dim // 4
        inv = (np.float32(ROPE_THETA) ** (-np.arange(quarter, dtype=np.float32) / np.float32(quarter))).astype(np.float32)
        row, col = (token // GRID_W).astype(np.float32), (token % GRID_W).astype(np.float32)
        angle = np.concatenate([row[:, None] * inv, col[:, None] * inv], axis=1).T
        cos, sin = np.ones((P, T)), np.zeros((P, T))
        for b in range(first, MLA_QK if name == "mla" else P, dim):
            for i in range(h):
                rot[b + h + i, b + i] = -1.0
                rot[b + i, b + h + i] = 1.0
            cos[b:b + h] = cos[b + h:b + dim] = np.cos(angle)
            sin[b:b + h] = sin[b + h:b + dim] = np.sin(angle)
        put("rot_" + name, rot)
        put("cos_" + name, cos)
        put("sin_" + name, sin)
    pick = np.zeros((N_EXP, N_EXP * P))
    for e in range(N_EXP):
        pick[e, e * P:(e + 1) * P] = 1.0
    put("pick", pick)
    put("iota", np.tile(np.arange(P), (P, 1)))
    put("head_id", np.eye(C_HEADS))
    return mat


def _feature_major(x):
    return np.ascontiguousarray(x.T.reshape(KT, P, T).transpose(1, 0, 2)).reshape(P, KT * T)


def kernel(**inputs):
    import concourse.bacc as bacc
    from concourse.bass_utils import run_bass_kernel_spmd

    a = {k: np.asarray(v) for k, v in inputs.items()}
    arrays = {
        "w_packs": _weight_packs(a),
        "vecs": _vectors(a),
        "mats": _matrices(),
        "x_t": _feature_major(a["x"][0]),
        "ctx_t": _feature_major(a["ctx_2"][0]),
        "w_s_t": np.ascontiguousarray(a["even_w_s"][0].transpose(2, 0, 1)).reshape(P, 4 * P),
        "b_s_row": np.ascontiguousarray(a["even_b_s"][0]).reshape(4 * P),
        "ln_g_row": np.ascontiguousarray(a["even_ln_g"][0]),
        "ln_b_row": np.ascontiguousarray(a["even_ln_b"][0]),
        "gate_up": np.ascontiguousarray(a["even_gate_up"][0]),
    }
    nc = bacc.Bacc("TRN2", target_bir_lowering=False, num_devices=1)
    args = [nc.dram_tensor(n, x.shape, F32, kind="ExternalInput").ap() for n, x in arrays.items()]
    out = nc.dram_tensor("out_t", (P, KT * T), F32, kind="ExternalOutput").ap()
    build(nc, *args, out)
    r = run_bass_kernel_spmd(nc, [arrays], core_ids=[0])
    y = r.results[0]["out_t"].reshape(P, KT, T).transpose(1, 0, 2).reshape(D, T).T
    return np.ascontiguousarray(y)[None]
```

```python
from contextlib import ExitStack

import numpy as np

import concourse.bass as bass
from concourse import mybir

ALU = mybir.AluOpType
ACT = mybir.ActivationFunctionType
AX = mybir.AxisListType
F32 = mybir.dt.float32
F32R = mybir.dt.float32r
U32 = mybir.dt.uint32
I32 = mybir.dt.int32

P = 128
D = 1024
KT = D // P
T = 256
CHUNK = 128
EPS = 1e-6
PACK = KT * P

A_W, B_QK, B_V, RANK = 512, 256, 512, 16
CLAMP = 70.0
SUB = 32
C_HEADS = 16
FF = 2816
FF_STEPS = FF // P
N_EXP, FF_EXP = 8, 3584
WIDE = 512
GROUPS = FF_EXP // WIDE
EXP_PACKS = 12 * GROUPS

GRID_W = 64
ROPE_THETA = 10000.0
MLA_QK = 96
MLA_SCALE = 96.0 ** -0.5
DIFF_SCALE = 32.0 ** -0.5
LAMBDA_INIT = [0.8 - 0.6 * float(np.exp(-0.3 * l)) for l in range(2)]

RING = 6
AHEAD = 5

N_EVEN_IN, N_ODD_IN, N_IN, N_IN_KV, N_ADA = 21, 33, 17, 9, 48
SECTIONS = [("ada0", N_ADA), ("ada1", N_ADA), ("even_in", N_EVEN_IN), ("even_o", 8), ("even_ffn", 3 * FF_STEPS),
            ("odd_in", N_ODD_IN), ("odd_o", 8), ("router", 1), ("moe", N_EXP * EXP_PACKS)]
for _l in range(2):
    SECTIONS += [(f"in{_l}", N_IN), (f"kvb{_l}", 1), (f"qb{_l}", 1), (f"out{_l}", 8), (f"ffn{_l}", 3 * FF_STEPS)]
START, _n = {}, 0
for _name, _count in SECTIONS:
    START[_name] = _n
    _n += _count
N_PACKS = _n
ADA_GROUPS = 2 * N_ADA // 4
COUNT = dict(SECTIONS)


def stream_order():
    def all_of(*names):
        return [(START[n], COUNT[n]) for n in names]
    order = all_of("ada0", "ada1", "even_in", "even_o", "even_ffn", "odd_in", "odd_o", "router", "moe")
    for _ in ("context", "latents"):
        order += all_of("in0", "kvb0", "qb0", "out0", "ffn0")
    order += [(START["in1"] + first, count) for first, count in ((0, 2), (8, 3), (13, 4))] + [(START["kvb1"], 1)]
    order += all_of("in1", "kvb1", "qb1", "out1", "ffn1")
    merged = []
    for s, n in order:
        if merged and sum(merged[-1]) == s:
            merged[-1] = (merged[-1][0], merged[-1][1] + n)
        else:
            merged.append((s, n))
    return merged


TOTAL = sum(n for _, n in stream_order())

VEC = {}
_n = 0
for _name, _count in ([("zero", 1), ("one", 1), ("eps", 1), ("eps64", 1),
                       ("g_even_mix", 8), ("g_even_ffn", 8), ("g_odd_mix", 8), ("g_odd_ffn", 8), ("g_final", 8),
                       ("head_g", 4), ("gate_bias", 2), ("odd_q_g", 1), ("odd_k_g", 1), ("forget_bias", 1),
                       ("cond", 16)]
                      + [(f"{n}{l}", c) for l in range(2) for n, c in
                         (("g_attn_pre", 8), ("g_attn_post", 8), ("g_ffn_pre", 8), ("g_ffn_post", 8), ("b_ada", 48),
                          ("g_mla_q", 2), ("g_mla_kv", 1), ("g_gqa_q", 1), ("g_gqa_k", 1), ("g_sub", 1),
                          ("lambdas", 4))]):
    VEC[_name] = (_n, _count)
    _n += _count
N_VEC = _n

MAT = {}
_n = 0
for _name, _count in [("ident", P), ("ones", P), ("block64", P), ("mask01", P), ("mask_add", P),
                      ("rot_mla", P), ("rot_diff", P), ("rot_gqa", P),
                      ("cos_mla", T), ("sin_mla", T), ("cos_diff", T), ("sin_diff", T), ("cos_gqa", T),
                      ("sin_gqa", T), ("pick", N_EXP * P), ("iota", P), ("head_id", C_HEADS)]:
    MAT[_name] = (_n, _count)
    _n += _count
N_MAT = _n


class Seen:

    def __init__(self):
        self.count = {}

    def next(self, sem, n=1):
        self.count[sem.name] = self.count.get(sem.name, 0) + n
        return self.count[sem.name]

    def now(self, sem):
        return self.count.get(sem.name, 0)


def build(nc, w_packs, vecs, mats, x_t, ctx_t, w_s_t, b_s_row, ln_g_row, ln_b_row, gate_up, out_t):
    with ExitStack() as stack:
        def sb(name, shape, dt=F32):
            return stack.enter_context(nc.sbuf_tensor(name, shape, dt))

        made = {}

        def ev(name):
            if name not in made:
                made[name] = stack.enter_context(nc.semaphore(name))
            return made[name]

        raw = sb("raw", [P, RING, PACK])
        w_hi = sb("w_hi", [P, RING, PACK], F32R)
        w_lo = sb("w_lo", [P, RING, PACK], F32R)
        lat = sb("lat", [P, KT, T])
        con = sb("con", [P, KT, T])
        h_hi = sb("h_hi", [P, KT, T], F32R)
        h_lo = sb("h_lo", [P, KT, T], F32R)
        tmp = sb("tmp", [P, KT, T])
        sq = sb("sq", [P, KT, T])
        vec = sb("vec", [P, N_VEC])
        mat = sb("mat", [P, N_MAT])
        rs2 = sb("rs", [P, 2, T])
        prob = sb("prob", [P, 2, 512])
        prob_t = sb("prob_t", [P, 2, 4 * T])
        logit_sg = sb("logit_sg_prod", [P, 6 * T])
        logit, sg, prod = (logit_sg[:, n * 2 * T:(n + 1) * 2 * T].rearrange("p (a t) -> p a t", t=T) for n in range(3))
        f_hi = sb("f_hi", [P, 2, T], F32R)
        f_lo = sb("f_lo", [P, 2, T], F32R)
        mod = sb("mod", [P, 2, N_ADA, 2])
        gains = sb("gains", [P, 2, 4, KT, 2])
        small = sb("small", [P, 64])
        cond_s = sb("cond_s", [P, KT, 2])
        ada_rows = logit_sg[0:2, :].rearrange("p (g c) -> p g c", c=512)
        neg_lam = sb("neg_lam", [P, 2])
        g_sub = sb("g_sub", [P, 2])
        choice_t = sb("choice_t", [P, T], F32R)
        fullest = sb("fullest", [P, 2], I32)
        arena = sb("arena", [P, 11264])

        def V(name, j=None):
            a, n = VEC[name]
            return vec[:, a:a + n] if j is None else vec[:, a + j:a + j + 1]

        def M(name):
            a, n = MAT[name]
            return mat[:, a:a + n]

        at = [0]

        def part(*shape, start=None):
            if start is not None:
                at[0] = start
            n = int(np.prod(shape))
            a = arena[:, at[0]:at[0] + n]
            at[0] += n
            assert at[0] <= 11264
            if len(shape) == 2:
                a = a.rearrange("p (a b) -> p a b", b=shape[1])
            if len(shape) == 3:
                a = a.rearrange("p (a b c) -> p a b c", b=shape[1], c=shape[2])
            return a

        cond_hi, cond_lo = (h[:].rearrange("p k t -> p (k t)")[:, 0:KT * P].rearrange("p (k m) -> p k m", m=P)
                            for h in (h_hi, h_lo))
        U = part(4, T, start=0)
        VA = part(2, A_W)
        VN = part(2, A_W)
        QT = part(2, T)
        KTT = part(2, T)
        VB = part(2, B_V)
        OG = part(4, T)
        G = part(2, T)
        GX = part(2, T)
        EK = part(2, 8, P)
        QQ = part(2, T)
        QI = part(2, P)
        KD = part(2, P)
        WS = part(4, P)
        BS = part(4, P)
        LNG, LNB = prob_t[:, 0, 0:A_W], prob_t[:, 0, A_W:2 * A_W]
        ATS = prob_t[:, 1, :].rearrange("p (a b c) -> p a b c", a=2, b=4)
        KDT = prob[:, 0, 0:2 * P].rearrange("p (a b) -> p a b", a=2)
        ST = prob[:, 0, 2 * P:4 * P].rearrange("p (a b) -> p a b", a=2)
        GUP = prob[0:RANK, 1, 0:B_QK]
        GLR = logit[:, 0, :]
        OQ = part(8, T, start=0)
        OK = part(8, T)
        OV = part(2, D)
        OO = part(8, T)
        OC = part(T)
        ONC = part(T)
        OF = part(T)
        OCT = part(2, C_HEADS)
        GB = part(8, T, start=0)
        RL = part(2, N_EXP, start=2048)
        RLT = part(T)
        GATE = part(2, N_EXP + 1)
        SLOT = part(2, N_EXP + 1)
        SEL = part(2, N_EXP)
        GATE2 = part(2, N_EXP)
        GT = part(T)
        HT = part(2, D)
        CHOICE = part(2, P)
        CUR_SLOT, CUR_GATE = small[:, 48:50], small[:, 50:52]
        SLOT_GATE = small[:, 52:53]
        KM = part(4, 2 * T, start=0)
        KD2 = part(2, 2 * T)
        KG = part(2 * T)
        VM = part(4, 256)
        VD = part(4, 256)
        VG = part(4, 128)
        QM = part(4, T)
        QD = part(2, T)
        QG = part(4, T)
        ZR = part(8, T)
        KPE = part(T)

        psum = [stack.enter_context(nc.psum_tensor(f"bank{b}", [P, 512], F32)) for b in range(8)]

        def half(b, j):
            return psum[b][:, j * T:(j + 1) * T]

        SG_WIDE = sg.rearrange("p a t -> p (a t)")
        PROD_WIDE = prod.rearrange("p a t -> p (a t)")
        F_HI, F_LO = (f[:].rearrange("p a t -> p (a t)").rearrange("p (j s) -> p j s", s=P) for f in (f_hi, f_lo))
        X_HI, X_LO = h_hi[:, :, 0:P], h_lo[:, :, 0:P]
        Y_HI, Y_LO = h_hi[:, :, P:2 * P], h_lo[:, :, P:2 * P]
        SCATTER_BANKS = (5, 6, 7, 4)

        def group_at(g):
            return 0 if g == 0 else 12 * g - 4

        MIXED_ORDER = (0, 1, 4, 5, 6, 7, 2, 3)
        BEFORE_ROOT = 3

        SCORE_BANKS = (0, 1, 4, 5)
        PROBS = [prob[:, 0, :], prob[:, 1, :]] + [sq[:, n:n + 2, :].rearrange("p a t -> p (a t)") for n in (0, 2)]
        NEG_MAX, SUM, RECIP = ([small[:, n + j:n + j + 1] for j in range(4)] for n in (8, 12, 56))

        raw_in = [ev(f"raw_in{j}") for j in range(RING)]
        hi_done, lo_done, pack_used = ev("hi_done"), ev("lo_done"), ev("pack_used")

        block = stack.enter_context(nc.Block())

        def odd_heads():
            return [dict(h=h, row=64 * (h % 2), k=64, q=lambda c, h=h: OQ[64 * (h % 2):64 * (h % 2) + 64, h // 2, c * P:(c + 1) * P],
                         keys=lambda n, h=h: OK[64 * (h % 2):64 * (h % 2) + 64, h // 2, 0:n],
                         v=lambda s, h=h: OV[:, s, h * 64:(h + 1) * 64],
                         out=(6 + (h // 2) % 2, 64 * (h % 2), 0), last=h % 2 == 1, tile=h // 2) for h in range(C_HEADS)]

        def block2_heads(k0, n_tiles):
            t0 = k0 // P
            kk = slice(k0, k0 + n_tiles * P)
            heads = []
            for h in range(4):
                heads.append(dict(q=lambda c, h=h: QM[0:MLA_QK, h, c * P:(c + 1) * P], keys=lambda n, h=h: KM[0:MLA_QK, h, kk],
                                  v=lambda s, h=h: VM[:, t0 + s, h * 64:(h + 1) * 64],
                                  out=(6 + (h // 2) % 2, 64 * (h % 2), 0), last=h % 2 == 1, tile=h // 2, kind="mla"))
            for pair in range(2):
                for j in (2 * pair, 2 * pair + 1):
                    for w in range(2):
                        h = 2 * j + w
                        r = 32 * (h % 4)
                        heads.append(dict(q=lambda c, h=h, r=r: QD[r:r + 32, h // 4, c * P:(c + 1) * P],
                                          keys=lambda n, h=h, r=r: KD2[r:r + 32, h // 4, kk],
                                          v=lambda s, j=j: VD[:, t0 + s, j * 64:(j + 1) * 64],
                                          out=(6 + pair, 64 * (j % 2), w), last=j % 2 == 1 and w == 1, tile=2 + pair,
                                          kind="diff"))
            for h in range(8):
                r = 64 * (h // 4)
                heads.append(dict(q=lambda c, h=h, r=r: QG[r:r + 64, h % 4, c * P:(c + 1) * P],
                                  keys=lambda n, r=r: KG[r:r + 64, kk],
                                  v=lambda s, h=h: VG[:, t0 + s, (h // 4) * 64:(h // 4) * 64 + 64],
                                  out=(6 + (h // 2) % 2, 64 * (h % 2), 0), last=h % 2 == 1, tile=4 + h // 2, kind="gqa"))
            return heads

        def heads_and_keys(kind):
            if kind == "odd":
                return odd_heads(), lambda c: c + 1
            if kind == "context":
                return block2_heads(T, 2), lambda c: 2
            return block2_heads(0, 4), lambda c: 4

        ROPED = [("rot_gqa", "cos_gqa", "sin_gqa", P, QG[:, 0:2, :]),
                 ("rot_gqa", "cos_gqa", "sin_gqa", P, QG[:, 2:4, :]),
                 ("rot_gqa", "cos_gqa", "sin_gqa", P, KG[:, 0:T].unsqueeze(1)),
                 ("rot_diff", "cos_diff", "sin_diff", P, QD),
                 ("rot_diff", "cos_diff", "sin_diff", P, KD2[:, :, 0:T]),
                 ("rot_mla", "cos_mla", "sin_mla", MLA_QK, KPE[0:MLA_QK].unsqueeze(1)),
                 ("rot_mla", "cos_mla", "sin_mla", MLA_QK, QM[0:MLA_QK, 0:2, :]),
                 ("rot_mla", "cos_mla", "sin_mla", MLA_QK, QM[0:MLA_QK, 2:4, :])]

        @block.sync
        def _(sp):
            sp.dma_start(vec[:], vecs).then_inc(ev("vec_in"), 16)
            n = 0

            def load(c, it, slot, wait):
                if wait:
                    sp.wait_ge(lo_done, c)
                sp.dma_start(raw[:, slot, :], w_packs[it]).then_inc(raw_in[slot], 16)

            def others(n):
                if n == RING:
                    sp.dma_start(mat[:, 0:P], mats[:, 0:P]).then_inc(ev("ident_in"), 16)
                if n == AFTER_ADA:
                    sp.dma_start(lat[:].rearrange("p k t -> p (k t)"), x_t).then_inc(ev("lat_in"), 16)
                    sp.dma_start(mat[:, P:N_MAT], mats[:, P:N_MAT]).then_inc(ev("mat_in"), 16)
                    sp.dma_start(WS.rearrange("p a b -> p (a b)"), w_s_t).then_inc(ev("ws_in"), 16)
                    sp.dma_start(BS.rearrange("p a b -> p (a b)"), b_s_row.partition_broadcast(P)).then_inc(ev("bs_in"), 16)
                    sp.dma_start(LNG, ln_g_row.partition_broadcast(P)).then_inc(ev("lng_in"), 16)
                    sp.dma_start(LNB, ln_b_row.partition_broadcast(P)).then_inc(ev("lnb_in"), 16)
                    sp.dma_start(GUP, gate_up).then_inc(ev("gup_in"), 16)
                if n == LATER:
                    sp.dma_start(con[:].rearrange("p k t -> p (k t)"), ctx_t).then_inc(ev("con_in"), 16)

            AFTER_ADA, LATER = 2 * N_ADA + RING, 2 * N_ADA + 12 * RING
            for first, count in stream_order():
                done = 0
                while done < count:
                    room = min([count - done] + [m - n for m in (AFTER_ADA, LATER) if m > n])
                    loops = room // RING
                    if n >= RING and loops > 1:
                        with sp.Fori(0, loops) as i:
                            for j in range(RING):
                                load(i * RING + (n + j - RING + 1), i * RING + (first + done + j), (n + j) % RING, True)
                        n += loops * RING
                        done += loops * RING
                    else:
                        load(n - RING + 1, first + done, n % RING, n >= RING)
                        n += 1
                        done += 1
                    others(n)
            assert n == TOTAL
            sp.wait_ge(ev("out_ready"), 1)
            sp.dma_start(out_t, lat[:].rearrange("p k t -> p (k t)")).then_inc(ev("stored"), 16)
            sp.wait_ge(ev("stored"), 16)

        @block.tensor
        def _(pe):
            seen = Seen()
            pos = [0]
            lin = [0]
            wide = [0]

            def mm3(out, a_hi, a_lo, first, last, w_slot, cols, swap=False, check=False):
                hi, lo = w_hi[:, w_slot, cols], w_lo[:, w_slot, cols]
                for n, (x, y) in enumerate(((hi, a_hi), (hi, a_lo), (lo, a_hi))):
                    if swap:
                        x, y = y, x
                    ins = pe.matmul(out, x, y, start=first and n == 0, stop=last and n == 2, skip_group_check=check)
                return ins

            def linear(order=range(KT)):
                s = pos[0] % RING
                pe.wait_ge(lo_done, pos[0] + 1)
                if lin[0] >= 2:
                    pe.wait_ge(ev("lin_read"), lin[0] - 1)
                b = 4 + lin[0] % 2
                for n, k in enumerate(order):
                    input_tile(n)
                    ins = mm3(half(b, 0), h_hi[:, k, :], h_lo[:, k, :], n == 0, n == KT - 1, s, slice(k * P, (k + 1) * P))
                ins.then_inc(pack_used, 1)
                pos[0] += 1
                lin[0] += 1

            def linear_tokens(bank, width=512):
                for q in range(4):
                    s = pos[0] % RING
                    pe.wait_ge(lo_done, pos[0] + 1)
                    for j in range(2):
                        k = 2 * q + j
                        for tk in range(2):
                            tt = slice(tk * P, (tk + 1) * P)
                            ins = mm3(psum[bank + tk][:, 0:width], h_hi[:, k, tt], h_lo[:, k, tt], k == 0, k == KT - 1, s,
                                      slice(j * 512, j * 512 + width), swap=True)
                    ins.then_inc(pack_used, 1)
                    pos[0] += 1
                wide[0] += 2

            def lin_all_read():
                pe.wait_ge(ev("lin_read"), lin[0])
                if wide[0]:
                    pe.wait_ge(ev("wide_read"), wide[0])

            def norm_pair(n):
                for k in (2 * n, 2 * n + 1):
                    ins = pe.matmul(half(6, 0), M("ones"), sq[:, k, :], start=k == 0, stop=k == KT - 1)
                if n == 3:
                    ins.then_inc(ev("sum_ready"), 1)

            def norm_sum():
                for n in range(4):
                    pe.wait_ge(ev("squares"), seen.next(ev("squares")))
                    norm_pair(n)

            def out_linears(added, order=range(KT)):
                base = lin[0]

                def pair(n):
                    if added:
                        pe.wait_ge(ev("squares"), seen.next(ev("squares")))
                    else:
                        pe.wait_ge(ev("lin_read"), base + 2 * n + 2)
                    norm_pair(n)

                for m in range(KT):
                    linear(order)
                    if m in (3, 5, 7):
                        pair((m - 3) // 2)
                pair(3)

            fresh = [None]

            def input_comes():
                fresh[0] = seen.next(ev("h_ready"), KT) - KT

            def input_tile(k):
                if fresh[0] is not None:
                    pe.wait_ge(ev("h_ready"), fresh[0] + k + 1)
                    if k == KT - 1:
                        fresh[0] = None

            def ffn(steps):
                base = pos[0]
                up_base = seen.now(ev("act_ready"))

                def up(s, par, p):
                    if not isinstance(s, int) or up_base + s >= 2:
                        pe.wait_ge(ev("act_ready"), up_base + s - 1)
                    for w in range(2):
                        pe.wait_ge(lo_done, p + w + 1)
                        slot = (base + (3 * par[1] - 1 if par[1] else 0) + w) % RING
                        for k in range(KT):
                            input_tile(k)
                            ins = mm3(half(4 + par[0], w), h_hi[:, k, :], h_lo[:, k, :], k == 0, k == KT - 1,
                                      slot, slice(k * P, (k + 1) * P))
                        ins.then_inc(pack_used, 1)

                def down(s, par, p, first=False, last=False):
                    pe.wait_ge(lo_done, p + 1)
                    pe.wait_ge(ev("act_ready"), up_base + s + 1)
                    slot = (base + par[1]) % RING
                    for m in range(KT):
                        ins = mm3(half(m // 2, m % 2), f_hi[:, par[0], :], f_lo[:, par[0], :],
                                  first and m % 2 == 0, last, slot, slice(m * P, (m + 1) * P), check=True)
                        if last and m in (1, 3, 5):
                            ins.then_inc(ev("bank_down"), 1)
                    ins.then_inc(pack_used, 1)

                up(0, (0, 0), base)
                up(1, (1, 1), base + 2)
                down(0, (0, 4), base + 4, first=True)
                assert (steps - 2) % 2 == 0
                with pe.Fori(0, (steps - 2) // 2) as i:
                    for j in range(2):
                        up(i * 2 + (2 + j), (j, 2 + j), i * 6 + (base + 5 + 3 * j))
                        down(i * 2 + (1 + j), ((1 + j) % 2, 7 + 3 * j), i * 6 + (base + 7 + 3 * j))
                down(steps - 1, ((steps - 1) % 2, 3 * steps - 1), base + 3 * steps - 1, last=True)
                pos[0] = base + 3 * steps
                seen.next(ev("act_ready"), steps)

            def attention(kind):
                heads, n_keys = heads_and_keys(kind)
                units = [(i, c) for i in range(len(heads)) for c in range(2)]
                lin_all_read()
                pe.wait_ge(ev("qk_ready"), seen.next(ev("qk_ready")))

                def scores(u):
                    i, c = units[u]
                    hd, n = heads[i], n_keys(c) * P
                    if u >= 4:
                        pe.wait_ge(ev("exp_done"), seen.now(ev("exp_done")) + u - 3)
                    out = psum[SCORE_BANKS[u % 4]][:, 0:n]
                    if kind == "odd":
                        hh = hd["h"]
                        pick = M("head_id")[0:C_HEADS, hh:hh + 1]
                        pe.matmul(out, hd["q"](c), hd["keys"](n), start=True, stop=False)
                        pe.matmul(out, pick.to_broadcast([C_HEADS, P]), ONC[0:C_HEADS, 0:n], start=False, stop=True)\
                          .then_inc(ev("scores_done"), 1)
                    else:
                        pe.matmul(out, hd["q"](c), hd["keys"](n), start=True, stop=True).then_inc(ev("scores_done"), 1)

                def turn(u):
                    i, c = units[u]
                    pe.wait_ge(ev("prob_ready"), seen.now(ev("prob_ready")) + u + 1)
                    if u >= 2:
                        pe.wait_ge(ev("prob_t_ready"), seen.now(ev("prob_t_ready")) + u - 1)
                    for s in range(n_keys(c)):
                        ins = pe.transpose(psum[2 + u % 2][:, s * P:(s + 1) * P], PROBS[u % 4][:, s * P:(s + 1) * P], M("ident"))
                    ins.then_inc(ev("turned"), 1)

                def values(i):
                    hd = heads[i]
                    bank, row, w = hd["out"]
                    pe.wait_ge(ev("prob_t_ready"), seen.now(ev("prob_t_ready")) + 2 * i + 2)
                    pair = sum(h["last"] for h in heads[:i])
                    if pair >= 2:
                        pe.wait_ge(ev("pair_read"), seen.now(ev("pair_read")) + pair - 1)
                    pt = prob_t[:, i % 2, :].rearrange("p (s t) -> p s t", t=T)
                    ns = n_keys(1)
                    for s in range(ns):
                        c0 = 0 if n_keys(0) > s else 1
                        ins = pe.matmul(psum[bank][row:row + 64, w * T + c0 * P:(w + 1) * T], hd["v"](s), pt[:, s, c0 * P:T],
                                        start=s == 0, stop=s == ns - 1)
                    ins.then_inc(ev("value_done"), 1)

                for u in range(3):
                    scores(u)
                for u in range(len(units)):
                    if u + 3 < len(units):
                        scores(u + 3)
                    turn(u)
                    if u % 2 == 0 and u >= 2:
                        values(u // 2 - 1)
                values(len(heads) - 1)
                seen.next(ev("exp_done"), len(units))
                seen.next(ev("prob_ready"), len(units))
                seen.next(ev("prob_t_ready"), len(units))
                seen.next(ev("pair_read"), sum(h["last"] for h in heads))

            def sparse_experts(base):
                def up(bank, p, at):
                    for q in range(4):
                        pe.wait_ge(lo_done, p + (q + 1))
                        for t in range(2):
                            k = 2 * q + t
                            ins = mm3(psum[bank][:, :], X_HI[:, k, :], X_LO[:, k, :], k == 0, k == KT - 1, (at + q) % RING,
                                      slice(t * WIDE, (t + 1) * WIDE), swap=True)
                        ins.then_inc(pack_used, 1)

                def ups(g, p, at):
                    pe.wait_ge(ev("m_silu"), g + 1)
                    up(0, p, at)

                def turn(g):
                    pe.wait_ge(ev("m_prod"), g + 2)
                    for j in range(4):
                        ins = pe.transpose(psum[4][:, j * P:(j + 1) * P], PROD_WIDE[:, j * P:(j + 1) * P], M("ident"))
                    ins.then_inc(ev("m_turned"), 1)

                def down(g, p, at, first, last):
                    pe.wait_ge(ev("m_split"), g + 1)
                    for q in range(4):
                        pe.wait_ge(lo_done, p + (q + 1))
                        for c in range(2):
                            ins = mm3(psum[2 + c][:, :], F_HI[:, q, :], F_LO[:, q, :], first and q == 0, last and q == 3,
                                      (at + q) % RING, slice(c * 512, (c + 1) * 512), swap=True)
                        ins.then_inc(pack_used, 1)

                def gather(n):
                    pe.wait_ge(ev("m_choice"), n + 1)
                    for k in range(KT):
                        for t in range(2):
                            ins = pe.matmul(psum[5 + k // 4][:, (k % 4) * P:(k % 4 + 1) * P], HT[:, t, k * P:(k + 1) * P],
                                            CHOICE[:, t, :], start=t == 0, stop=t == 1)
                    ins.then_inc(ev("m_gathered"), 1)

                def scatter(n):
                    pe.wait_ge(ev("m_y_split"), n + 1)
                    pe.wait_ge(ev("m_choice_t"), n + 1)
                    for m in range(KT):
                        out = half(SCATTER_BANKS[m // 2], m % 2)
                        pe.matmul(out, Y_HI[:, m, :], choice_t[:], start=True, stop=False)
                        ins = pe.matmul(out, Y_LO[:, m, :], choice_t[:], start=False, stop=True)
                    ins.then_inc(ev("m_scattered"), 1)

                gather(0)
                with pe.Fori(0, N_EXP) as e:
                    p = e * EXP_PACKS + base
                    g = e * GROUPS
                    pe.wait_ge(ev("m_x_split"), e + 1)
                    ups(g, p, base)
                    up(1, p + 4, base + 4)
                    scatter(e)
                    at = base + group_at(1)
                    ups(g + 1, p + group_at(1), at)
                    pe.wait_ge(ev("m_added"), e + 1)
                    turn(g)
                    up(1, p + (group_at(1) + 4), at + 4)
                    down(g, p + (group_at(1) + 8), at + 8, True, False)
                    for t in range(2):
                        pe.transpose(psum[7][:, t * P:(t + 1) * P], CHOICE[:, t, :], M("ident"))
                    for t in range(2):
                        ins = pe.matmul(psum[7][:, T:T + 1], CHOICE[:, t, :], CUR_GATE[:, t:t + 1], start=t == 0, stop=t == 1)
                    ins.then_inc(ev("m_choice_turned"), 1)
                    with pe.Fori(0, GROUPS - 2) as i:
                        at = base + group_at(2)
                        p2 = e * EXP_PACKS + i * 12 + at
                        g2 = e * GROUPS + i
                        ups(g2 + 2, p2, at)
                        turn(g2 + 1)
                        up(1, p2 + 4, at + 4)
                        down(g2 + 1, p2 + 8, at + 8, False, False)
                    turn(g + (GROUPS - 1))
                    gather(e + 1)
                    down(g + (GROUPS - 1), p + (EXP_PACKS - 4), base + EXP_PACKS - 4, False, True)
                scatter(N_EXP)

            def dense_experts(base):
                for t in range(2):
                    ins = pe.transpose(psum[7][0:N_EXP, t * P:(t + 1) * P], GATE[:, t, 0:N_EXP], M("ident"))
                ins.then_inc(ev("gates_turned"), 1)
                pe.wait_ge(ev("gt_ready"), 1)
                for e in range(N_EXP):
                    ins = pe.matmul(half(e // 2, e % 2), M("pick")[0:N_EXP, e * P:(e + 1) * P], GT[0:N_EXP, :], start=True, stop=True)
                ins.then_inc(ev("gates_spread"), 1)

                def up(bank, p, at):
                    for q in range(4):
                        pe.wait_ge(lo_done, p + (q + 1))
                        for t in range(2):
                            k = 2 * q + t
                            for j in range(4):
                                ins = mm3(half(bank + j // 2, j % 2), h_hi[:, k, :], h_lo[:, k, :], k == 0 and j % 2 == 0,
                                          k == KT - 1, (at + q) % RING, slice(t * WIDE + j * P, t * WIDE + (j + 1) * P), check=True)
                        ins.then_inc(pack_used, 1)

                def ups(g, p, at):
                    pe.wait_ge(ev("d_prod"), g + 1)
                    up(4, p, at)
                    up(6, p + 4, at + 4)

                def down(g, p, at, first=False, last=False):
                    for q in range(4):
                        if q % 2 == 0:
                            pe.wait_ge(ev("d_split"), g * 2 + (q // 2 + 2))
                        pe.wait_ge(lo_done, p + (q + 1))
                        for m in range(KT):
                            ins = mm3(half(m // 2, m % 2), f_hi[:, q % 2, :], f_lo[:, q % 2, :], first and q == 0 and m % 2 == 0,
                                      last and q == 3, (at + q) % RING, slice(m * P, (m + 1) * P), check=True)
                        ins.then_inc(pack_used, 1)

                with pe.Fori(0, N_EXP) as e:
                    p = e * EXP_PACKS + base
                    g = e * GROUPS
                    ups(g, p, base)
                    ups(g + 1, p + group_at(1), base + group_at(1))
                    pe.wait_ge(ev("d_added"), e + 1)
                    down(g, p + (group_at(1) + 8), base + group_at(1) + 8, first=True)
                    with pe.Fori(0, GROUPS - 2) as i:
                        at = base + group_at(2)
                        p2 = e * EXP_PACKS + i * 12 + at
                        g2 = e * GROUPS + i
                        ups(g2 + 2, p2, at)
                        down(g2 + 1, p2 + 8, at + 8)
                    down(g + (GROUPS - 1), p + (EXP_PACKS - 4), base + EXP_PACKS - 4, last=True)

            pe.wait_ge(ev("cond_ready"), seen.next(ev("cond_ready")))

            def ada(g, j, p):
                if not isinstance(g, int) or g >= 3:
                    pe.wait_ge(ev("ada_row"), g - 2)
                for q in range(4):
                    pe.wait_ge(lo_done, p + q + 1)
                    for t in range(2):
                        k = 2 * q + t
                        ins = mm3(psum[4 + j % 3][:, :], cond_hi[:, k, :], cond_lo[:, k, :], k == 0, k == KT - 1, (4 * j + q) % RING,
                                  slice(t * 512, (t + 1) * 512), swap=True)
                    ins.then_inc(pack_used, 1)

            def ada_turn(g, j):
                pe.wait_ge(ev("ada_row"), g + 1)
                for q in range(4):
                    col = bass.ds(g * 8 + 2 * q, 2)
                    ins = pe.matmul(psum[7][:, col], ada_rows[0:2, j % 3, q * P:(q + 1) * P], M("ident")[0:2, 0:2],
                                    start=True, stop=True)
                ins.then_inc(ev("ada_turned"), 1)

            ada(0, 0, 0)
            pe.wait_ge(ev("ident_in"), 16)
            for g in (1, 2):
                ada(g, g, 4 * g)
                ada_turn(g - 1, g - 1)
            with pe.Fori(1, ADA_GROUPS // 3) as i:
                for j in range(3):
                    ada(i * 3 + j, j, i * 12 + 4 * j)
                    ada_turn(i * 3 + (j - 1), (j - 1) % 3)
            ada_turn(ADA_GROUPS - 1, 2)
            pos[0] = 2 * N_ADA
            pe.wait_ge(ev("mat_in"), 16)
            pe.wait_ge(ev("lam_prod"), seen.next(ev("lam_prod")))
            pe.matmul(psum[6][:, 0:4], M("ones")[0:32, :], small[0:32, 0:4], start=True, stop=True).then_inc(ev("lam_sum"), 1)

            norm_sum()
            input_comes()
            for _ in range(5):
                linear()
            pe.wait_ge(ev("lin_read"), 1)
            pe.wait_ge(ev("gup_in"), 16)
            for t in range(2):
                ins = pe.matmul(half(6, t), GUP[:, t * P:(t + 1) * P], GLR[0:RANK, :], start=True, stop=True)
            ins.then_inc(ev("gate_done"), 1)
            for bank in (0, 2):
                linear_tokens(bank)
            for _ in range(8):
                linear()
            lin_all_read()
            pe.wait_ge(ev("vn_ready"), 1)
            pe.wait_ge(ev("ws_ready"), 1)
            for g in range(4):
                for c in range(2):
                    ins = pe.matmul(psum[2 + g // 2][:, (g % 2) * T + c * P:(g % 2) * T + (c + 1) * P],
                                    VN[:, c, g * P:(g + 1) * P], WS[:, g, :], start=True, stop=True)
            ins.then_inc(ev("spatial_done"), 1)
            pe.wait_ge(ev("decays_ready"), 1)
            for t in range(2):
                ins = pe.transpose(psum[7][:, t * P:(t + 1) * P], KD[:, t, :], M("ident"))
            ins.then_inc(ev("kd_turned"), 1)
            for par in range(2):
                r = 64 * par
                for t in range(2):
                    for c in range(2):
                        for i in range(4):
                            ins = pe.matmul(psum[par][:, (t * 2 + c) * P + i * SUB:(t * 2 + c) * P + (i + 1) * SUB],
                                            EK[r:r + 64, t, c * 4 + i, :], QQ[r:r + 64, t, c * P + i * SUB:c * P + (i + 1) * SUB],
                                            start=True, stop=True)
            ins.then_inc(ev("gla_scores"), 1)
            pe.wait_ge(ev("kdt_ready"), 1)
            for h in range(4):
                r = 64 * (h % 2)
                ins = pe.matmul(psum[6][r:r + 64, (h // 2) * P:(h // 2 + 1) * P], KDT[:, h // 2, r:r + 64], VB[:, 0, h * P:(h + 1) * P],
                                start=True, stop=True)
            ins.then_inc(ev("state_done"), 1)
            pe.wait_ge(ev("state_ready"), 1)
            pe.wait_ge(ev("ats_ready"), 1)
            for h in range(4):
                r = 64 * (h % 2)
                for c in range(2):
                    o = psum[4 + h % 2][:, (h // 2) * T + c * P:(h // 2) * T + (c + 1) * P]
                    ins = pe.matmul(o, VB[:, c, h * P:(h + 1) * P], ATS[:, h % 2, (h // 2) * 2 + c, :], start=True, stop=c == 0)
                    if c == 1:
                        ins = pe.matmul(o, ST[r:r + 64, h // 2, :], QI[r:r + 64, h // 2, :], start=False, stop=True)
            ins.then_inc(ev("gla_out"), 1)
            pe.wait_ge(ev("squares"), seen.next(ev("squares")))
            for b in range(2):
                ins = pe.matmul(psum[b][:, :], M("ones"), sq[:, 2 * b:2 * b + 2, :], start=True, stop=True)
            ins.then_inc(ev("sum_ready"), 1)
            input_comes()
            pe.wait_ge(ev("gla_read"), 1)
            out_linears(True)
            input_comes()
            lin_all_read()
            ffn(FF_STEPS)
            norm_sum()
            input_comes()

            def head_sums(squares, tiles):
                pe.wait_ge(ev("lin_read"), tiles)
                for k in range(8):
                    ins = pe.matmul(half(k // 2, k % 2), M("block64"), squares[:, k, :], start=True, stop=True)
                ins.then_inc(ev("sum_ready"), 1)

            lin_base = lin[0]
            for _ in range(11):
                linear()
            head_sums(sq, lin_base + 9)
            for _ in range(6):
                linear()
            linear_tokens(6)
            pe.wait_ge(ev("q_scaled"), 1)
            head_sums(tmp, lin_base + 17)
            pe.wait_ge(ev("wide_read"), wide[0])
            linear_tokens(6)
            linear()
            pe.wait_ge(ev("gates_summed"), 1)
            pe.wait_ge(ev("wide_read"), wide[0])
            for c in range(2):
                ins = pe.transpose(psum[7][:, c * C_HEADS:(c + 1) * C_HEADS], OC[0:C_HEADS, c * P:(c + 1) * P],
                                   M("ident")[0:C_HEADS, 0:C_HEADS])
            ins.then_inc(ev("gates_sum_turned"), 1)
            for _ in range(7):
                linear()
            attention("odd")
            input_comes()
            out_linears(True)
            input_comes()
            linear()
            lin_all_read()
            pe.wait_ge(ev("logits_ready"), 1)
            for t in range(2):
                ins = pe.transpose(psum[7][:, t * 8:t * 8 + 8], RLT[0:N_EXP, t * P:(t + 1) * P], M("ident")[0:N_EXP, 0:N_EXP])
            ins.then_inc(ev("logits_turned"), 1)
            for t in range(2):
                for k in range(KT):
                    ins = pe.transpose(psum[2 * t + k // 4][:, (k % 4) * P:(k % 4 + 1) * P], tmp[:, k, t * P:(t + 1) * P],
                                       M("ident"))
            ins.then_inc(ev("m_h_turned"), 1)
            pe.wait_ge(ev("chosen"), 1)
            pe.matmul(psum[7][:, 0:N_EXP], M("mask01"), SEL[:, 0, :], start=True, stop=True)
            pe.matmul(psum[7][:, 8:8 + N_EXP], M("ones"), SEL[:, 0, :], start=True, stop=False)
            pe.matmul(psum[7][:, 8:8 + N_EXP], M("mask01"), SEL[:, 1, :], start=False, stop=True)
            for t in range(2):
                ins = pe.matmul(psum[7][:, 16:16 + N_EXP], M("ones"), SEL[:, t, :], start=t == 0, stop=t == 1)
            ins.then_inc(ev("slots_counted"), 1)
            pe.wait_ge(ev("routed"), 1)
            pe.wait_ge(ev("m_h_t"), 1)
            n = pe.value_load(fullest[0:1, 0:1], min_val=0, max_val=T)
            with pe.If(n > P):
                dense_experts(pos[0])
            with pe.Else():
                sparse_experts(pos[0])
            pos[0] += N_EXP * EXP_PACKS
            norm_sum()
            downs = [0]
            for l in range(2):
                for stream in ("context", "latents"):
                    only_kv = l == 1 and stream == "context"
                    norm_sum()
                    input_comes()
                    n_normed = 2 if only_kv else 8
                    lin_base = lin[0]
                    for _ in range(n_normed + 1):
                        linear()
                    pe.wait_ge(ev("lin_read"), lin_base + n_normed)
                    if downs[0]:
                        pe.wait_ge(ev("x_part"), 12 + 8 * downs[0])
                    pe.matmul(half(0, 0), M("ones"), sq[:, 0, :], start=True, stop=True)
                    ins = pe.matmul(half(1, 0), M("block64"), sq[:, 1, :], start=True, stop=True)
                    if not only_kv:
                        for k in range(4):
                            pe.matmul(half(2 + k // 2, k % 2), M("block64"), sq[:, 2 + k, :], start=True, stop=True)
                        pe.matmul(half(0, 1), M("ones"), sq[:, 6, :], start=True, stop=False)
                        ins = pe.matmul(half(0, 1), M("ones"), sq[:, 7, :], start=False, stop=True)
                    ins.then_inc(ev("sum_ready"), 1)
                    for _ in range(2 if only_kv else 4):
                        linear()

                    def rotate(n):
                        rot, _, _, rows, x = ROPED[n]
                        width = x.shape[1] * T
                        if n >= 4:
                            pe.wait_ge(ev("rope_out"), seen.now(ev("rope_out")) + n - 3)
                        pe.matmul(psum[n % 4 if n < 6 else n % 2][0:rows, 0:width], M(rot)[0:rows, 0:rows], x, start=True, stop=True)\
                          .then_inc(ev("rotated"), 1)

                    if stream == "latents":
                        pe.wait_ge(ev("rope_in"), seen.next(ev("rope_in")))
                        lin_all_read()
                        for n in range(4):
                            rotate(n)
                    linear_tokens(6, 384)
                    if stream == "latents":
                        rotate(4)
                        rotate(5)
                    pe.wait_ge(ev("latent_split"), seen.next(ev("latent_split")))
                    lin_all_read()
                    pe.wait_ge(lo_done, pos[0] + 1)
                    s = pos[0] % RING
                    for h in range(4):
                        mm3(half(4 + h // 2, h % 2), h_hi[:, 0, :], h_lo[:, 0, :], True, True, s, slice(h * P, (h + 1) * P))
                    vh = w_hi[:, s, 0:512].rearrange("p (h c) -> p h c", h=4)[:, :, 64:128]
                    vl = w_lo[:, s, 0:512].rearrange("p (h c) -> p h c", h=4)[:, :, 64:128]
                    for tk in range(2):
                        tt = slice(tk * P, (tk + 1) * P)
                        pe.matmul(half(6, tk), h_hi[:, 0, tt], vh, start=True, stop=False)
                        pe.matmul(half(6, tk), h_lo[:, 0, tt], vh, start=False, stop=False)
                        ins = pe.matmul(half(6, tk), h_hi[:, 0, tt], vl, start=False, stop=True)
                    ins.then_inc(pack_used, 1)
                    pos[0] += 1
                    if not only_kv:
                        pe.wait_ge(ev("latent_split"), seen.next(ev("latent_split")))
                        pe.wait_ge(lo_done, pos[0] + 1)
                        if stream == "latents":
                            pe.wait_ge(ev("rope_out"), seen.now(ev("rope_out")) + 4)
                        s = pos[0] % RING
                        for h in range(4):
                            for k in range(2):
                                ins = mm3(half(2 + h // 2, h % 2), h_hi[:, 1 + k, :], h_lo[:, 1 + k, :], k == 0, k == 1, s,
                                          slice((2 * h + k) * P, (2 * h + k + 1) * P))
                        ins.then_inc(pack_used, 1)
                        pos[0] += 1
                    if stream == "latents":
                        pe.wait_ge(ev("rope_in"), seen.next(ev("rope_in")))
                        rotate(6)
                        rotate(7)
                        seen.next(ev("rope_out"), len(ROPED))
                    if only_kv:
                        continue
                    attention(stream)
                    pe.wait_ge(ev("squares"), seen.next(ev("squares")))
                    pe.matmul(psum[0][:, :], M("block64"), sq[:, 0:2, :], start=True, stop=True).then_inc(ev("sum_ready"), 1)
                    input_comes()
                    out_linears(False, MIXED_ORDER)
                    norm_sum()
                    input_comes()
                    lin_all_read()
                    ffn(FF_STEPS)
                    norm_sum()
                    downs[0] += 1
            assert pos[0] == TOTAL

        @block.scalar
        def _(act):
            seen = Seen()
            steps = [0]
            nsplit = [0]
            nlin = [0]

            def A(out, in_, func, **kw):
                return act.activation(out, in_, func, **kw)

            def step(ins):
                steps[0] += 1
                ins.then_inc(ev("act_step"), 1)

            def settle():
                act.wait_ge(ev("act_step"), steps[0])

            def wait(name, n=1):
                act.wait_ge(ev(name), seen.next(ev(name), n))

            def split_at(p, slot, turn, reuse):
                act.wait_ge(raw_in[slot], 16 * turn + 16)
                if reuse:
                    act.wait_ge(pack_used, p - RING + 1)
                    act.wait_ge(lo_done, p - RING + 1)
                A(w_hi[:, slot, :], raw[:, slot, :], ACT.Copy).then_inc(hi_done, 1)

            def split_to(p):
                while nsplit[0] < min(p, TOTAL):
                    n = nsplit[0]
                    split_at(n, n % RING, n // RING, n >= RING)
                    nsplit[0] += 1

            def lin_wait():
                split_to(2 * N_ADA + nlin_pos[0] + AHEAD)
                nlin_pos[0] += 1
                act.wait_ge(pack_used, 2 * N_ADA + nlin_pos[0])
                b = 4 + nlin[0] % 2
                nlin[0] += 1
                return b

            nlin_pos = [0]
            nwide = [0]
            nffn = [0]
            nrs = [0]
            ndown = [0]

            def fm(out, func=ACT.Copy, **kw):
                b = lin_wait()
                A(out, half(b, 0), func, **kw).then_inc(ev("lin_read"), 1)

            def fm_squared(m):
                b = lin_wait()
                A(ZR[:, m, :], half(b, 0), ACT.Copy)
                A(sq[:, m, :], half(b, 0), ACT.Square).then_inc(ev("lin_read"), 1)

            def tokens_wide(bank, outs, func=ACT.Copy):
                for _ in range(4):
                    split_to(2 * N_ADA + nlin_pos[0] + AHEAD)
                    nlin_pos[0] += 1
                act.wait_ge(pack_used, 2 * N_ADA + nlin_pos[0])
                for tk in range(2):
                    for out, cols in outs:
                        ins = A(out[:, tk, :], psum[bank + tk][:, cols], func)
                    ins.then_inc(ev("wide_read"), 1)
                nwide[0] += 2

            def ln_exp_tables():
                act.preload_act_table_set("natural_log_exp_and_others")

            def rsqrt_of(out, in_, scale, bias, sem):
                step(A(out, in_, ACT.Ln, scale=scale, bias=bias))
                settle()
                A(out, out, ACT.Exp, scale=-0.5).then_inc(sem, 1)

            def squares(x, parts=False, linears=False):
                for k in range(0, KT, 2):
                    if linears:
                        skip_linears(2)
                    if parts:
                        wait("x_part")
                    A(sq[:, k:k + 2, :], x[:, k:k + 2, :], ACT.Square).then_inc(ev("squares"), 1)

            def norm(shift=None):
                ln_exp_tables()
                wait("sum_ready")
                rsqrt_of(rs2[:, nrs[0] % 2, :], half(6, 0), 1.0 / D, V("eps"), ev("rs_ready"))
                nrs[0] += 1
                if shift is not None:
                    for k in range(KT):
                        wait("scaled")
                        A(h_hi[:, k, :], tmp[:, k, :], ACT.Identity, bias=shift(k)).then_inc(ev("h_hi_ready"), 1)

            def split_tmp(tiles=range(KT)):
                for k in tiles:
                    wait("scaled")
                    A(h_hi[:, k, :], tmp[:, k, :], ACT.Copy).then_inc(ev("h_hi_ready"), 1)

            def skip_linears(n):
                for _ in range(n):
                    split_to(2 * N_ADA + nlin_pos[0] + AHEAD)
                    nlin_pos[0] += 1
                    nlin[0] += 1

            def ffn(n_steps):
                base = nffn[0]
                first = 2 * N_ADA + nlin_pos[0]
                split_to(first + AHEAD)
                p0 = nsplit[0]

                def one(s, par, off, it):
                    act.wait_ge(pack_used, first + 2 if isinstance(s, int) and s == 0 else s * 3 + (first + 1))
                    if not isinstance(s, int) or base + s >= 2:
                        act.wait_ge(ev("act_ready"), base + s - 1)
                    A(sg[:, par, :], half(4 + par, 0), ACT.Silu).then_inc(ev("silu_done"), 1)
                    for j in range(3):
                        p = p0 + off + j
                        if isinstance(s, int) and p >= TOTAL:
                            continue
                        slot = p % RING
                        split_at(it * RING + p if it is not None else p, slot,
                                 (it + p // RING) if it is not None else p // RING, True)

                last = p0 + 3 * n_steps >= TOTAL
                head, tail = 2, 4 if last else 0
                for s in range(head):
                    one(s, s % 2, 3 * s, None)
                with act.Fori(0, (n_steps - head - tail) // 2) as i:
                    for j in range(2):
                        one(i * 2 + (head + j), j, 3 * (head + j), i)
                for s in range(n_steps - tail, n_steps):
                    one(s, s % 2, 3 * s, None)
                nffn[0] += n_steps
                nsplit[0] = min(p0 + 3 * n_steps, TOTAL)
                nlin_pos[0] += 3 * n_steps

            def attention(kind):
                heads, n_keys = heads_and_keys(kind)
                for u in range(2 * len(heads) + 2):
                    if u < 2 * len(heads):
                        n = n_keys(u % 2) * P
                        wait("max_ready")
                        src = logit[:, u % 2, 0:n] if kind == "odd" else psum[SCORE_BANKS[u % 4]][:, 0:n]
                        A(PROBS[u % 4][:, 0:n], src, ACT.Exp, bias=NEG_MAX[u % 4], accum_out=SUM[u % 4])\
                            .then_inc(ev("exp_done"), 1)
                    if u >= 2:
                        v = u - 2
                        c, i = v % 2, v // 2
                        ns = n_keys(c)
                        wait("turned")
                        if i >= 2:
                            act.wait_ge(ev("value_done"), seen.now(ev("value_done")) + i - 1)
                        out = prob_t[:, i % 2, :].rearrange("p (s t) -> p s t", t=T)[:, 0:ns, c * P:(c + 1) * P]
                        A(out, psum[2 + v % 2][:, 0:ns * P].rearrange("p (s t) -> p s t", t=P), ACT.Copy)\
                            .then_inc(ev("prob_t_ready"), 1)
                seen.next(ev("value_done"), len(heads))

            def experts(sparse):
                base = 2 * N_ADA + nlin_pos[0]

                class Ahead:
                    n = AHEAD

                def split(n, e, i=None):
                    while Ahead.n < n:
                        c = base + Ahead.n
                        p, turn = e * EXP_PACKS + c, e * (EXP_PACKS // RING) + c // RING
                        if i is not None:
                            p, turn = i * 12 + p, i * (12 // RING) + turn
                        split_at(p, c % RING, turn, True)
                        Ahead.n += 1

                def silu(g, p):
                    act.wait_ge(pack_used, p + 4)
                    if sparse:
                        act.wait_ge(ev("m_prod"), g + 1)
                        A(SG_WIDE, psum[0][:, :], ACT.Silu).then_inc(ev("m_silu"), 1)
                    else:
                        A(sq[:, 0:2, :], psum[4][:, :].rearrange("p (a t) -> p a t", a=2), ACT.Silu)
                        A(sq[:, 2:4, :], psum[5][:, :].rearrange("p (a t) -> p a t", a=2), ACT.Silu).then_inc(ev("d_silu"), 1)

                def high(g):
                    if sparse:
                        act.wait_ge(ev("m_turned"), g + 1)
                        A(F_HI, psum[4][:, :].rearrange("p (j s) -> p j s", s=P), ACT.Copy).then_inc(ev("m_f_hi"), 1)

                def gathered(n):
                    act.wait_ge(ev("m_gathered"), n + 1)
                    for c in range(2):
                        ins = A(X_HI[:, 4 * c:4 * c + 4, :], psum[5 + c][:, :].rearrange("p (k s) -> p k s", s=P), ACT.Copy)
                    ins.then_inc(ev("m_x_hi"), 1)

                if sparse:
                    act.sem_inc(ev("m_silu"), 1)
                    gathered(0)
                with act.Fori(0, N_EXP) as e:
                    Ahead.n = AHEAD
                    for n in (0, 1):
                        at = group_at(n)
                        split(at + 4 + AHEAD, e)
                        silu(e * GROUPS + n, e * EXP_PACKS + (base + at))
                        if n:
                            high(e * GROUPS)
                        split(at + 8 + AHEAD, e)
                    split(group_at(2) + AHEAD, e)
                    if sparse:
                        act.wait_ge(ev("m_choice_turned"), e + 1)
                        A(choice_t[:], half(7, 0), ACT.Copy)
                        A(SLOT_GATE, psum[7][:, T:T + 1], ACT.Copy).then_inc(ev("m_choice_t"), 1)
                    with act.Fori(0, GROUPS - 2) as i:
                        at = group_at(2)
                        split(at + 4 + AHEAD, e, i)
                        silu(e * GROUPS + i + 2, e * EXP_PACKS + i * 12 + (base + at))
                        high(e * GROUPS + i + 1)
                        split(at + 12 + AHEAD, e, i)
                    Ahead.n = group_at(GROUPS) + AHEAD
                    if sparse:
                        high(e * GROUPS + (GROUPS - 1))
                        gathered(e + 1)
                    split(EXP_PACKS + AHEAD, e)
                    if sparse:
                        act.wait_ge(pack_used, e * EXP_PACKS + (base + EXP_PACKS))
                        act.wait_ge(ev("m_choice_t"), e + 2)
                        for c in range(2):
                            ins = A(Y_HI[:, 4 * c:4 * c + 4, :], psum[2 + c][:, :].rearrange("p (k s) -> p k s", s=P), ACT.Copy,
                                    scale=SLOT_GATE)
                        ins.then_inc(ev("m_y_hi"), 1)

            act.wait_ge(ev("vec_in"), 16)
            A(cond_s[:].rearrange("p k s -> p (k s)"), V("cond"), ACT.Silu).then_inc(ev("cond_silu"), 1)
            split_to(RING)

            def ada_row(g, j):
                act.wait_ge(pack_used, g * 4 + 4)
                if not isinstance(g, int) or g >= 3:
                    act.wait_ge(ev("ada_turned"), g - 2)
                A(ada_rows[0:2, j, :], psum[4 + j][0:2, :], ACT.Copy).then_inc(ev("ada_row"), 1)

            for g in range(3):
                split_to(4 * g + 4 + AHEAD)
                ada_row(g, g)
            with act.Fori(0, ADA_GROUPS // 3 - 1) as i:
                for j in range(3):
                    for q in range(4):
                        n = 12 + AHEAD + 4 * j + q
                        split_at(i * 12 + n, n % RING, i * 2 + n // RING, True)
                    ada_row(i * 3 + (3 + j), j)
            nsplit[0] = 2 * N_ADA + AHEAD
            wait("lam_sum")
            A(small[:, 4:8], psum[6][:, 0:4], ACT.Exp).then_inc(ev("lam_exp"), 1)
            act.wait_ge(ev("lat_in"), 16)
            squares(lat)
            norm(lambda k: V("zero"))
            fm(GLR)
            for t in range(2):
                fm(QT[:, t, :], scale=0.125)
            for t in range(2):
                fm(KTT[:, t, :])
            wait("gate_done")
            for t in range(2):
                A(GX[:, t, :], half(6, t), ACT.Identity, bias=V("gate_bias", t)).then_inc(ev("gx_ready"), 1)
            tokens_wide(0, [(VB, slice(0, 512))])
            wait("abs_ready")
            step(A(QQ, QQ, ACT.Exp))
            settle()
            A(QQ, QQ, ACT.Ln, bias=V("one")).then_inc(ev("softplus_ready"), 1)
            tokens_wide(2, [(VA, slice(0, 512))], ACT.Gelu_apprx_tanh)
            wait("diffs_ready")
            A(EK, EK, ACT.Exp, scale=-1.0 / 16).then_inc(ev("exps_ready"), 1)
            A(QQ, QQ, ACT.Exp, scale=1.0 / 16).then_inc(ev("exps_ready"), 1)
            A(QI, G[:, :, P:2 * P], ACT.Exp, scale=1.0 / 16).then_inc(ev("exps_ready"), 1)
            A(KD, KD, ACT.Exp, scale=-1.0 / 16).then_inc(ev("exps_ready"), 1)
            wait("var_ready")
            step(A(small[:, 16:18], small[:, 16:18], ACT.Ln, bias=V("eps")))
            settle()
            A(small[:, 16:18], small[:, 16:18], ACT.Exp, scale=-0.5).then_inc(ev("rstd_ready"), 1)
            for t in range(4):
                fm(U[:, t, :], ACT.Gelu_apprx_tanh)
            for t in range(4):
                fm(OG[:, t, :], ACT.Silu)
            split_tmp(range(4))
            wait("gla_out")
            for b in range(2):
                ins = A(sq[:, b:4:2, :], psum[4 + b][:, :].rearrange("p (a t) -> p a t", a=2), ACT.Square)
                if b == 1:
                    ins.then_inc(ev("squares"), 1)
            for b in range(2):
                step(A(tmp[:, 4 + b:8:2, :], psum[4 + b][:, :].rearrange("p (a t) -> p a t", a=2), ACT.Copy))
            settle()
            act.sem_inc(ev("gla_read"), 1)
            ln_exp_tables()
            wait("sum_ready")
            for b in range(2):
                step(A(sq[:, 4 + 2 * b:6 + 2 * b, :], psum[b][:, :].rearrange("p (a t) -> p a t", a=2), ACT.Ln,
                       scale=1.0 / P, bias=V("eps")))
            settle()
            A(sq[:, 4:8, :], sq[:, 4:8, :], ACT.Exp, scale=-0.5).then_inc(ev("rs_ready"), 1)
            split_tmp(range(4, 8))
            squares(lat, parts=True, linears=True)
            norm(lambda k: V("zero"))
            ffn(FF_STEPS)
            ndown[0] += 1
            squares(lat, parts=True)
            norm(lambda k: V("zero"))
            fm(OF)

            def with_square(out, square):
                b = lin_wait()
                A(out, half(b, 0), ACT.Copy)
                A(square, half(b, 0), ACT.Square).then_inc(ev("lin_read"), 1)

            def head_roots(r, scale, bias):
                ln_exp_tables()
                wait("sum_ready")
                for b in range(4):
                    step(A(r[:, 2 * b:2 * b + 2, :], psum[b][:, :].rearrange("p (a t) -> p a t", a=2), ACT.Ln,
                           scale=scale, bias=V(bias)))
                settle()
                A(r[:], r[:], ACT.Exp, scale=-0.5).then_inc(ev("rs_ready"), 1)

            for t in range(8):
                with_square(OQ[:, t, :], sq[:, t, :])
            for t in range(2):
                with_square(OK[:, t, :], tmp[:, t, :])
            head_roots(sq, 1.0, "eps64")
            for t in range(2, 8):
                with_square(OK[:, t, :], tmp[:, t, :])
            A(OF[0:C_HEADS], OF[0:C_HEADS], ACT.Identity, bias=V("forget_bias")[0:C_HEADS]).then_inc(ev("f_ready"), 1)
            wait("abs_ready")
            step(A(ONC[0:C_HEADS], ONC[0:C_HEADS], ACT.Exp))
            settle()
            A(ONC[0:C_HEADS], ONC[0:C_HEADS], ACT.Ln, bias=V("one")[0:C_HEADS]).then_inc(ev("softplus_ready"), 1)
            tokens_wide(6, [(OV[:, :, 0:512], slice(0, 512))])
            head_roots(tmp, 1.0 / 64, "eps")
            tokens_wide(6, [(OV[:, :, 512:1024], slice(0, 512))])
            for t in range(8):
                fm(OO[:, t, :], ACT.Sigmoid)
            attention("odd")
            split_tmp()
            squares(lat, parts=True, linears=True)
            norm(lambda k: V("zero"))
            fm(RLT)
            act.wait_ge(ev("lin_read"), nlin[0])
            act.sem_inc(ev("logits_ready"), 1)
            act.wait_ge(ev("m_h_turned"), 1)
            for c in range(2):
                ins = A(HT[:, 0, c * 512:(c + 1) * 512], psum[c][:, :], ACT.Copy)
            ins.then_inc(ev("m_h_t0"), 1)
            wait("top_diff")
            A(small[:, 24:26], small[:, 24:26], ACT.Exp).then_inc(ev("top_exp"), 1)
            split_to(2 * N_ADA + nlin_pos[0] + AHEAD)
            act.wait_ge(ev("routed"), 1)
            n = act.value_load(fullest[0:1, 0:1], min_val=0, max_val=T)
            with act.If(n > P):
                experts(sparse=False)
            with act.Else():
                experts(sparse=True)
            nlin_pos[0] += N_EXP * EXP_PACKS
            nsplit[0] += N_EXP * EXP_PACKS
            wait("x_ready")
            squares(lat)
            norm()
            for l in range(2):
                for s, (stream, x) in enumerate((("context", con), ("latents", lat))):
                    only_kv = l == 1 and stream == "context"
                    k0 = T if stream == "context" else 0
                    col = 1 - s
                    if (l, s) == (0, 0):
                        act.wait_ge(ev("con_in"), 16)
                        wait("x_ready")
                    if l == 1:
                        act.wait_ge(ev("x_part"), seen.now(ev("x_part")) - (4 if stream == "context" else 0))
                    squares(x)
                    norm(lambda k: mod[:, l, k, col:col + 1])
                    for m in (0, 1) if only_kv else (0, 1, 6, 7, 2, 3, 4, 5):
                        fm_squared(m)
                    fm(KPE)
                    ln_exp_tables()
                    wait("sum_ready")
                    step(A(sq[:, 0, :], half(0, 0), ACT.Ln, scale=1.0 / 128, bias=V("eps")))
                    step(A(sq[:, 1, :], half(1, 0), ACT.Ln, scale=1.0 / 64, bias=V("eps")))
                    if not only_kv:
                        for b in range(2):
                            step(A(sq[:, 2 + 2 * b:4 + 2 * b, :], psum[2 + b][:, :].rearrange("p (a t) -> p a t", a=2),
                                   ACT.Ln, scale=1.0, bias=V("eps64")))
                        step(A(sq[:, 6, :], half(0, 1), ACT.Ln, scale=1.0 / 256, bias=V("eps")))
                    settle()
                    n = 2 if only_kv else 7
                    A(sq[:, 0:n, :], sq[:, 0:n, :], ACT.Exp, scale=-0.5).then_inc(ev("rs_ready"), 1)
                    for t in range(2):
                        fm(KD2[:, t, k0:k0 + T])
                    if not only_kv:
                        for t in range(2):
                            fm(QD[:, t, :], scale=DIFF_SCALE)
                    rows = slice(k0 // P, k0 // P + 2)
                    tokens_wide(6, [(VD[:, rows, :], slice(0, 256)), (VG[:, rows, :], slice(256, 384))])
                    wait("latents_normed")
                    A(h_hi[:, 0, :], tmp[:, 0, :], ACT.Copy).then_inc(ev("latents_hi"), 1)
                    if not only_kv:
                        A(h_hi[:, 1:3, :], tmp[:, 1:3, :], ACT.Copy).then_inc(ev("latents_hi"), 1)
                    split_to(2 * N_ADA + nlin_pos[0] + AHEAD)
                    nlin_pos[0] += 1
                    act.wait_ge(pack_used, 2 * N_ADA + nlin_pos[0])
                    for b in range(2):
                        A(KM[0:64, 2 * b:2 * b + 2, k0:k0 + T], psum[4 + b][0:64, :].rearrange("p (a t) -> p a t", a=2), ACT.Copy)\
                            .then_inc(ev("km_ready"), 1)
                    A(VM[:, k0 // P:k0 // P + 2, :], psum[6][:, :].rearrange("p (a t) -> p a t", a=2), ACT.Copy)\
                        .then_inc(ev("km_ready"), 1)
                    if not only_kv:
                        split_to(2 * N_ADA + nlin_pos[0] + AHEAD)
                        nlin_pos[0] += 1
                        act.wait_ge(pack_used, 2 * N_ADA + nlin_pos[0])
                        for b in range(2):
                            A(QM[0:MLA_QK, 2 * b:2 * b + 2, :], psum[2 + b][0:MLA_QK, :].rearrange("p (a t) -> p a t", a=2),
                              ACT.Copy, scale=MLA_SCALE).then_inc(ev("qm_ready"), 1)
                    if only_kv:
                        wait("context_keys_ready")
                        continue
                    attention(stream)
                    wait("diff_ready")
                    A(sq[:, 0:2, :], tmp[:, 2:4, :], ACT.Square).then_inc(ev("squares"), 1)
                    ln_exp_tables()
                    split_tmp(MIXED_ORDER[:BEFORE_ROOT])
                    wait("sum_ready")
                    step(A(sq[:, 2:4, :], psum[0][:, :].rearrange("p (a t) -> p a t", a=2), ACT.Ln, scale=1.0 / 64, bias=V("eps")))
                    settle()
                    A(sq[:, 2:4, :], sq[:, 2:4, :], ACT.Exp, scale=-0.5).then_inc(ev("rs_ready"), 1)
                    split_tmp(MIXED_ORDER[BEFORE_ROOT:])
                    for m in range(KT):
                        fm_squared(m)
                    norm()
                    squares(x, parts=True)
                    norm(lambda k: mod[:, l, 24 + k, col:col + 1])
                    ffn(FF_STEPS)
                    for b in range(4):
                        if b < 3:
                            act.wait_ge(ev("bank_down"), 3 * ndown[0] + b + 1)
                        else:
                            act.wait_ge(pack_used, 2 * N_ADA + nlin_pos[0])
                        A(sq[:, 2 * b:2 * b + 2, :], psum[b][:, :].rearrange("p (a t) -> p a t", a=2), ACT.Square)\
                            .then_inc(ev("squares"), 1)
                    ndown[0] += 1
                    norm()
                    seen.next(ev("x_part"), 4)

        @block.vector
        def _(v):
            seen = Seen()
            steps = [0]
            nsplit = [0]
            npos = [0]
            nlin = [0]
            nwide = [0]
            nrs = [0]
            nx = [0]

            def step(ins):
                steps[0] += 1
                ins.then_inc(ev("dve_step"), 1)

            def settle():
                v.wait_ge(ev("dve_step"), steps[0])

            def link(ins):
                step(ins)
                settle()

            def wait(name, n=1):
                v.wait_ge(ev(name), seen.next(ev(name), n))

            def split_at(p, slot, reuse):
                v.wait_ge(hi_done, p + 1)
                if reuse:
                    v.wait_ge(pack_used, p - RING + 1)
                v.tensor_tensor(w_lo[:, slot, :], raw[:, slot, :], w_hi[:, slot, :].bitcast(F32), ALU.subtract)\
                    .then_inc(lo_done, 1)

            def split_to(p):
                while nsplit[0] < min(p, TOTAL):
                    n = nsplit[0]
                    split_at(n, n % RING, n >= RING)
                    nsplit[0] += 1

            def next_rs():
                wait("rs_ready")
                nrs[0] += 1
                return rs2[:, (nrs[0] - 1) % 2, :]

            def norm(x, gain, shift):
                rs = next_rs()

                def scale(k):
                    v.scalar_tensor_tensor(tmp[:, k, :], x[:, k, :], gain(k), rs, ALU.mult, ALU.mult).then_inc(ev("scaled"), 1)

                scale(0)
                scale(1)
                for k in range(KT):
                    wait("h_hi_ready")
                    v.scalar_tensor_tensor(h_lo[:, k, :], tmp[:, k, :], shift(k), h_hi[:, k, :].bitcast(F32), ALU.add,
                                           ALU.subtract).then_inc(ev("h_ready"), 1)
                    if k + 2 < KT:
                        scale(k + 2)

            def low_part(k):
                wait("h_hi_ready")
                v.tensor_tensor(h_lo[:, k, :], tmp[:, k, :], h_hi[:, k, :].bitcast(F32), ALU.subtract)\
                    .then_inc(ev("h_ready"), 1)

            def others_read(n, tokens=0):
                for _ in range(n):
                    split_to(2 * N_ADA + npos[0] + AHEAD)
                    npos[0] += 1
                nlin[0] += n - tokens
                nwide[0] += tokens // 2

            def add_linears(x):
                for m in range(KT):
                    split_to(2 * N_ADA + npos[0] + AHEAD)
                    npos[0] += 1
                    v.wait_ge(pack_used, 2 * N_ADA + npos[0])
                    b = 4 + nlin[0] % 2
                    nlin[0] += 1
                    v.tensor_tensor(x[:, m, :], x[:, m, :], half(b, 0), ALU.add).then_inc(ev("lin_read"), 1)
                    if m % 2:
                        v.wait_ge(ev("lin_read"), nlin[0])
                        v.sem_inc(ev("x_part"), 1)
                        nx[0] += 1

            def ffn(n_steps):
                base = seen.now(ev("silu_done"))
                start = 2 * N_ADA + npos[0]
                split_to(2 * N_ADA + npos[0] + AHEAD)
                p0 = nsplit[0]

                def one(s, par, off, it):
                    v.wait_ge(ev("silu_done"), base + s + 1)
                    if not isinstance(s, int) or base + s >= 2:
                        v.wait_ge(pack_used, s * 3 + (start - 1))
                    v.tensor_tensor(prod[:, par, :], sg[:, par, :], half(4 + par, 1), ALU.mult).then_inc(ev("prod_done"), 1)
                    v.wait_ge(ev("prod_done"), base + s + 1)
                    v.tensor_copy(f_hi[:, par, :], prod[:, par, :]).then_inc(ev("f_hi_done"), 1)
                    v.wait_ge(ev("f_hi_done"), base + s + 1)
                    v.tensor_tensor(f_lo[:, par, :], prod[:, par, :], f_hi[:, par, :].bitcast(F32), ALU.subtract)\
                        .then_inc(ev("act_ready"), 1)
                    for j in range(3):
                        p = p0 + off + j
                        if isinstance(s, int) and p >= TOTAL:
                            continue
                        split_at(p if it is None else it * RING + p, p % RING, True)

                last = p0 + 3 * n_steps >= TOTAL
                head, tail = 2, 4 if last else 0
                for s in range(head):
                    one(s, s % 2, 3 * s, None)
                with v.Fori(0, (n_steps - head - tail) // 2) as i:
                    for j in range(2):
                        one(i * 2 + (head + j), j, 3 * (head + j), i)
                for s in range(n_steps - tail, n_steps):
                    one(s, s % 2, 3 * s, None)
                seen.next(ev("silu_done"), n_steps)
                nsplit[0] = min(p0 + 3 * n_steps, TOTAL)
                npos[0] += 3 * n_steps

            def experts(sparse):
                base = 2 * N_ADA + npos[0]

                class Ahead:
                    n = AHEAD

                def split(n, e, i=None):
                    while Ahead.n < n:
                        c = base + Ahead.n
                        split_at(e * EXP_PACKS + c if i is None else e * EXP_PACKS + i * 12 + c, c % RING, True)
                        Ahead.n += 1

                def product(g, p):
                    v.wait_ge(ev("m_silu"), g + 2)
                    v.wait_ge(pack_used, p)
                    v.tensor_tensor(PROD_WIDE, SG_WIDE, psum[1][:, :], ALU.mult).then_inc(ev("m_prod"), 1)

                def product_all(g, p, e):
                    v.wait_ge(ev("d_silu"), g + 1)
                    v.wait_ge(pack_used, p)
                    v.wait_ge(ev("d_split"), g * 2 + 1)
                    for b in range(2):
                        ins = v.tensor_tensor(sq[:, 4 + 2 * b:6 + 2 * b, :], sq[:, 2 * b:2 * b + 2, :],
                                              psum[6 + b][:, :].rearrange("p (a t) -> p a t", a=2), ALU.mult)
                        ins.then_inc(ev("d_mul"), 1)
                    v.wait_ge(ev("d_mul"), g * 2 + 2)
                    v.tensor_tensor(sq[:, 4:8, :], sq[:, 4:8, :], GB[:, bass.ds(e, 1), :].to_broadcast([P, 4, T]), ALU.mult)\
                        .then_inc(ev("d_prod"), 1)

                def pair_parts(g, n):
                    v.wait_ge(ev("d_prod"), g + 2)
                    src = sq[:, 4 + 2 * n:6 + 2 * n, :]
                    v.tensor_copy(f_hi[:], src).then_inc(ev("d_f_hi"), 1)
                    v.wait_ge(ev("d_f_hi"), g * 2 + (n + 1))
                    v.tensor_tensor(f_lo[:], src, f_hi[:].bitcast(F32), ALU.subtract).then_inc(ev("d_split"), 1)

                def low(g):
                    v.wait_ge(ev("m_f_hi"), g + 1)
                    v.tensor_tensor(F_LO, psum[4][:, :].rearrange("p (j s) -> p j s", s=P), F_HI.bitcast(F32), ALU.subtract)\
                        .then_inc(ev("m_split"), 1)

                def choose(n):
                    v.tensor_copy(CUR_SLOT.unsqueeze(2), SLOT[:, :, bass.ds(n, 1)]).then_inc(ev("m_columns"), 1)
                    v.tensor_copy(CUR_GATE.unsqueeze(2), GATE[:, :, bass.ds(n, 1)]).then_inc(ev("m_columns"), 1)
                    v.wait_ge(ev("m_columns"), n * 2 + 2)
                    for t in range(2):
                        ins = v.tensor_scalar(CHOICE[:, t, :], M("iota"), CUR_SLOT[:, t:t + 1], None, ALU.is_equal)
                    ins.then_inc(ev("m_choice"), 1)

                def gathered(n):
                    v.wait_ge(ev("m_x_hi"), n + 1)
                    for c in range(2):
                        ins = v.tensor_tensor(X_LO[:, 4 * c:4 * c + 4, :], psum[5 + c][:, :].rearrange("p (k s) -> p k s", s=P),
                                              X_HI[:, 4 * c:4 * c + 4, :].bitcast(F32), ALU.subtract)
                    ins.then_inc(ev("m_x_split"), 1)

                def add(n):
                    v.wait_ge(ev("m_scattered"), n + 1)
                    for b in range(4):
                        ins = v.tensor_tensor(lat[:, 2 * b:2 * b + 2, :], lat[:, 2 * b:2 * b + 2, :],
                                              psum[SCATTER_BANKS[b]][:, :].rearrange("p (a t) -> p a t", a=2), ALU.add)
                    ins.then_inc(ev("m_added"), 1)

                def sparse_expert(e):
                    g, p = e * GROUPS, e * EXP_PACKS + base
                    split(8 + AHEAD, e)
                    product(g, p + 8)
                    add(e)
                    at = group_at(1)
                    split(at + 4 + AHEAD, e)
                    low(g)
                    split(at + 8 + AHEAD, e)
                    product(g + 1, p + (at + 8))
                    split(at + 12 + AHEAD, e)
                    v.wait_ge(ev("m_choice_turned"), e + 1)
                    choose(e + 1)
                    with v.Fori(0, GROUPS - 2) as i:
                        at = group_at(2)
                        g2, p2 = e * GROUPS + i + 1, e * EXP_PACKS + i * 12 + (base + at + 8)
                        split(at + 4 + AHEAD, e, i)
                        low(g2)
                        split(at + 8 + AHEAD, e, i)
                        product(g2 + 1, p2)
                        split(at + 12 + AHEAD, e, i)
                    Ahead.n = group_at(GROUPS) + AHEAD
                    low(g + (GROUPS - 1))
                    gathered(e + 1)
                    split(EXP_PACKS + AHEAD, e)
                    v.wait_ge(ev("m_y_hi"), e + 1)
                    for c in range(2):
                        ins = v.scalar_tensor_tensor(Y_LO[:, 4 * c:4 * c + 4, :], psum[2 + c][:, :].rearrange("p (k s) -> p k s", s=P),
                                                     SLOT_GATE, Y_HI[:, 4 * c:4 * c + 4, :].bitcast(F32), ALU.mult, ALU.subtract)
                    ins.then_inc(ev("m_y_split"), 1)

                def dense_expert(e):
                    g, p = e * GROUPS, e * EXP_PACKS + base
                    split(8 + AHEAD, e)
                    product_all(g, p + 8, e)
                    pair_parts(g, 0)

                    def group(at, g, p, i=None):
                        split(at + 10 + AHEAD, e, i)
                        v.wait_ge(pack_used, p + 10)
                        pair_parts(g - 1, 1)
                        split(at + 12 + AHEAD, e, i)
                        product_all(g, p + 12, e)
                        pair_parts(g, 0)

                    group(group_at(1), g + 1, p + group_at(1))
                    with v.Fori(0, GROUPS - 2) as i:
                        group(group_at(2), e * GROUPS + i + 2, e * EXP_PACKS + i * 12 + (base + group_at(2)), i)
                    Ahead.n = group_at(GROUPS) + AHEAD
                    split(EXP_PACKS - 2 + AHEAD, e)
                    v.wait_ge(pack_used, p + (EXP_PACKS - 2))
                    pair_parts(g + (GROUPS - 1), 1)
                    split(EXP_PACKS + AHEAD, e)
                    v.wait_ge(pack_used, p + EXP_PACKS)
                    for b in range(4):
                        ins = v.tensor_tensor(lat[:, 2 * b:2 * b + 2, :], lat[:, 2 * b:2 * b + 2, :],
                                              psum[b][:, :].rearrange("p (a t) -> p a t", a=2), ALU.add)
                    ins.then_inc(ev("d_added"), 1)

                for name in ("m_prod",) if sparse else ("d_prod", "d_split"):
                    v.sem_inc(ev(name), 1)
                if sparse:
                    choose(0)
                    zero = V("zero")
                    for a in (Y_HI, Y_LO):
                        v.tensor_copy(a, zero.unsqueeze(2).to_broadcast([P, KT, P])).then_inc(ev("m_zeroed"), 1)
                    v.tensor_copy(choice_t[:], zero.to_broadcast([P, T])).then_inc(ev("m_zeroed"), 1)
                    v.wait_ge(ev("m_zeroed"), 3)
                    v.sem_inc(ev("m_y_split"), 1)
                    v.sem_inc(ev("m_choice_t"), 1)
                    gathered(0)
                    with v.Fori(0, N_EXP) as e:
                        Ahead.n = AHEAD
                        sparse_expert(e)
                    add(N_EXP)
                    v.wait_ge(ev("m_added"), N_EXP + 1)
                else:
                    wait("gates_turned")
                    v.tensor_copy(GT[0:N_EXP, :], psum[7][0:N_EXP, 0:T]).then_inc(ev("gt_ready"), 1)
                    wait("gates_spread")
                    for b in range(4):
                        v.tensor_copy(GB[:, 2 * b:2 * b + 2, :], psum[b][:, :].rearrange("p (a t) -> p a t", a=2))\
                            .then_inc(ev("d_gates"), 1)
                    v.wait_ge(ev("d_gates"), 4)
                    v.sem_inc(ev("d_added"), 1)
                    with v.Fori(0, N_EXP) as e:
                        Ahead.n = AHEAD
                        dense_expert(e)
                    v.wait_ge(ev("d_added"), N_EXP + 1)

            def attention(kind, pair_done):
                heads, n_keys = heads_and_keys(kind)
                pair = 0
                total = 2 * len(heads)

                def merged(i):
                    v.wait_ge(ev("value_done"), seen.now(ev("value_done")) + i + 1)
                    pair_done(heads[i])

                for u in range(total + 3):
                    if u < total:
                        c = u % 2
                        n = n_keys(c) * P
                        wait("scores_done")
                        bank = psum[SCORE_BANKS[u % 4]]
                        src = bank[:, 0:n]
                        if kind == "odd":
                            if u >= 2:
                                v.wait_ge(ev("exp_done"), seen.now(ev("exp_done")) + u - 1)
                            d = c * P
                            gate = OCT[:, c, u // 2:u // 2 + 1]
                            if c:
                                step(v.tensor_scalar(logit[:, 1, 0:P], bank[:, 0:P], gate, None, ALU.add))
                            link(v.scalar_tensor_tensor(logit[:, c, d:d + P], bank[:, d:d + P], gate, M("mask_add"), ALU.add, ALU.add))
                            src = logit[:, c, 0:n]
                        elif u >= 4:
                            v.wait_ge(ev("exp_done"), seen.now(ev("exp_done")) + u - 3)
                        v.tensor_reduce(NEG_MAX[u % 4], src, AX.X, ALU.max, negate=True).then_inc(ev("max_ready"), 1)
                    if 1 <= u <= total:
                        w = u - 1
                        n = n_keys(w % 2) * P
                        v.wait_ge(ev("exp_done"), seen.now(ev("exp_done")) + w + 1)
                        link(v.reciprocal(RECIP[w % 4], SUM[w % 4]))
                        v.tensor_scalar(PROBS[w % 4][:, 0:n], PROBS[w % 4][:, 0:n], RECIP[w % 4], None, ALU.mult)\
                            .then_inc(ev("prob_ready"), 1)
                    if u >= 4 and u % 2 == 0 and heads[u // 2 - 2]["last"]:
                        merged(u // 2 - 2)
                seen.next(ev("exp_done"), total)
                seen.next(ev("value_done"), len(heads))

            wait("cond_silu")
            cond = cond_s[:].unsqueeze(2).to_broadcast([P, KT, P // 2, 2])
            hi, lo = (a.rearrange("p k (r s) -> p k r s", s=2) for a in (cond_hi, cond_lo))
            link(v.tensor_copy(hi, cond))
            v.tensor_tensor(lo, cond, hi.bitcast(F32), ALU.subtract).then_inc(ev("cond_ready"), 1)
            v.wait_ge(ev("vec_in"), 16)
            for l in range(2):
                lam = V(f"lambdas{l}")
                ins = v.tensor_tensor(small[0:32, 2 * l:2 * l + 2], lam[0:32, 0:2], lam[0:32, 2:4], ALU.mult)
                if l == 1:
                    ins.then_inc(ev("lam_prod"), 1)
            split_to(RING)
            with v.Fori(0, (2 * N_ADA - RING) // RING) as i:
                for j in range(RING):
                    split_at(i * RING + (RING + j), j, True)
            nsplit[0] = 2 * N_ADA
            split_to(2 * N_ADA + AHEAD)
            wait("lam_exp")
            for l in range(2):
                link(v.tensor_tensor(neg_lam[:, l:l + 1], small[:, 4 + 2 * l + 1:6 + 2 * l], small[:, 4 + 2 * l:5 + 2 * l], ALU.subtract))
                link(v.tensor_scalar(neg_lam[:, l:l + 1], neg_lam[:, l:l + 1], -LAMBDA_INIT[l], None, ALU.add))
                link(v.tensor_scalar(g_sub[:, l:l + 1], V(f"g_sub{l}"), 1.0 - LAMBDA_INIT[l], None, ALU.mult))
                v.wait_ge(ev("ada_turned"), ADA_GROUPS)
                src = psum[7][:, l * 96:(l + 1) * 96].rearrange("p (m s) -> p m s", s=2)
                link(v.tensor_tensor(mod[:, l, :, :], src, V(f"b_ada{l}").unsqueeze(2).to_broadcast([P, N_ADA, 2]), ALU.add))

                def g(name):
                    return V(name).unsqueeze(2).to_broadcast([P, KT, 2])
                link(v.scalar_tensor_tensor(gains[:, l, 0], mod[:, l, 8:16, :], 1.0, g(f"g_attn_pre{l}"), ALU.add, ALU.mult))
                link(v.tensor_tensor(gains[:, l, 1], mod[:, l, 16:24, :], g(f"g_attn_post{l}"), ALU.mult))
                link(v.scalar_tensor_tensor(gains[:, l, 2], mod[:, l, 32:40, :], 1.0, g(f"g_ffn_pre{l}"), ALU.add, ALU.mult))
                link(v.tensor_tensor(gains[:, l, 3], mod[:, l, 40:48, :], g(f"g_ffn_post{l}"), ALU.mult))
            v.wait_ge(ev("mat_in"), 16)
            v.wait_ge(ev("ws_in"), 16)
            v.tensor_tensor(WS, WS, M("mask01").unsqueeze(1).to_broadcast([P, 4, P]), ALU.mult).then_inc(ev("ws_ready"), 1)
            norm(lat, lambda k: V("g_even_mix", k), lambda k: V("zero"))
            others_read(5)
            wait("gx_ready", 2)
            v.scalar_tensor_tensor(QQ, GX, -1.0, GX, ALU.mult, ALU.min).then_inc(ev("abs_ready"), 1)
            others_read(4, 4)
            wait("softplus_ready")
            link(v.scalar_tensor_tensor(GX, GX, 0.0, QQ, ALU.min, ALU.subtract))
            link(v.memset(sq[:, 0, :], 1.0))
            for t in range(2):
                for c in range(2):
                    cc = slice(c * P, (c + 1) * P)
                    step(v.tensor_tensor_scan(G[:, t, cc], sq[:, 0, cc], GX[:, t, cc], 0.0, ALU.mult, ALU.add))
            link(v.memset(small[:, 32:48], 0.0))
            ref = small[:, 32:48].rearrange("p (t c i) -> p t c i", t=2, c=2)
            for t in range(2):
                for c in range(2):
                    step(v.tensor_copy(ref[:, t, c, 1:4], G[:, t, c * P + SUB - 1:c * P + 3 * SUB:SUB]))
            settle()
            for t in range(2):
                for c in range(2):
                    g3 = G[:, t, c * P:(c + 1) * P].unsqueeze(1).to_broadcast([P, 4, P])
                    r3 = ref[:, t, c, :].unsqueeze(2).to_broadcast([P, 4, P])
                    step(v.tensor_tensor(EK[:, t, 4 * c:4 * c + 4, :], g3, r3, ALU.subtract))
            for t in range(2):
                g3 = G[:, t, :].rearrange("p (i s) -> p i s", s=SUB)
                r3 = small[:, 32 + 8 * t:40 + 8 * t].unsqueeze(2).to_broadcast([P, 8, SUB])
                step(v.tensor_tensor(QQ[:, t, :].rearrange("p (i s) -> p i s", s=SUB), g3, r3, ALU.subtract))
                step(v.tensor_scalar(KD[:, t, :], G[:, t, 0:P], G[:, t, P - 1:P], None, ALU.subtract))
            settle()
            v.tensor_scalar(EK, EK, -16.0 * CLAMP, None, ALU.max).then_inc(ev("diffs_ready"), 1)
            others_read(4, 4)
            v.wait_ge(ev("wide_read"), nwide[0])
            for c in range(2):
                link(v.bn_stats(small[:, 32 + 6 * c:38 + 6 * c], VA[:, c, :]))
                link(v.bn_aggr(small[:, 48 + 2 * c:50 + 2 * c], small[:, 32 + 6 * c:38 + 6 * c]))
            v.tensor_copy(small[:, 16:18], small[:, 49:52:2]).then_inc(ev("var_ready"), 1)
            others_read(2)
            wait("rstd_ready")
            for c in range(2):
                step(v.tensor_scalar(VN[:, c, :], VA[:, c, :], small[:, 48 + 2 * c:49 + 2 * c], small[:, 16 + c:17 + c],
                                     ALU.subtract, ALU.mult))
            settle()
            v.wait_ge(ev("lng_in"), 16)
            v.wait_ge(ev("lnb_in"), 16)
            link(v.tensor_tensor(VN, VN, LNG.unsqueeze(1).to_broadcast([P, 2, A_W]), ALU.mult))
            v.tensor_tensor(VN, VN, LNB.unsqueeze(1).to_broadcast([P, 2, A_W]), ALU.add).then_inc(ev("vn_ready"), 1)
            others_read(2)
            wait("exps_ready", 4)
            for t in range(2):
                for c in range(2):
                    k3 = KTT[:, t, c * P:(c + 1) * P].unsqueeze(1).to_broadcast([P, 4, P])
                    step(v.tensor_tensor(EK[:, t, 4 * c:4 * c + 4, :], EK[:, t, 4 * c:4 * c + 4, :], k3, ALU.mult))
            step(v.tensor_tensor(QQ, QQ, QT, ALU.mult))
            step(v.tensor_tensor(QI, QI, QT[:, :, P:2 * P], ALU.mult))
            step(v.tensor_tensor(KD, KD, KTT[:, :, 0:P], ALU.mult))
            settle()
            v.sem_inc(ev("decays_ready"), 1)
            others_read(4)
            v.wait_ge(ev("lin_read"), nlin[0])
            v.wait_ge(ev("bs_in"), 16)
            wait("spatial_done")
            for b in range(2):
                for g in range(2):
                    src = half(2 + b, g).rearrange("p (c s) -> p c s", c=2)
                    step(v.tensor_tensor(sq[:, 4 + 2 * b + g, :].rearrange("p (c s) -> p c s", c=2), src,
                                         BS[:, 2 * b + g, :].unsqueeze(1).to_broadcast([P, 2, P]), ALU.add))
            settle()
            for k in range(4):
                v.tensor_tensor(tmp[:, k, :], U[:, k, :], sq[:, 4 + k, :], ALU.mult).then_inc(ev("scaled"), 1)
            wait("kd_turned")
            v.tensor_copy(KDT, psum[7][:, 0:2 * P].rearrange("p (a b) -> p a b", a=2)).then_inc(ev("kdt_ready"), 1)
            wait("gla_scores")
            for par in range(2):
                ins = v.tensor_tensor(ATS[:, par], psum[par][:, :].rearrange("p (a b) -> p a b", a=4),
                                      M("mask01").unsqueeze(1).to_broadcast([P, 4, P]), ALU.mult)
            ins.then_inc(ev("ats_ready"), 1)
            wait("state_done")
            v.tensor_copy(ST, psum[6][:, 0:2 * P].rearrange("p (a b) -> p a b", a=2)).then_inc(ev("state_ready"), 1)
            for k in range(4):
                low_part(k)
            wait("rs_ready")
            link(v.tensor_tensor(tmp[:, 4:8, :], tmp[:, 4:8, :], sq[:, 4:8, :], ALU.mult))
            for h in range(4):
                v.scalar_tensor_tensor(tmp[:, 4 + h, :], tmp[:, 4 + h, :], V("head_g", h), OG[:, h, :], ALU.mult, ALU.mult)\
                    .then_inc(ev("scaled"), 1)
            for k in range(4, KT):
                low_part(k)
            add_linears(lat)
            norm(lat, lambda k: V("g_even_ffn", k), lambda k: V("zero"))
            ffn(FF_STEPS)

            for b in range(4):
                if b < 3:
                    v.wait_ge(ev("bank_down"), b + 1)
                else:
                    v.wait_ge(pack_used, 2 * N_ADA + npos[0])
                v.tensor_tensor(lat[:, 2 * b:2 * b + 2, :], lat[:, 2 * b:2 * b + 2, :],
                                psum[b][:, :].rearrange("p (a t) -> p a t", a=2), ALU.add).then_inc(ev("x_part"), 1)
            nx[0] += 4
            v.wait_ge(ev("x_part"), nx[0])
            norm(lat, lambda k: V("g_odd_mix", k), lambda k: V("zero"))
            others_read(17)
            wait("rs_ready")
            v.scalar_tensor_tensor(OQ, OQ, V("odd_q_g"), sq[:], ALU.mult, ALU.mult).then_inc(ev("q_scaled"), 1)
            wait("f_ready")
            f, neg_c = OF[0:C_HEADS], ONC[0:C_HEADS]
            v.scalar_tensor_tensor(neg_c, f, -1.0, f, ALU.mult, ALU.min).then_inc(ev("abs_ready"), 1)
            wait("softplus_ready")
            link(v.scalar_tensor_tensor(f, f, 0.0, neg_c, ALU.min, ALU.subtract))
            link(v.memset(logit[:, 0, :], 1.0))
            link(v.tensor_tensor_scan(OC[0:C_HEADS], logit[0:C_HEADS, 0, :], f, 0.0, ALU.mult, ALU.add))
            link(v.tensor_scalar(neg_c, OC[0:C_HEADS], -1.0, None, ALU.mult))
            v.sem_inc(ev("gates_summed"), 1)
            others_read(4, 4)
            wait("rs_ready")
            v.scalar_tensor_tensor(OK, OK, V("odd_k_g"), tmp[:], ALU.mult, ALU.mult).then_inc(ev("k_scaled"), 1)
            v.wait_ge(ev("k_scaled"), 1)
            others_read(4, 4)
            wait("gates_sum_turned")
            link(v.tensor_copy(OCT, psum[7][:, 0:2 * C_HEADS].rearrange("p (c h) -> p c h", c=2)))
            v.sem_inc(ev("qk_ready"), 1)
            others_read(8)
            v.wait_ge(ev("lin_read"), nlin[0])
            v.wait_ge(ev("q_scaled"), 1)

            def odd_pair(hd):
                t = hd["tile"]
                v.tensor_tensor(tmp[:, t, :], half(hd["out"][0], 0), OO[:, t, :], ALU.mult).then_inc(ev("pair_read"), 1)

            attention("odd", odd_pair)
            v.wait_ge(ev("pair_read"), seen.next(ev("pair_read"), 8))

            def hand_on():
                for k in range(KT):
                    v.sem_inc(ev("scaled"), 1)
                for k in range(KT):
                    low_part(k)

            hand_on()
            add_linears(lat)
            norm(lat, lambda k: V("g_odd_ffn", k), lambda k: V("zero"))
            others_read(1)
            wait("logits_turned")
            link(v.tensor_copy(RL, psum[7][:, 0:2 * N_EXP].rearrange("p (t n) -> p t n", t=2)))
            for t in range(2):
                link(v.max(small[:, 32 + 8 * t:40 + 8 * t], RL[:, t, :]))
                link(v.max_index(GATE2[:, t, :].bitcast(U32), small[:, 32 + 8 * t:40 + 8 * t], RL[:, t, :]))
                link(v.tensor_copy(small[:, 16 + 2 * t:18 + 2 * t], GATE2[:, t, 0:2].bitcast(U32)))
            top = small[:, 32:48].rearrange("p (t n) -> p t n", t=2)
            v.tensor_tensor(small[:, 24:26].unsqueeze(2), top[:, :, 1:2], top[:, :, 0:1], ALU.subtract).then_inc(ev("top_diff"), 1)
            wait("top_exp")
            link(v.tensor_scalar(small[:, 26:28], small[:, 24:26], 1.0, None, ALU.add))
            link(v.reciprocal(small[:, 26:28], small[:, 26:28]))
            link(v.tensor_tensor(small[:, 28:30], small[:, 26:28], small[:, 24:26], ALU.mult))
            link(v.memset(GATE, 0.0))
            link(v.memset(SLOT, 0.0))
            for t in range(2):
                first, second = (small[:, n + 2 * t:n + 1 + 2 * t] for n in (16, 17))
                ids = M("iota")[:, 0:N_EXP]
                step(v.tensor_scalar(GATE[:, t, 0:N_EXP], ids, first, small[:, 26 + t:27 + t], ALU.is_equal, ALU.mult))
                step(v.tensor_scalar(GATE2[:, t, :], ids, second, small[:, 28 + t:29 + t], ALU.is_equal, ALU.mult))
                link(v.tensor_scalar(SEL[:, t, :], ids, first, None, ALU.is_equal))
                step(v.scalar_tensor_tensor(SEL[:, t, :], ids, second, SEL[:, t, :], ALU.is_equal, ALU.add))
            settle()
            v.sem_inc(ev("chosen"), 1)
            step(v.tensor_tensor(GATE[:, :, 0:N_EXP], GATE[:, :, 0:N_EXP], GATE2, ALU.add))
            v.wait_ge(ev("m_h_turned"), 1)
            for c in range(2):
                step(v.tensor_copy(HT[:, 1, c * 512:(c + 1) * 512], psum[2 + c][:, :]))
            wait("slots_counted")
            step(v.tensor_tensor(SLOT[:, :, 0:N_EXP], psum[7][:, 0:2 * N_EXP].rearrange("p (t n) -> p t n", t=2), SEL, ALU.mult))
            link(v.tensor_reduce(small[:, 53:54], psum[7][:, 2 * N_EXP:3 * N_EXP], AX.X, ALU.max))
            step(v.tensor_scalar(SLOT, SLOT, -1.0, None, ALU.add))
            link(v.tensor_copy(fullest[:, 0:1], small[:, 53:54]))
            v.sem_inc(ev("routed"), 1)
            v.wait_ge(ev("m_h_t0"), 1)
            v.sem_inc(ev("m_h_t"), 1)
            split_to(2 * N_ADA + npos[0] + AHEAD)
            n = v.value_load(fullest[0:1, 0:1], min_val=0, max_val=T)
            with v.If(n > P):
                experts(sparse=False)
            with v.Else():
                experts(sparse=True)
            npos[0] += N_EXP * EXP_PACKS
            nsplit[0] += N_EXP * EXP_PACKS
            v.sem_inc(ev("x_ready"), 1)
            rs = next_rs()
            for k in range(KT):
                step(v.scalar_tensor_tensor(lat[:, k, :], lat[:, k, :], V("g_final", k), rs, ALU.mult, ALU.mult))
            settle()
            v.sem_inc(ev("x_ready"), 1)
            for l in range(2):
                for s, (stream, x) in enumerate((("context", con), ("latents", lat))):
                    only_kv = l == 1 and stream == "context"
                    k0 = T if stream == "context" else 0
                    col = 1 - s
                    norm(x, lambda k: gains[:, l, 0, k, col:col + 1], lambda k: mod[:, l, k, col:col + 1])
                    others_read(3 if only_kv else 9)
                    wait("rs_ready")
                    step(v.scalar_tensor_tensor(tmp[:, 0, :], ZR[:, 0, :], V(f"g_mla_kv{l}"), sq[:, 0, :], ALU.mult, ALU.mult))
                    if not only_kv:
                        for k in range(2):
                            step(v.scalar_tensor_tensor(tmp[:, 1 + k, :], ZR[:, 6 + k, :], V(f"g_mla_q{l}", k), sq[:, 6, :],
                                                        ALU.mult, ALU.mult))
                    step(v.scalar_tensor_tensor(KG[:, k0:k0 + T], ZR[:, 1, :], V(f"g_gqa_k{l}"), sq[:, 1, :], ALU.mult, ALU.mult))
                    if not only_kv:
                        step(v.scalar_tensor_tensor(QG, ZR[:, 2:6, :], V(f"g_gqa_q{l}"), sq[:, 2:6, :], ALU.mult, ALU.mult))
                    settle()
                    v.sem_inc(ev("latents_normed"), 1)

                    def rope(n):
                        _, cos, sin, rows, z = ROPED[n]
                        w = z.shape[1]
                        wait("rotated")
                        src = psum[n % 4 if n < 6 else n % 2][0:rows, 0:w * T].rearrange("p (a t) -> p a t", a=w)
                        t = sq[0:rows, 0:w, :]
                        v.tensor_tensor(t, src, M(sin)[0:rows].unsqueeze(1).to_broadcast([rows, w, T]), ALU.mult)\
                            .then_inc(ev("rope_out"), 1)
                        step(v.tensor_tensor(z, z, M(cos)[0:rows].unsqueeze(1).to_broadcast([rows, w, T]), ALU.mult))
                        v.wait_ge(ev("rope_out"), seen.next(ev("rope_out")))
                        settle()
                        link(v.tensor_tensor(z, z, t, ALU.add))

                    if stream == "latents":
                        v.sem_inc(ev("rope_in"), 1)
                    others_read(2 if only_kv else 4)
                    if stream == "latents":
                        for n in range(4):
                            rope(n)
                            others_read(1)
                        nlin[0] -= 4
                        nwide[0] += 2
                    else:
                        others_read(4, 4)
                    for kk in (slice(0, 1),) if only_kv else (slice(0, 1), slice(1, 3)):
                        wait("latents_hi")
                        v.tensor_tensor(h_lo[:, kk, :], tmp[:, kk, :], h_hi[:, kk, :].bitcast(F32), ALU.subtract)\
                            .then_inc(ev("latent_split"), 1)
                    others_read(1)
                    nlin[0] -= 1
                    if stream == "latents":
                        rope(4)
                        rope(5)
                    if not only_kv:
                        others_read(1)
                        nlin[0] -= 1
                        wait("qm_ready", 2)
                    if stream == "latents":
                        v.sem_inc(ev("rope_in"), 1)
                        rope(6)
                        rope(7)
                    wait("km_ready", 3)
                    link(v.tensor_copy(KM[64:MLA_QK, :, k0:k0 + T], KPE[64:MLA_QK].unsqueeze(1).to_broadcast([32, 4, T])))
                    if only_kv:
                        v.sem_inc(ev("context_keys_ready"), 1)
                        continue
                    v.sem_inc(ev("qk_ready"), 1)

                    def pair(hd):
                        t, b = hd["tile"], hd["out"][0]
                        if hd["kind"] == "diff":
                            link(v.tensor_scalar(sq[:, 4 + t, :], half(b, 1), neg_lam[:, l:l + 1], None, ALU.mult))
                            v.tensor_tensor(tmp[:, t, :], half(b, 0), sq[:, 4 + t, :], ALU.add).then_inc(ev("pair_read"), 1)
                        else:
                            v.tensor_copy(tmp[:, t, :], half(b, 0)).then_inc(ev("pair_read"), 1)

                    attention(stream, pair)
                    v.wait_ge(ev("pair_read"), seen.next(ev("pair_read"), 8))
                    v.sem_inc(ev("diff_ready"), 1)
                    for _ in range(6):
                        v.sem_inc(ev("scaled"), 1)
                    for k in MIXED_ORDER[:BEFORE_ROOT]:
                        low_part(k)
                    wait("rs_ready")
                    for k in (2, 3):
                        v.scalar_tensor_tensor(tmp[:, k, :], tmp[:, k, :], g_sub[:, l:l + 1], sq[:, k, :], ALU.mult, ALU.mult)\
                            .then_inc(ev("scaled"), 1)
                    for k in MIXED_ORDER[BEFORE_ROOT:]:
                        low_part(k)
                    others_read(KT)

                    def post(which, y):
                        rs = next_rs()
                        for k in range(KT):
                            v.scalar_tensor_tensor(tmp[:, k, :], y(k), gains[:, l, which, k, col:col + 1], rs, ALU.mult, ALU.mult)\
                                .then_inc(ev("post_scaled"), 1)
                            if k % 2 and k > 1:
                                add(k - 3)
                        add(KT - 2)
                        v.wait_ge(ev("x_part"), nx[0])

                    def add(k):
                        v.wait_ge(ev("post_scaled"), seen.next(ev("post_scaled"), 2))
                        v.tensor_tensor(x[:, k:k + 2, :], x[:, k:k + 2, :], tmp[:, k:k + 2, :], ALU.add).then_inc(ev("x_part"), 1)
                        nx[0] += 1

                    post(1, lambda k: ZR[:, k, :])
                    norm(x, lambda k: gains[:, l, 2, k, col:col + 1], lambda k: mod[:, l, 24 + k, col:col + 1])
                    ffn(FF_STEPS)
                    post(3, lambda k: half(k // 2, k % 2))
            v.sem_inc(ev("out_ready"), 1)


def _column_packs(w):
    k, n = w.shape
    pad = -n % P
    if pad:
        w = np.concatenate([w, np.zeros((k, pad), w.dtype)], axis=1)
    return w.reshape(KT, P, -1, P).transpose(2, 1, 0, 3).reshape(-1, P, PACK)


def _wide_packs(w):
    return w.reshape(4, 2, P, -1, 512).transpose(3, 0, 2, 1, 4).reshape(-1, P, PACK)


def _fill_ffn(out, w1, w3, w2):
    n = w2.shape[0] // P
    for w, a in enumerate((w1, w3)):
        packs = _column_packs(a)
        for s in range(n):
            out[w if s == 0 else 3 * s - 1 + w] = packs[s]
    for s in range(n):
        out[3 * s + 4 if s < n - 1 else 3 * n - 1] = w2[s * P:(s + 1) * P]


def _fill_expert(out, w1, w3, w2):
    ups = [_wide_packs(a) for a in (w1, w3)]
    rows = w2.reshape(-1, P, D)
    for g in range(GROUPS):
        at = 0 if g == 0 else 12 * g - 4
        for w in range(2):
            out[at + 4 * w:at + 4 * w + 4] = ups[w][4 * g:4 * g + 4]
        down = 12 * g + 16 if g < GROUPS - 1 else EXP_PACKS - 4
        out[down:down + 4] = rows[4 * g:4 * g + 4]


def _weight_packs(a):
    packs = np.zeros((N_PACKS, P, PACK), np.float32)

    def put(name, values):
        packs[START[name]:START[name] + values.shape[0]] = values

    for l in range(2):
        put(f"ada{l}", _wide_packs(a["w_ada_2"][l]))
    w = a["even_w_in"][0]
    u, v, q, k, g, vb, og = np.split(w, np.cumsum([A_W, A_W, B_QK, B_QK, RANK, B_V])[:6], axis=1)
    put("even_in", np.concatenate([_column_packs(x) for x in (g, q, k)] + [_wide_packs(x) for x in (vb, v)]
                                  + [_column_packs(x) for x in (u, og)]))
    put("even_o", _column_packs(a["even_w_o"][0]))
    w = a["odd_w_in"][0]
    q, k, v, og, f = np.split(w, [D, 2 * D, 3 * D, 4 * D], axis=1)
    put("odd_in", np.concatenate([_column_packs(x) for x in (f, q, k)] + [_wide_packs(v), _column_packs(og)]))
    put("odd_o", _column_packs(a["odd_w_o"][0]))
    put("router", _column_packs(a["odd_router"][0]))

    def ffn(name, w1, w3, w2):
        _fill_ffn(packs[START[name]:START[name] + COUNT[name]], w1, w3, w2)

    ffn("even_ffn", a["even_ffn_w1"][0], a["even_ffn_w3"][0], a["even_ffn_w2"][0])
    for e in range(N_EXP):
        _fill_expert(packs[START["moe"] + e * EXP_PACKS:START["moe"] + (e + 1) * EXP_PACKS],
                     a["odd_exp_w1"][0, e], a["odd_exp_w3"][0, e], a["odd_exp_w2"][0, e])
    for l in range(2):
        w = a["w_in_2"][l]
        qa, kva, dq, dk, dv, gq, gk, gv = np.split(w, np.cumsum([256, 160, 256, 256, 256, 512, 128])[:7], axis=1)
        ckv, kpe = kva[:, :128], kva[:, 128:]
        kpe = np.concatenate([np.zeros((D, 64), w.dtype), kpe], axis=1)
        gq = gq.reshape(D, 2, 4, 64).transpose(0, 2, 1, 3).reshape(D, 512)
        values = np.concatenate([dv, gv, np.zeros((D, 512 - 384), w.dtype)], axis=1)
        put(f"in{l}", np.concatenate([_column_packs(x) for x in (ckv, gk, qa, gq, kpe, dk, dq)] + [_wide_packs(values)]))
        packs[START[f"kvb{l}"], :, 0:512] = a["w_mla_kvb_2"][l]
        qb = a["w_mla_qb_2"][l].reshape(2, P, 4, MLA_QK).transpose(1, 2, 0, 3)
        packs[START[f"qb{l}"]].reshape(P, 4, 2, P)[..., 0:MLA_QK] = qb
        put(f"out{l}", _column_packs(a["w_out_2"][l]))
        ffn(f"ffn{l}", a["w_ffn_gate_2"][l], a["w_ffn_up_2"][l], a["w_ffn_down_2"][l])
    return packs


def _vectors(a):
    vec = np.zeros((P, N_VEC), np.float32)

    def put(name, values):
        at, n = VEC[name]
        values = np.asarray(values).reshape(-1)
        rows = values.size // n
        vec[0:rows, at:at + n] = values.reshape(n, rows).T

    vec[:, VEC["one"][0]] = 1.0
    vec[:, VEC["eps"][0]] = EPS
    vec[:, VEC["eps64"][0]] = 64 * EPS
    put("g_even_mix", a["even_norm_mix"][0])
    put("g_even_ffn", a["even_norm_ffn"][0])
    put("g_odd_mix", a["odd_norm_mix"][0])
    put("g_odd_ffn", a["odd_norm_ffn"][0])
    put("g_final", a["final_norm"])
    put("head_g", a["even_head_g"][0])
    put("gate_bias", a["even_gate_bias"][0])
    put("odd_q_g", np.tile(a["odd_q_g"][0], 2))
    put("odd_k_g", np.tile(a["odd_k_g"][0], 2))
    put("forget_bias", a["odd_forget_bias"][0])
    put("cond", np.stack([a["c_2"][0], a["c_ctx_2"]]).reshape(2, KT, P).transpose(1, 0, 2))
    for l in range(2):
        for name, key in (("g_attn_pre", "g_attn_pre_2"), ("g_attn_post", "g_attn_post_2"), ("g_ffn_pre", "g_ffn_pre_2"),
                          ("g_ffn_post", "g_ffn_post_2"), ("b_ada", "b_ada_2"), ("g_mla_q", "g_mla_q_2"), ("g_mla_kv", "g_mla_kv_2")):
            put(f"{name}{l}", a[key][l])
        for name, key in (("g_gqa_q", "g_gqa_q_2"), ("g_gqa_k", "g_gqa_k_2"), ("g_sub", "g_diff_sub_2")):
            put(f"{name}{l}", np.tile(a[key][l], 2))
        put(f"lambdas{l}", np.stack([a[f"lambda_{n}_2"][l] for n in ("q1", "q2", "k1", "k2")]))
    return vec


def _matrices():
    mat = np.zeros((P, N_MAT), np.float32)

    def put(name, values):
        at, n = MAT[name]
        mat[0:values.shape[0], at:at + values.shape[1]] = values

    r = np.arange(P)
    put("ident", np.eye(P))
    put("ones", np.ones((P, P)))
    put("block64", (r[:, None] // 64 == r[None, :] // 64).astype(np.float32))
    put("mask01", (r[:, None] <= r[None, :]).astype(np.float32))
    put("mask_add", np.where(r[None, :] <= r[:, None], 0.0, -1e30))
    token = np.arange(T)
    for name, dim, first in (("mla", 32, 64), ("diff", 32, 0), ("gqa", 64, 0)):
        h = dim // 2
        rot = np.zeros((P, P))
        quarter = dim // 4
        inv = (np.float32(ROPE_THETA) ** (-np.arange(quarter, dtype=np.float32) / np.float32(quarter))).astype(np.float32)
        row, col = (token // GRID_W).astype(np.float32), (token % GRID_W).astype(np.float32)
        angle = np.concatenate([row[:, None] * inv, col[:, None] * inv], axis=1).T
        cos, sin = np.ones((P, T)), np.zeros((P, T))
        for b in range(first, MLA_QK if name == "mla" else P, dim):
            for i in range(h):
                rot[b + h + i, b + i] = -1.0
                rot[b + i, b + h + i] = 1.0
            cos[b:b + h] = cos[b + h:b + dim] = np.cos(angle)
            sin[b:b + h] = sin[b + h:b + dim] = np.sin(angle)
        put("rot_" + name, rot)
        put("cos_" + name, cos)
        put("sin_" + name, sin)
    pick = np.zeros((N_EXP, N_EXP * P))
    for e in range(N_EXP):
        pick[e, e * P:(e + 1) * P] = 1.0
    put("pick", pick)
    put("iota", np.tile(np.arange(P), (P, 1)))
    put("head_id", np.eye(C_HEADS))
    return mat


def _feature_major(x):
    return np.ascontiguousarray(x.T.reshape(KT, P, T).transpose(1, 0, 2)).reshape(P, KT * T)


def kernel(**inputs):
    import concourse.bacc as bacc
    from concourse.bass_utils import run_bass_kernel_spmd

    a = {k: np.asarray(v) for k, v in inputs.items()}
    arrays = {
        "w_packs": _weight_packs(a),
        "vecs": _vectors(a),
        "mats": _matrices(),
        "x_t": _feature_major(a["x"][0]),
        "ctx_t": _feature_major(a["ctx_2"][0]),
        "w_s_t": np.ascontiguousarray(a["even_w_s"][0].transpose(2, 0, 1)).reshape(P, 4 * P),
        "b_s_row": np.ascontiguousarray(a["even_b_s"][0]).reshape(4 * P),
        "ln_g_row": np.ascontiguousarray(a["even_ln_g"][0]),
        "ln_b_row": np.ascontiguousarray(a["even_ln_b"][0]),
        "gate_up": np.ascontiguousarray(a["even_gate_up"][0]),
    }
    nc = bacc.Bacc("TRN2", target_bir_lowering=False, num_devices=1)
    args = [nc.dram_tensor(n, x.shape, F32, kind="ExternalInput").ap() for n, x in arrays.items()]
    out = nc.dram_tensor("out_t", (P, KT * T), F32, kind="ExternalOutput").ap()
    build(nc, *args, out)
    r = run_bass_kernel_spmd(nc, [arrays], core_ids=[0])
    y = r.results[0]["out_t"].reshape(P, KT, T).transpose(1, 0, 2).reshape(D, T).T
    return np.ascontiguousarray(y)[None]
```
